# Optimizing a Trainium2 kernel written in Bass

```python
import jax, jax.numpy as jnp
from jax import lax
import numpy as np
import math

D_MODEL = 1024
BATCH = 1
SEQ = 256
DEPTH = 2

BRANCH_W = 512
N_BRANCH = 3
GM_GROUPS = 4
GM_GROUP_W = BRANCH_W // GM_GROUPS
GM_CHUNK = 128
RET_HEADS = 4
RET_HD = BRANCH_W // RET_HEADS
RET_CHUNK = 128
ROPE_BASE = 10000.0
GDN_HEADS = 4
GDN_HD = BRANCH_W // GDN_HEADS
GDN_CHUNK = 64
CONV_K = 3
EPS = 1e-6

IN_SPLITS = (BRANCH_W,) * 3 + (BRANCH_W,) * 4 + (BRANCH_W,) * 4 + (GDN_HEADS,) * 4
IN_COLS = sum(IN_SPLITS)
IN_OFFSETS = tuple(int(o) for o in np.cumsum(IN_SPLITS)[:-1])


F32 = jnp.float32

def rms_norm(x, g):
    xf = x.astype(F32)
    y = xf * lax.rsqrt(jnp.mean(xf * xf, axis=-1, keepdims=True) + EPS)
    return (y * g.astype(F32)).astype(x.dtype)

def layer_norm(x, g, b):
    xf = x.astype(F32)
    mu = jnp.mean(xf, axis=-1, keepdims=True)
    var = jnp.mean(jnp.square(xf - mu), axis=-1, keepdims=True)
    y = (xf - mu) * lax.rsqrt(var + EPS)
    return (y * g.astype(F32) + b.astype(F32)).astype(x.dtype)

def to_chunks(x, c):
    b, s, h, d = x.shape
    return x.reshape(b, s // c, c, h, d).transpose(1, 0, 3, 2, 4)

def from_chunks(x):
    n, b, h, c, d = x.shape
    return x.transpose(1, 0, 3, 2, 4).reshape(b, n * c, h, d)

def gmlp_branch(u, v, z, ln_g, ln_b, w_s, b_s):
    bsz, seq, _ = u.shape
    u = jax.nn.gelu(u, approximate=False)
    v = layer_norm(jax.nn.gelu(v, approximate=False), ln_g, ln_b)
    vc = v.reshape(bsz, seq // GM_CHUNK, GM_CHUNK, GM_GROUPS, GM_GROUP_W)
    mixed = jnp.einsum("gpq,bnqgc->bnpgc", w_s, vc) + b_s.T[None, None, :, :, None]
    return u * mixed.reshape(bsz, seq, BRANCH_W) * jax.nn.silu(z)

def rotary(x):
    seq, hd = x.shape[1], x.shape[-1]
    inv = ROPE_BASE ** (-jnp.arange(0, hd, 2, dtype=F32) / hd)
    ang = jnp.arange(seq, dtype=F32)[:, None] * inv[None, :]
    cos = jnp.cos(ang)[None, :, None, :]
    sin = jnp.sin(ang)[None, :, None, :]
    x1, x2 = x[..., : hd // 2], x[..., hd // 2:]
    return jnp.concatenate([x1 * cos - x2 * sin, x2 * cos + x1 * sin], axis=-1)

def retention_branch(q, k, v, z, decay_logit, norm_g):
    bsz, seq, _ = q.shape
    shp = (bsz, seq, RET_HEADS, RET_HD)
    q = rotary(q.reshape(shp).astype(F32))
    k = rotary(k.reshape(shp).astype(F32)) * (RET_HD ** -0.5)
    v = v.reshape(shp).astype(F32)
    log_g = jax.nn.log_sigmoid(decay_logit.astype(F32))
    lf = log_g[0][:, None]
    lb = log_g[1][:, None]
    pos = jnp.arange(RET_CHUNK, dtype=F32)[None, :]
    rel = pos.T - pos
    mask = jnp.exp(jnp.where(rel[None] >= 0, lf[:, :, None] * rel[None], -lb[:, :, None] * rel[None]))
    q_dec_f = jnp.exp(lf * (pos + 1.0))[None, :, :, None]
    k_dec_f = jnp.exp(lf * (RET_CHUNK - 1.0 - pos))[None, :, :, None]
    q_dec_b = jnp.exp(lb * (RET_CHUNK - pos))[None, :, :, None]
    k_dec_b = jnp.exp(lb * pos)[None, :, :, None]
    chunk_f = jnp.exp(lf * RET_CHUNK)[None, :, :, None]
    chunk_b = jnp.exp(lb * RET_CHUNK)[None, :, :, None]
    qc, kc, vc = to_chunks(q, RET_CHUNK), to_chunks(k, RET_CHUNK), to_chunks(v, RET_CHUNK)
    state0 = jnp.zeros((bsz, RET_HEADS, RET_HD, RET_HD), F32)

    def fwd_step(state, inp):
        qi, ki, vi = inp
        scores = jnp.einsum("bhqd,bhkd->bhqk", qi, ki) * mask[None]
        out = (jnp.einsum("bhqk,bhke->bhqe", scores, vi)
               + jnp.einsum("bhcd,bhde->bhce", qi * q_dec_f, state))
        state = state * chunk_f + jnp.einsum("bhcd,bhce->bhde", ki * k_dec_f, vi)
        return state, out

    def bwd_step(state, inp):
        qi, ki, vi = inp
        out = jnp.einsum("bhcd,bhde->bhce", qi * q_dec_b, state)
        state = state * chunk_b + jnp.einsum("bhcd,bhce->bhde", ki * k_dec_b, vi)
        return state, out

    _, o_f = lax.scan(fwd_step, state0, (qc, kc, vc))
    _, o_b = lax.scan(bwd_step, state0, (qc, kc, vc), reverse=True)
    o = from_chunks(o_f + o_b)
    mu = jnp.mean(o, axis=-1, keepdims=True)
    o = (o - mu) * lax.rsqrt(jnp.mean(jnp.square(o - mu), axis=-1, keepdims=True) + EPS)
    o = o.reshape(bsz, seq, BRANCH_W) * norm_g.astype(F32)
    return o.astype(z.dtype) * jax.nn.silu(z)

def centred_depthwise_conv(x, w):
    ch = x.shape[-1]
    pad = (CONV_K - 1) // 2
    return lax.conv_general_dilated(
        x, w[:, None, :].astype(x.dtype), window_strides=(1,), padding=[(pad, pad)],
        dimension_numbers=("NWC", "WIO", "NWC"), feature_group_count=ch)

def l2_normalize(x):
    return x * lax.rsqrt(jnp.sum(x * x, axis=-1, keepdims=True) + EPS)

def gdn_direction(q, k, v, beta, g):
    bsz = q.shape[0]
    c = GDN_CHUNK
    qc, kc, vc = to_chunks(q, c), to_chunks(k, c), to_chunks(v, c)
    bc = to_chunks(beta[..., None], c)[..., 0]
    gc = jnp.cumsum(to_chunks(g[..., None], c)[..., 0], axis=-1)
    idx = jnp.arange(c)
    incl = idx[:, None] >= idx[None, :]
    strict = idx[:, None] > idx[None, :]
    decay = jnp.exp(jnp.where(incl, gc[..., :, None] - gc[..., None, :], -jnp.inf))
    kb = kc * bc[..., None]
    lower = jnp.where(strict, jnp.einsum("nbhid,nbhjd->nbhij", kb, kc) * decay, 0.0)
    eye = jnp.eye(c, dtype=F32)
    rhs = jnp.concatenate([vc * bc[..., None], kb * jnp.exp(gc)[..., None]], axis=-1)
    sol = lax.linalg.triangular_solve(lower + eye, rhs, left_side=True, lower=True)
    u, w = sol[..., :GDN_HD], sol[..., GDN_HD:]

    def step(state, inp):
        qi, ki, ui, wi, gi, di = inp
        v_new = ui - jnp.einsum("bhcd,bhde->bhce", wi, state)
        scores = jnp.einsum("bhqd,bhkd->bhqk", qi, ki) * di
        out = (jnp.einsum("bhcd,bhde->bhce", qi * jnp.exp(gi)[..., None], state)
               + jnp.einsum("bhqk,bhke->bhqe", scores, v_new))
        g_last = gi[..., -1:]
        state = (state * jnp.exp(g_last)[..., None]
                 + jnp.einsum("bhcd,bhce->bhde", ki * jnp.exp(g_last - gi)[..., None], v_new))
        return state, out

    state0 = jnp.zeros((bsz, GDN_HEADS, GDN_HD, GDN_HD), F32)
    _, o = lax.scan(step, state0, (qc, kc, u, w, gc, decay))
    return from_chunks(o)

def gdn_branch(q, k, v, z, a_f, b_f, a_b, b_b, conv_w, a_log, dt_bias, norm_g):
    bsz, seq, _ = q.shape
    qkv = jax.nn.silu(centred_depthwise_conv(jnp.concatenate([q, k, v], axis=-1), conv_w))
    q, k, v = jnp.split(qkv.astype(F32), 3, axis=-1)
    shp = (bsz, seq, GDN_HEADS, GDN_HD)
    q = l2_normalize(q.reshape(shp)) * (GDN_HD ** -0.5)
    k = l2_normalize(k.reshape(shp))
    v = v.reshape(shp)
    a_rate = jnp.exp(a_log.astype(F32))
    dtb = dt_bias.astype(F32)
    g_f = -a_rate[0] * jax.nn.softplus(a_f.astype(F32) + dtb[0])
    g_b = -a_rate[1] * jax.nn.softplus(a_b.astype(F32) + dtb[1])
    beta_f = jax.nn.sigmoid(b_f.astype(F32))
    beta_b = jax.nn.sigmoid(b_b.astype(F32))
    o_f = gdn_direction(q, k, v, beta_f, g_f)
    rev = lambda t: jnp.flip(t, axis=1)
    o_b = rev(gdn_direction(rev(q), rev(k), rev(v), rev(beta_b), rev(g_b)))
    o = o_f + o_b
    o = o * lax.rsqrt(jnp.mean(o * o, axis=-1, keepdims=True) + EPS) * norm_g.astype(F32)
    return o.reshape(bsz, seq, BRANCH_W).astype(z.dtype) * jax.nn.silu(z)

def first_inputs(seed: int = 0) -> dict:
    key = jax.random.key(seed)
    ks = jax.random.split(key, 17)
    nrm = lambda k, shape, scale: jax.random.normal(k, shape, F32) * scale
    x = nrm(ks[0], (BATCH, SEQ, D_MODEL), 1.0)
    norm_g = 1.0 + nrm(ks[1], (DEPTH, D_MODEL), 0.05)
    w_in = nrm(ks[2], (DEPTH, D_MODEL, IN_COLS), D_MODEL ** -0.5)
    gm_ln_g = 1.0 + nrm(ks[3], (DEPTH, BRANCH_W), 0.05)
    gm_ln_b = nrm(ks[4], (DEPTH, BRANCH_W), 0.02)
    gm_w_s = nrm(ks[5], (DEPTH, GM_GROUPS, GM_CHUNK, GM_CHUNK), GM_CHUNK ** -0.5)
    gm_b_s = 1.0 + nrm(ks[6], (DEPTH, GM_GROUPS, GM_CHUNK), 0.05)
    base_gamma = 1.0 - 2.0 ** (-5.0 - np.arange(RET_HEADS))
    base_logit = np.log(base_gamma / (1.0 - base_gamma)).astype(np.float32)
    ret_decay_logit = jnp.asarray(base_logit)[None, None, :] + nrm(ks[7], (DEPTH, 2, RET_HEADS), 0.1)
    ret_norm_g = 1.0 + nrm(ks[8], (DEPTH, BRANCH_W), 0.05)
    gdn_conv_w = nrm(ks[9], (DEPTH, CONV_K, 3 * BRANCH_W), CONV_K ** -0.5)
    gdn_a_log = jnp.log(jax.random.uniform(ks[10], (DEPTH, 2, GDN_HEADS), F32, 1.0, 16.0))
    dt = jnp.exp(jax.random.uniform(ks[11], (DEPTH, 2, GDN_HEADS), F32,
                                    float(np.log(1e-3)), float(np.log(1e-1))))
    gdn_dt_bias = dt + jnp.log(-jnp.expm1(-dt))
    gdn_norm_g = 1.0 + nrm(ks[12], (DEPTH, GDN_HD), 0.05)
    w_gate = nrm(ks[13], (DEPTH, D_MODEL, N_BRANCH, D_MODEL), D_MODEL ** -0.5)
    w_branch_out = nrm(ks[14], (DEPTH, N_BRANCH, BRANCH_W, D_MODEL), BRANCH_W ** -0.5)
    w_out = nrm(ks[15], (DEPTH, D_MODEL, D_MODEL), D_MODEL ** -0.5)
    final_norm_g = 1.0 + nrm(ks[16], (D_MODEL,), 0.05)
    return {"x": x, "norm_g": norm_g, "w_in": w_in, "gm_ln_g": gm_ln_g, "gm_ln_b": gm_ln_b,
            "gm_w_s": gm_w_s, "gm_b_s": gm_b_s, "ret_decay_logit": ret_decay_logit,
            "ret_norm_g": ret_norm_g, "gdn_conv_w": gdn_conv_w, "gdn_a_log": gdn_a_log,
            "gdn_dt_bias": gdn_dt_bias, "gdn_norm_g": gdn_norm_g, "w_gate": w_gate,
            "w_branch_out": w_branch_out, "w_out": w_out, "final_norm_g": final_norm_g}

def first_block(x, norm_g, w_in, gm_ln_g, gm_ln_b, gm_w_s, gm_b_s, ret_decay_logit, ret_norm_g,
              gdn_conv_w, gdn_a_log, gdn_dt_bias, gdn_norm_g, w_gate, w_branch_out, w_out,
              final_norm_g):
    for l in range(DEPTH):
        h = rms_norm(x, norm_g[l])
        (gu, gv, gz, rq, rk, rv, rz, dq, dk, dv, dz,
         a_f, b_f, a_b, b_b) = jnp.split(h @ w_in[l], IN_OFFSETS, axis=-1)
        y_a = gmlp_branch(gu, gv, gz, gm_ln_g[l], gm_ln_b[l], gm_w_s[l], gm_b_s[l])
        y_b = retention_branch(rq, rk, rv, rz, ret_decay_logit[l], ret_norm_g[l])
        y_c = gdn_branch(dq, dk, dv, dz, a_f, b_f, a_b, b_b, gdn_conv_w[l], gdn_a_log[l],
                         gdn_dt_bias[l], gdn_norm_g[l])
        branches = jnp.stack([y_a, y_b, y_c], axis=2)
        proj = jnp.einsum("bsnw,nwd->bsnd", branches, w_branch_out[l])
        gates = jax.nn.sigmoid(jnp.einsum("bsd,dne->bsne", h, w_gate[l]))
        merged = jnp.sum(gates * proj, axis=2)
        x = x + merged @ w_out[l]
    return rms_norm(x, final_norm_g)


N_HYB = (DEPTH + 1) // 2
N_REC = DEPTH // 2
NORM_EPS = 1e-6
CONV_K_2 = 4
D_FF = 2816
D_SSM = D_MODEL
SSM_HEAD_DIM = 64
SSM_HEADS = D_SSM // SSM_HEAD_DIM
SSM_GROUPS = 2
SSM_STATE = 128
SSM_CONV_DIM = D_SSM + 2 * SSM_GROUPS * SSM_STATE
SSD_CHUNK = 128
FOX_HEAD_DIM = 128
FOX_HEADS = 8
D_FOX = FOX_HEADS * FOX_HEAD_DIM
Q_BLOCK = 128
HYB_IN = D_SSM + SSM_CONV_DIM + SSM_HEADS + 3 * D_FOX + FOX_HEADS
D_RNN = D_MODEL
RNN_BLOCKS = 8
RNN_BLOCK = D_RNN // RNN_BLOCKS
RG_LRU_C = 8.0


def rms_norm_2(x, g):
    xf = x.astype(jnp.float32)
    y = xf * lax.rsqrt(jnp.mean(xf * xf, axis=-1, keepdims=True) + NORM_EPS)
    return (y * g.astype(jnp.float32)).astype(x.dtype)

def swiglu(x, w_in, w_out):
    gate, up = jnp.split(x @ w_in, 2, axis=-1)
    return (jax.nn.silu(gate) * up) @ w_out

def causal_conv(x, w, bias):
    s = x.shape[1]
    kw = w.shape[0]
    xp = jnp.pad(x, ((0, 0), (kw - 1, 0), (0, 0)))
    y = xp[:, 0:s] * w[0]
    for k in range(1, kw):
        y = y + xp[:, k:k + s] * w[k]
    return y + bias

def ssd_chunked(xh, dt, a, bm, cm):
    b, s, nh, p = xh.shape
    g, n = bm.shape[-2:]
    kh = nh // g
    c = s // SSD_CHUNK
    X = (xh.astype(jnp.float32) * dt[..., None]).reshape(b, c, SSD_CHUNK, g, kh, p)
    Bc = bm.astype(jnp.float32).reshape(b, c, SSD_CHUNK, g, n)
    Cc = cm.astype(jnp.float32).reshape(b, c, SSD_CHUNK, g, n)
    dA = (dt * a).reshape(b, c, SSD_CHUNK, g, kh).transpose(0, 3, 4, 1, 2)
    a_cs = jnp.cumsum(dA, axis=-1)
    causal = jnp.tril(jnp.ones((SSD_CHUNK, SSD_CHUNK), dtype=bool))
    seg = a_cs[..., :, None] - a_cs[..., None, :]
    L = jnp.exp(jnp.where(causal, seg, -jnp.inf))
    cb = jnp.einsum("bclgn,bcsgn->bgcls", Cc, Bc)
    y_diag = jnp.einsum("bgkcls,bcsgkp->bclgkp", L * cb[:, :, None], X)
    decay_states = jnp.exp(a_cs[..., -1:] - a_cs)
    states = jnp.einsum("bclgn,bgkcl,bclgkp->bcgkpn", Bc, decay_states, X)
    chunk_tot = a_cs[..., -1]
    chunk_cs = jnp.cumsum(chunk_tot, axis=-1)
    cs_prev = chunk_cs - chunk_tot
    seg_c = cs_prev[..., :, None] - chunk_cs[..., None, :]
    strict = jnp.tril(jnp.ones((c, c), dtype=bool), k=-1)
    decay_chunk = jnp.exp(jnp.where(strict, seg_c, -jnp.inf))
    init_states = jnp.einsum("bgkzc,bcgkpn->bzgkpn", decay_chunk, states)
    state_decay_out = jnp.exp(a_cs)
    y_off = jnp.einsum("bclgn,bcgkpn,bgkcl->bclgkp", Cc, init_states, state_decay_out)
    return (y_diag + y_off).reshape(b, s, nh, p)

def forgetting_attention(q, k, v, log_f):
    b, s, h, d = q.shape
    nblk = s // Q_BLOCK
    cum = jnp.cumsum(log_f, axis=1).transpose(0, 2, 1)
    qb = q.reshape(b, nblk, Q_BLOCK, h, d).transpose(1, 0, 2, 3, 4)
    cqb = cum.reshape(b, h, nblk, Q_BLOCK).transpose(2, 0, 1, 3)
    kpos = jnp.arange(s)
    scale = d ** -0.5

    def block(args):
        qi, ci, i = args
        logits = jnp.einsum("bqhd,bkhd->bhqk", qi, k).astype(jnp.float32) * scale
        logits = logits + ci[..., :, None] - cum[:, :, None, :]
        qpos = i * Q_BLOCK + jnp.arange(Q_BLOCK)
        mask = kpos[None, :] <= qpos[:, None]
        probs = jax.nn.softmax(jnp.where(mask, logits, -jnp.inf), axis=-1)
        return jnp.einsum("bhqk,bkhd->bqhd", probs.astype(v.dtype), v)

    out = lax.map(block, (qb, cqb, jnp.arange(nblk)))
    return out.transpose(1, 0, 2, 3, 4).reshape(b, s, h, d)

def hybrid_mixer(h, w_in, conv_w, conv_b, dt_bias, a_log, d_skip, ssm_norm_g, fox_b_f, w_out):
    b, s, _ = h.shape
    sizes = (D_SSM, SSM_CONV_DIM, SSM_HEADS, D_FOX, D_FOX, D_FOX)
    offs = np.cumsum(sizes).tolist()
    z, xbc, dt_raw, q, k, v, f_raw = jnp.split(h @ w_in, offs, axis=-1)
    xbc = jax.nn.silu(causal_conv(xbc, conv_w, conv_b))
    xs, bm, cm = jnp.split(xbc, [D_SSM, D_SSM + SSM_GROUPS * SSM_STATE], axis=-1)
    xh = xs.reshape(b, s, SSM_HEADS, SSM_HEAD_DIM)
    dt = jax.nn.softplus(dt_raw.astype(jnp.float32) + dt_bias.astype(jnp.float32))
    a = -jnp.exp(a_log.astype(jnp.float32))
    y = ssd_chunked(xh, dt, a,
                    bm.reshape(b, s, SSM_GROUPS, SSM_STATE),
                    cm.reshape(b, s, SSM_GROUPS, SSM_STATE))
    y = y + d_skip.astype(jnp.float32)[:, None] * xh.astype(jnp.float32)
    y = y.reshape(b, s, D_SSM) * jax.nn.silu(z.astype(jnp.float32))
    yg = y.reshape(b, s, SSM_GROUPS, D_SSM // SSM_GROUPS)
    yg = yg * lax.rsqrt(jnp.mean(yg * yg, axis=-1, keepdims=True) + NORM_EPS)
    y_ssm = (yg.reshape(b, s, D_SSM) * ssm_norm_g.astype(jnp.float32)).astype(h.dtype)
    log_f = jax.nn.log_sigmoid(f_raw.astype(jnp.float32) + fox_b_f.astype(jnp.float32))
    o = forgetting_attention(q.reshape(b, s, FOX_HEADS, FOX_HEAD_DIM),
                             k.reshape(b, s, FOX_HEADS, FOX_HEAD_DIM),
                             v.reshape(b, s, FOX_HEADS, FOX_HEAD_DIM), log_f)
    o = o.reshape(b, s, D_FOX).astype(h.dtype)
    return jnp.concatenate([y_ssm, o], axis=-1) @ w_out

def rg_lru(x, w_a, b_a, w_x, b_x, lam):
    b, s, d = x.shape
    xb = x.reshape(b, s, RNN_BLOCKS, RNN_BLOCK)
    r = jax.nn.sigmoid((jnp.einsum("bsnj,njk->bsnk", xb, w_a).reshape(b, s, d) + b_a).astype(jnp.float32))
    i = jax.nn.sigmoid((jnp.einsum("bsnj,njk->bsnk", xb, w_x).reshape(b, s, d) + b_x).astype(jnp.float32))
    log_a = RG_LRU_C * r * jax.nn.log_sigmoid(lam.astype(jnp.float32))
    a = jnp.exp(log_a)
    u = jnp.sqrt(-jnp.expm1(2.0 * log_a)) * (i * x.astype(jnp.float32))

    def combine(left, right):
        a1, b1 = left
        a2, b2 = right
        return a1 * a2, a2 * b1 + b2

    _, hs = lax.associative_scan(combine, (a, u), axis=1)
    return hs.astype(x.dtype)

def recurrent_mixer(h, w_in, conv_w, conv_b, w_a, b_a, w_x, b_x, lam, w_out):
    gate, xr = jnp.split(h @ w_in, 2, axis=-1)
    gate = jax.nn.gelu(gate, approximate=True)
    xr = causal_conv(xr, conv_w, conv_b)
    return (rg_lru(xr, w_a, b_a, w_x, b_x, lam) * gate) @ w_out

def second_inputs(seed: int = 0) -> dict:
    key = jax.random.key(seed)
    ks = jax.random.split(key, 24)
    f32 = jnp.float32

    def nrm(k, shape, scale):
        return jax.random.normal(k, shape, f32) * scale

    def unif(k, shape, lo, hi):
        return jax.random.uniform(k, shape, f32, lo, hi)

    x = nrm(ks[0], (BATCH, SEQ, D_MODEL), 1.0)
    norm_g = 1.0 + nrm(ks[1], (DEPTH, 6, D_MODEL), 0.05)
    ffn_w_in = nrm(ks[2], (DEPTH, 2, D_MODEL, 2 * D_FF), D_MODEL ** -0.5)
    ffn_w_out = nrm(ks[3], (DEPTH, 2, D_FF, D_MODEL), D_FF ** -0.5)
    hyb_w_in = nrm(ks[4], (N_HYB, D_MODEL, HYB_IN), D_MODEL ** -0.5)
    ssm_conv_w = nrm(ks[5], (N_HYB, CONV_K_2, SSM_CONV_DIM), CONV_K_2 ** -0.5)
    ssm_conv_b = nrm(ks[6], (N_HYB, SSM_CONV_DIM), 0.02)
    dt0 = jnp.exp(unif(ks[7], (N_HYB, SSM_HEADS), math.log(1e-3), math.log(1e-1)))
    ssm_dt_bias = dt0 + jnp.log(-jnp.expm1(-dt0))
    ssm_a_log = jnp.log(unif(ks[8], (N_HYB, SSM_HEADS), 1.0, 16.0))
    ssm_d = 1.0 + nrm(ks[9], (N_HYB, SSM_HEADS), 0.1)
    ssm_norm_g = 1.0 + nrm(ks[10], (N_HYB, D_SSM), 0.05)
    fox_b_f = unif(ks[11], (N_HYB, FOX_HEADS), 1.0, 4.0)
    hyb_w_out = nrm(ks[12], (N_HYB, D_SSM + D_FOX, D_MODEL), (D_SSM + D_FOX) ** -0.5)
    rec_w_in = nrm(ks[13], (N_REC, D_MODEL, 2 * D_RNN), D_MODEL ** -0.5)
    rec_conv_w = nrm(ks[14], (N_REC, CONV_K_2, D_RNN), CONV_K_2 ** -0.5)
    rec_conv_b = nrm(ks[15], (N_REC, D_RNN), 0.02)
    rec_w_a = nrm(ks[16], (N_REC, RNN_BLOCKS, RNN_BLOCK, RNN_BLOCK), RNN_BLOCK ** -0.5)
    rec_b_a = nrm(ks[17], (N_REC, D_RNN), 0.02)
    rec_w_x = nrm(ks[18], (N_REC, RNN_BLOCKS, RNN_BLOCK, RNN_BLOCK), RNN_BLOCK ** -0.5)
    rec_b_x = nrm(ks[19], (N_REC, D_RNN), 0.02)
    a0 = unif(ks[20], (N_REC, D_RNN), 0.9, 0.999)
    s0 = a0 ** (1.0 / RG_LRU_C)
    rec_lambda = jnp.log(s0) - jnp.log1p(-s0)
    rec_w_out = nrm(ks[21], (N_REC, D_RNN, D_MODEL), D_RNN ** -0.5)
    return {"x": x, "norm_g": norm_g, "ffn_w_in": ffn_w_in, "ffn_w_out": ffn_w_out,
            "hyb_w_in": hyb_w_in, "ssm_conv_w": ssm_conv_w, "ssm_conv_b": ssm_conv_b,
            "ssm_dt_bias": ssm_dt_bias, "ssm_a_log": ssm_a_log, "ssm_d": ssm_d,
            "ssm_norm_g": ssm_norm_g, "fox_b_f": fox_b_f, "hyb_w_out": hyb_w_out,
            "rec_w_in": rec_w_in, "rec_conv_w": rec_conv_w, "rec_conv_b": rec_conv_b,
            "rec_w_a": rec_w_a, "rec_b_a": rec_b_a, "rec_w_x": rec_w_x, "rec_b_x": rec_b_x,
            "rec_lambda": rec_lambda, "rec_w_out": rec_w_out}

def second_block(x, norm_g, ffn_w_in, ffn_w_out, hyb_w_in, ssm_conv_w, ssm_conv_b, ssm_dt_bias,
              ssm_a_log, ssm_d, ssm_norm_g, fox_b_f, hyb_w_out, rec_w_in, rec_conv_w, rec_conv_b,
              rec_w_a, rec_b_a, rec_w_x, rec_b_x, rec_lambda, rec_w_out):
    for layer in range(DEPTH):
        g = norm_g[layer]
        h = swiglu(rms_norm_2(x, g[0]), ffn_w_in[layer, 0], ffn_w_out[layer, 0])
        x = x + 0.5 * rms_norm_2(h, g[1])
        h = rms_norm_2(x, g[2])
        if layer % 2 == 0:
            i = layer // 2
            h = hybrid_mixer(h, hyb_w_in[i], ssm_conv_w[i], ssm_conv_b[i], ssm_dt_bias[i],
                             ssm_a_log[i], ssm_d[i], ssm_norm_g[i], fox_b_f[i], hyb_w_out[i])
        else:
            j = layer // 2
            h = recurrent_mixer(h, rec_w_in[j], rec_conv_w[j], rec_conv_b[j], rec_w_a[j], rec_b_a[j],
                                rec_w_x[j], rec_b_x[j], rec_lambda[j], rec_w_out[j])
        x = x + rms_norm_2(h, g[3])
        h = swiglu(rms_norm_2(x, g[4]), ffn_w_in[layer, 1], ffn_w_out[layer, 1])
        x = x + 0.5 * rms_norm_2(h, g[5])
    return x


def setup_inputs(seed=0):
    out = dict(first_inputs(seed))
    for name, value in second_inputs(seed + 1).items():
        if name != "x":
            out[name + "_2"] = value
    return out


def reference(
    x, norm_g, w_in, gm_ln_g, gm_ln_b, gm_w_s, gm_b_s, ret_decay_logit, ret_norm_g, gdn_conv_w,
    gdn_a_log, gdn_dt_bias, gdn_norm_g, w_gate, w_branch_out, w_out, final_norm_g, norm_g_2,
    ffn_w_in_2, ffn_w_out_2, hyb_w_in_2, ssm_conv_w_2, ssm_conv_b_2, ssm_dt_bias_2, ssm_a_log_2,
    ssm_d_2, ssm_norm_g_2, fox_b_f_2, hyb_w_out_2, rec_w_in_2, rec_conv_w_2, rec_conv_b_2,
    rec_w_a_2, rec_b_a_2, rec_w_x_2, rec_b_x_2, rec_lambda_2, rec_w_out_2,
):
    x = first_block(
        x, norm_g, w_in, gm_ln_g, gm_ln_b, gm_w_s, gm_b_s, ret_decay_logit, ret_norm_g,
        gdn_conv_w, gdn_a_log, gdn_dt_bias, gdn_norm_g, w_gate, w_branch_out, w_out,
        final_norm_g,
    )
    return second_block(
        x, norm_g_2, ffn_w_in_2, ffn_w_out_2, hyb_w_in_2, ssm_conv_w_2, ssm_conv_b_2,
        ssm_dt_bias_2, ssm_a_log_2, ssm_d_2, ssm_norm_g_2, fox_b_f_2, hyb_w_out_2, rec_w_in_2,
        rec_conv_w_2, rec_conv_b_2, rec_w_a_2, rec_b_a_2, rec_w_x_2, rec_b_x_2, rec_lambda_2,
        rec_w_out_2,
    )


_drawn_inputs = setup_inputs


def setup_inputs(seed=0):
    import zlib

    import numpy as np

    out = dict(_drawn_inputs(seed))
    spreads = {}
    factors = {'gm_ln_b': 6.426, 'rec_b_a_2': 30.761, 'rec_b_x_2': 8.0}
    for name, (base, spread) in spreads.items():
        noise = np.random.default_rng([zlib.crc32(name.encode()), seed]).standard_normal(out[name].shape)
        drawn = base * np.exp(spread * noise) if base else spread * noise
        out[name] = __import__('jax').numpy.asarray(drawn.astype(out[name].dtype))
    for name, factor in factors.items():
        out[name] = (out[name] * factor).astype(out[name].dtype)
    return out
```

```python
from contextlib import ExitStack

import concourse.bass as bass
from concourse import mybir
import numpy as np

F32 = mybir.dt.float32
F32R = mybir.dt.float32r
I32 = mybir.dt.int32
ALU = mybir.AluOpType
ACT = mybir.ActivationFunctionType
AX = mybir.AxisListType

P = 128
S = 256
M = S // P
D = 1024
DEPTH = 2
BW = 512
NH = 4
HD = 128
FF = 2816
EPS = 1e-6
UNIT = 2048
RAW_SLOTS = 3
SPLIT_SLOTS = 3
KD = D // P
KF = FF // P

W_IN_STAGES = (("dq", 7), ("dk", 8), ("dv", 9), ("dz", 10), ("rq", 3), ("rk", 4), ("rv", 5), ("rz", 6),
               ("gu", 0), ("gv", 1), ("gz", 2))
FF_WIDTHS = (512,) * 5 + (256,)
HYB_SPLIT = (("z", 0, 2), ("xbc", 1024, 3), ("q", 2576, 2), ("k", 3600, 2), ("v", 4624, 2))


def units_of(rows, width):
    per, chunks = UNIT // width, rows // P
    return [min(per, chunks - c) for c in range(0, chunks, per)]


def pack_block(matrix, col, width):
    out, row = [], 0
    for kc in units_of(matrix.shape[0], width):
        u = np.zeros((P, UNIT), np.float32)
        part = matrix[row:row + kc * P, col:col + width].reshape(kc, P, width).transpose(1, 0, 2)
        u[:, :kc * width] = part.reshape(P, kc * width)
        out.append(u)
        row += kc * P
    return out


def pack_ffn(w_in, w_out):
    out, col = [], 0
    for w in FF_WIDTHS:
        out += pack_block(w_in, col, w) + pack_block(w_in, FF + col, w)
        col += w
    for b in range(2):
        out += pack_block(w_out, 512 * b, 512)
    return out


def pack_weights(a):
    out = []
    for l in range(DEPTH):
        for _, b in W_IN_STAGES:
            out += pack_block(a["w_in"][l], 512 * b, 512)
        for n in range(3):
            for b in range(2):
                out += pack_block(a["w_gate"][l, :, n, :], 512 * b, 512)
            for b in range(2):
                out += pack_block(a["w_branch_out"][l, n], 512 * b, 512)
        for b in range(2):
            out += pack_block(a["w_out"][l], 512 * b, 512)
    out += pack_ffn(a["ffn_w_in_2"][0, 0], a["ffn_w_out_2"][0, 0])
    for _, col, n in HYB_SPLIT:
        for b in range(n):
            out += pack_block(a["hyb_w_in_2"][0], col + 512 * b, 512)
    for b in range(2):
        out += pack_block(a["hyb_w_out_2"][0], 512 * b, 512)
    out += pack_ffn(a["ffn_w_in_2"][0, 1], a["ffn_w_out_2"][0, 1])
    out += pack_ffn(a["ffn_w_in_2"][1, 0], a["ffn_w_out_2"][1, 0])
    for b in range(4):
        out += pack_block(a["rec_w_in_2"][0], 512 * b, 512)
    for b in range(2):
        out += pack_block(a["rec_w_out_2"][0], 512 * b, 512)
    out += pack_ffn(a["ffn_w_in_2"][1, 1], a["ffn_w_out_2"][1, 1])
    return np.stack(out)


def cols(v):
    return np.asarray(v, np.float32).reshape(-1, P).T


def rows(v):
    v = np.asarray(v, np.float32).reshape(1, -1)
    return np.broadcast_to(v, (P, v.shape[1]))


def chunked(m):
    k, n = m.shape
    return np.asarray(m, np.float32).reshape(k // P, P, n).transpose(1, 0, 2).reshape(P, -1)


FP = {}
_at = 0
for _n, _w in (("small_w", KD * 16), ("norm_g", KD), ("conv", 36), ("dtb", 8), ("a_log", 8), ("ret_g", 4),
               ("gdn_g", 1), ("b_s", 4), ("decay", 8)):
    FP[_n] = (_at, _at + _w)
    _at += _w
FP_W = _at
SP = {}
_at = 0
for _n, _w in (("small_w", KD * 24), ("g0", KD), ("g2", KD), ("g4", KD), ("conv", 48), ("conv_b", 12),
               ("dtb", 16), ("a_log", 16), ("d", 16), ("norm_g", KD), ("fox_b", 8)):
    SP[_n] = (_at, _at + _w)
    _at += _w
SP_W = _at
RP = {}
_at = 0
for _n, _w in (("g0", KD), ("g2", KD), ("g4", KD), ("conv", 32), ("conv_b", 8), ("b_a", 8), ("b_x", 8), ("lam", 8)):
    RP[_n] = (_at, _at + _w)
    _at += _w
RP_W = _at
PAR_W = max(FP_W, SP_W, RP_W)


def pack_params(a):
    out = np.zeros((4, P, PAR_W), np.float32)
    for l in range(DEPTH):
        parts = {
            "small_w": chunked(a["w_in"][l][:, 11 * 512:]), "norm_g": cols(a["norm_g"][l]),
            "conv": np.concatenate([cols(a["gdn_conv_w"][l, k]) for k in range(3)], 1),
            "dtb": rows(a["gdn_dt_bias"][l]), "a_log": rows(a["gdn_a_log"][l]),
            "ret_g": cols(a["ret_norm_g"][l]), "gdn_g": cols(a["gdn_norm_g"][l]),
            "b_s": np.asarray(a["gm_b_s"][l]).T, "decay": rows(a["ret_decay_logit"][l]),
        }
        for n, v in parts.items():
            out[l, :, FP[n][0]:FP[n][1]] = v
    w = a["hyb_w_in_2"][0]
    g = a["norm_g_2"]
    parts = {
        "small_w": chunked(np.concatenate([w[:, 2560:2576], w[:, 5648:5656]], 1)),
        "g0": cols(g[0, 0]), "g2": cols(g[0, 2]), "g4": cols(g[0, 4]),
        "conv": np.concatenate([cols(a["ssm_conv_w_2"][0, k]) for k in range(4)], 1),
        "conv_b": cols(a["ssm_conv_b_2"][0]), "dtb": rows(a["ssm_dt_bias_2"][0]),
        "a_log": rows(a["ssm_a_log_2"][0]), "d": rows(a["ssm_d_2"][0]), "norm_g": cols(a["ssm_norm_g_2"][0]),
        "fox_b": rows(a["fox_b_f_2"][0]),
    }
    for n, v in parts.items():
        out[2, :, SP[n][0]:SP[n][1]] = v
    parts = {
        "g0": cols(g[1, 0]), "g2": cols(g[1, 2]), "g4": cols(g[1, 4]),
        "conv": np.concatenate([cols(a["rec_conv_w_2"][0, k]) for k in range(4)], 1),
        "conv_b": cols(a["rec_conv_b_2"][0]), "b_a": cols(a["rec_b_a_2"][0]), "b_x": cols(a["rec_b_x_2"][0]),
        "lam": cols(a["rec_lambda_2"][0]),
    }
    for n, v in parts.items():
        out[3, :, RP[n][0]:RP[n][1]] = v
    return out


def pack_wide(a):
    g = a["norm_g_2"]
    v = [g[0, 1], g[0, 3], g[0, 5], g[1, 1], g[1, 3], g[1, 5], a["final_norm_g"]]
    v += [np.concatenate([a["gm_ln_g"][l], a["gm_ln_b"][l]]) for l in range(DEPTH)]
    return np.ascontiguousarray(np.stack([np.broadcast_to(np.asarray(x, np.float32), (P, D)) for x in v]))


def pack_token_mix(a):
    ws = np.ascontiguousarray(np.asarray(a["gm_w_s"]).transpose(0, 3, 1, 2).reshape(DEPTH, P, 4 * P))
    wax = [np.asarray(a[n][0]).transpose(1, 0, 2).reshape(P, 8 * P) for n in ("rec_w_a_2", "rec_w_x_2")]
    return ws, np.ascontiguousarray(np.stack(wax))


CONST_NAMES = ("ident", "up64", "lo64", "los64", "ups64", "same64", "half0", "half1",
               "nlo1", "nlo2", "nlo4", "nlo8", "nlo16", "nlo32", "nup1", "up128", "ones", "neg_causal")


def constants():
    i = np.arange(P)
    p, f = i[:, None], i[None, :]
    same = (p // 64) == (f // 64)
    c = {
        "ident": p == f, "up64": same & (p <= f), "lo64": same & (p >= f), "los64": same & (p > f),
        "ups64": same & (p < f), "same64": same, "half0": (p < 64) & (f >= 0), "half1": (p >= 64) & (f >= 0),
        "up128": p <= f, "ones": np.ones((P, P)), "neg_causal": np.where(f > p, -1e30, 0.0),
    }
    for s in (1, 2, 4, 8, 16, 32):
        c[f"nlo{s}"] = -1.0 * ((p // (2 * s) == f // (2 * s)) & (p // s > f // s))
    c["nup1"] = c["nlo1"].T
    main = np.concatenate([np.asarray(c[n], np.float32) for n in CONST_NAMES], 1)
    inv = np.float32(10000.0) ** (-np.arange(0, HD, 2, dtype=np.float32) / np.float32(HD))
    ang = np.arange(S, dtype=np.float32)[:, None] * inv[None, :]
    rope = [t.reshape(M, P, HD // 2).transpose(1, 0, 2).reshape(P, M * HD // 2) for t in (np.cos(ang), np.sin(ang))]
    dist = []
    for sign in (1, -1):
        for jm in range(M):
            q = np.arange(S)[None, :]
            k = (jm * P + i)[:, None]
            dist.append(np.maximum(sign * (q - k), 0))
    return (np.ascontiguousarray(np.concatenate([main] + rope, 1).astype(np.float32)),
            np.ascontiguousarray(np.concatenate(dist, 1).astype(np.float32)))


class Counter:

    def __init__(self, eng, sems, own):
        self.eng, self.sems, self.own, self.seen = eng, sems, own, {}

    def wait(self, name, k=1):
        self.seen[name] = self.seen.get(name, 0) + k
        self.eng.wait_ge(self.sems[name], self.seen[name])

    def sig(self, ins, name):
        ins.then_inc(self.sems[name], 1)
        self.wait(name)

    def step(self, ins):
        self.sig(ins, self.own)


class Stream:

    def __init__(self):
        self.split = self.used = self.block = 0
        self.evacs = {"evac_act": 0, "evac_dve": 0}
        self.history = []


def program(nc, x_in, weights, params, wide, token_mix, gate_mix, const, dist, out):
    NU = weights.shape[0]
    with ExitStack() as ctx:
        def sb(name, shape, dt=F32):
            return ctx.enter_context(nc.sbuf_tensor(name, shape, dt))

        SEMS = (
            "a_ready", "act_step", "back_read", "back_tr", "cb_ready", "const_landed", "conv_act", "conv_read",
            "conv_tr", "cum_done", "cum_exp", "cum_read", "cum_t", "cum_t_read", "decay_ready", "dist_landed",
            "dve_step", "evac_act", "evac_dve", "feat_read", "feat_tr", "final_g_landed", "fox_done",
            "fox_read", "gate_abs", "gate_exp", "gate_g", "gram_done", "gt_done", "h_ready", "inv_t", "inv_tm",
            "inv_x", "inv_y", "inv_yt", "kv_done", "lam_ready", "layer_done", "lin_done", "logits_read",
            "logits_ready", "low_ready", "low_t", "low_t_read", "mask_arg", "mask_ready", "mix_done",
            "mix_landed", "o_ready", "o_sq", "out_landed", "out_read", "ov_done", "params_landed",
            "probs_ready", "product_sq", "probs_t", "probs_t_read", "qk_done", "qk_ready", "r_ready", "rec_out", "rhs_ready",
            "row_done", "rs_ready", "sc_ready", "small_done", "small_read", "small_w_high", "small_w_low",
            "split_high", "split_low", "sq_done", "sq_free", "sq_ready", "ssd_decay", "ssd_done", "ssd_mask",
            "state_ready", "state_zero", "sv_done", "sv_read", "tr_done", "tr_high", "tr_low", "u_ready",
            "u_sqrt", "unit_used", "uw_done", "uw_read", "v_ready", "vn_ready", "wide_landed", "ws_done",
            "x_landed", "x_ready", "x_squares", "y_ready",
        )
        sem = {n: ctx.enter_context(nc.semaphore(n)) for n in SEMS}
        weight_landed = [ctx.enter_context(nc.semaphore(f"weight_landed{i}")) for i in range(RAW_SLOTS)]

        raw = sb("raw", [P, RAW_SLOTS, UNIT])
        wh = sb("wh", [P, SPLIT_SLOTS, UNIT], F32R)
        wl = sb("wl", [P, SPLIT_SLOTS, UNIT], F32R)
        hTh = sb("hTh", [P, KF, S], F32R)
        hTl = sb("hTl", [P, KF, S], F32R)
        x = sb("x", [P, M, D])
        xn = sb("xn", [P, M * D])
        cst = sb("cst", [P, const.shape[1]])
        par = sb("par", [P, PAR_W])
        swh = sb("swh", [P, KD * 24], F32R)
        swl = sb("swl", [P, KD * 24], F32R)
        sm = sb("sm", [P, 948])
        arena = sb("arena", [P, 14848])
        pg = ctx.enter_context(nc.psum_tensor("pg", [P, 4, 512], F32))
        ps = ctx.enter_context(nc.psum_tensor("ps", [P, 4, 512], F32))

        C = {n: cst[:, i * P:(i + 1) * P] for i, n in enumerate(CONST_NAMES)}
        at = len(CONST_NAMES) * P
        COS = cst[:, at:at + P].rearrange("p (m d) -> p m d", m=M)
        SIN = cst[:, at + P:at + 2 * P].rearrange("p (m d) -> p m d", m=M)
        ident = C["ident"]

        def V(off, n=1024):
            return arena[:, off:off + n]

        def heads(ap, n=NH):
            return ap.rearrange("p (h e) -> p h e", h=n)

        def fp(name):
            return par[:, FP[name][0]:FP[name][1]]

        def spar(name):
            return par[:, SP[name][0]:SP[name][1]]

        def rp(name):
            return par[:, RP[name][0]:RP[name][1]]

        def over(ap, n):
            return ap.unsqueeze(2).broadcast_to([ap.shape[0], ap.shape[1], n])

        def times(ap, n):
            return ap.unsqueeze(1).broadcast_to([ap.shape[0], n, ap.shape[1]])

        SS, RS, SS4, SX4 = sm[:, 0:2], sm[:, 2:4], sm[:, 4:8], sm[:, 940:944]
        SPL = sm[:, 8:24]
        STATS = sm[:, 24:32]
        STATR = sm[:, 32:40]
        ABS = sm[:, 56:72]
        BETA = sm[:, 72:88]
        GLOG = sm[:, 88:104]
        NEGA = sm[:, 104:112]
        GC = sm[:, 112:128]
        NGC = sm[:, 128:144]
        EGC = sm[:, 144:160]
        EKD = sm[:, 160:176]
        EGL = sm[:, 176:208]
        BEG = sm[:, 208:224]
        TOT = sm[:, 224:240]
        BN = sm[:, 240:288]
        MV = sm[:, 288:304]
        GL = sm[:, 304:336]
        LAM, E8, TMP8 = sm[:, 336:344], sm[:, 8:16], sm[:, 16:24]
        GCT = sm[0:8, 344:600]
        SMR = sm[:, 600:616]
        NEWTON = sm[:, 892:940]
        QS = sm[:, 616:632]

        SAB, SG, SCUM = sm[:, 40:88], sm[:, 88:136], sm[:, 136:184]
        DT, SEXP = sm[:, 232:264], sm[:, 264:312]
        SCUMT, SCUMTN = sm[0:24, 344:600], sm[0:24, 632:888]
        SNEGA = sm[:, 312:336]
        NMAX, RSUM = sm[:, 600:616], sm[:, 616:632]

        kn, vt, knT, qnT, o_acc = V(0), V(1024), V(2048), V(3072), V(4096)
        Lm, LT, X_, XT_, TM_ = V(5120), V(6144), V(7168), V(8192), V(9216)
        U_, WT_ = V(10240, 2048), V(12288, 2048)
        SCT = xn[:, :]
        rawp = [V(5120), V(6144), V(7168)]
        cvp = [V(8192), V(9216), V(10240)]
        sq, qn = V(12288), V(13312)

        X_AT = KF - KD
        EARLY = range(X_AT // 2)
        LATE = range(X_AT // 2, KF // 2)

        block = ctx.enter_context(nc.Block())

        @block.tensor
        def _(pe):
            c = Counter(pe, sem, None)
            st = Stream()

            def split_product(dst, lh, ll, rh, rl, first, last):
                pe.matmul(dst, lh, rh, start=first, stop=False)
                pe.matmul(dst, lh, rl, start=False, stop=False)
                return pe.matmul(dst, ll, rh, start=False, stop=last)

            groups = {"made": 0, "waited": 0}
            group_of = {}

            def low_parts_of(position):
                need = group_of.get(position, 0)
                if need > groups["waited"]:
                    pe.wait_ge(sem["tr_low"], need)
                    groups["waited"] = need

            def gemm(rows_, widths, evacs, chunk0=0, order=None, between=None):
                units_done = 0
                for w, by in zip(widths, evacs):
                    if st.block >= 2:
                        pe.wait_ge(sem[st.history[-2][0]], st.history[-2][1])
                    pair = st.block % 2
                    k = 0
                    units = units_of(rows_, w)
                    for kc in units:
                        slot = st.used % SPLIT_SLOTS
                        pe.wait_ge(sem["split_low"], st.used + 1)
                        for i in range(kc):
                            ch = order[k] if order else chunk0 + k
                            low_parts_of(ch)
                            for m in range(M):
                                last = split_product(
                                    pg[:, 2 * pair + m, 0:w], hTh[:, ch, m * P:(m + 1) * P],
                                    hTl[:, ch, m * P:(m + 1) * P], wh[:, slot, i * w:(i + 1) * w],
                                    wl[:, slot, i * w:(i + 1) * w], k == 0, k == rows_ // P - 1)
                            k += 1
                        last.then_inc(sem["unit_used"], 1)
                        st.used += 1
                        if between and units_done == 1:
                            between()
                        units_done += 1
                    st.evacs[by] += 1
                    st.history.append((by, st.evacs[by]))
                    st.block += 1

            def transpose_groups(src, gs, dst):
                for g in gs:
                    n = groups["made"]
                    if n - 3 > groups["waited"]:
                        pe.wait_ge(sem["tr_low"], n - 3)
                        groups["waited"] = n - 3
                    for j in range(2):
                        for m in range(M):
                            last = pe.transpose(ps[:, n % 4, (2 * j + m) * P:(2 * j + m + 1) * P],
                                                src[:, m, (2 * g + j) * P:(2 * g + j + 1) * P], ident)
                    last.then_inc(sem["tr_done"], 1)
                    groups["made"] = n + 1
                    group_of[dst + 2 * g] = group_of[dst + 2 * g + 1] = n + 1

            def transpose_split(src, chunks, dst=0, drain=True):
                transpose_groups(src, range(chunks // 2), dst)
                if drain and groups["made"] > groups["waited"]:
                    pe.wait_ge(sem["tr_low"], groups["made"])
                    groups["waited"] = groups["made"]

            def small_gemm(n):
                c.wait("small_w_low")
                for m in range(M):
                    for k in range(KD):
                        last = split_product(ps[:, m, 0:n], hTh[:, k, m * P:(m + 1) * P], hTl[:, k, m * P:(m + 1) * P],
                                             swh[:, k * n:(k + 1) * n], swl[:, k * n:(k + 1) * n], k == 0, k == KD - 1)
                last.then_inc(sem["small_done"], 1)

            def features_of_x(dst=0):
                for b in range(2):
                    c.wait("x_ready")
                    transpose_groups(x, (2 * b, 2 * b + 1), dst)

            def gdn():
                gemm(D, (512,) * 3, ("evac_act",) * 3)
                small_gemm(16)
                c.wait("small_read")
                for t in range(3):
                    pe.wait_ge(sem["evac_act"], st.evacs["evac_act"] - 2 + t)
                    if t == 2:
                        c.wait("conv_read")
                    src = rawp[t].rearrange("p (m d) -> p m d", m=M)
                    for h in range(NH):
                        for m in range(M):
                            b = 2 * (t % 2) + h // 2
                            last = pe.transpose(ps[:, b, ((h % 2) * M + m) * P:((h % 2) * M + m + 1) * P],
                                                src[:, m, h * P:(h + 1) * P], ident)
                    last.then_inc(sem["conv_tr"], 1)
                c.wait("conv_read", 2)
                for t in range(3):
                    c.wait("conv_act")
                    if t == 2:
                        c.wait("qk_ready")
                    src = cvp[t].rearrange("p (h s) -> p h s", h=NH)
                    for m in range(M):
                        for h in range(NH):
                            last = pe.transpose(ps[:, 2 * (t % 2) + m, h * P:(h + 1) * P],
                                                src[:, h, m * P:(m + 1) * P], ident)
                    last.then_inc(sem["back_tr"], 1)
                c.wait("qk_ready")
                c.wait("back_read")
                for t, src in enumerate((qn, kn)):
                    s = src.rearrange("p (m d) -> p m d", m=M)
                    for h in range(NH):
                        for m in range(M):
                            last = pe.transpose(ps[:, 2 * t + h // 2, ((h % 2) * M + m) * P:((h % 2) * M + m + 1) * P],
                                                s[:, m, h * P:(h + 1) * P], ident)
                    last.then_inc(sem["feat_tr"], 1)
                c.wait("feat_read", 2)
                c.wait("gate_g")
                for m in range(M):
                    g = GLOG[:, 8 * m:8 * m + 8]
                    pe.matmul(ps[:, 0, 8 * m:8 * m + 4], C["up64"], g[:, 0:4], start=True, stop=True)
                    pe.matmul(ps[:, 0, 8 * m + 4:8 * m + 8], C["lo64"], g[:, 4:8], start=True, stop=True)
                    pe.matmul(ps[:, 0, 16 + 8 * m:24 + 8 * m], C["same64"], g, start=True, stop=True)
                    for par_ in range(2):
                        o = 32 + 8 * (2 * m + par_)
                        last = pe.matmul(ps[:, 0, o:o + 8], C[f"half{par_}"], g, start=True, stop=True)
                last.then_inc(sem["cum_done"], 1)
                c.wait("cum_read")
                for m in range(M):
                    last = pe.transpose(ps[0:8, 1, m * P:(m + 1) * P], GC[:, 8 * m:8 * m + 8], ident)
                last.then_inc(sem["cum_t"], 1)
                c.wait("cum_t_read")
                kT, qT = knT.rearrange("p (h s) -> p h s", h=NH), qnT.rearrange("p (h s) -> p h s", h=NH)
                for m in range(M):
                    tok = slice(m * P, (m + 1) * P)
                    for j in range(8):
                        last = pe.matmul(ps[:, 2 + j // 4, (j % 4) * P:(j % 4 + 1) * P],
                                         ident[0:8, j:j + 1].broadcast_to([8, P]), GCT[:, tok], start=True, stop=True)
                    last.then_inc(sem["row_done"], 1)
                    for h in range(NH):
                        pe.matmul(ps[:, 0, h * P:(h + 1) * P], kT[:, h, tok], kT[:, h, tok], start=True, stop=True)
                        last = pe.matmul(ps[:, 1, h * P:(h + 1) * P], kT[:, h, tok], qT[:, h, tok], start=True, stop=True)
                    last.then_inc(sem["gram_done"], 1)
                    c.wait("low_ready")
                    L3, LT3 = heads(Lm, 8), heads(LT, 8)
                    X3, XT3, T3 = heads(X_, 8), heads(XT_, 8), heads(TM_, 8)
                    for j in range(8):
                        last = pe.transpose(ps[:, j // 4, (j % 4) * P:(j % 4 + 1) * P], L3[:, j, :], ident)
                    last.then_inc(sem["low_t"], 1)
                    c.wait("inv_x", 2)
                    for s in (2, 4, 8, 16, 32):
                        for d in range(2):
                            AT = LT3 if d == 0 else L3
                            if s > 2:
                                c.wait("inv_x")
                            for h in range(NH):
                                j = 4 * d + h
                                last = pe.matmul(ps[:, d, h * P:(h + 1) * P], AT[:, j, :], X3[:, j, :], start=True, stop=True)
                            last.then_inc(sem["inv_t"], 1)
                        for d in range(2):
                            c.wait("inv_tm")
                            if s < 32 or d == 1:
                                for h in range(NH):
                                    j = 4 * d + h
                                    last = pe.matmul(ps[:, 2 + d, h * P:(h + 1) * P], XT3[:, j, :], T3[:, j, :],
                                                     start=True, stop=True)
                                last.then_inc(sem["inv_y"], 1)
                            if s < 32 or d == 0:
                                for h in range(NH):
                                    j = 4 * d + h
                                    last = pe.matmul(ps[:, d, h * P:(h + 1) * P], T3[:, j, :], XT3[:, j, :],
                                                     start=True, stop=True)
                                last.then_inc(sem["inv_yt"], 1)
                    c.wait("inv_x", 2)
                    c.wait("rhs_ready")
                    for j in range(8):
                        TT = (XT3 if j < 4 else X3)[:, j, :]
                        pe.matmul(ps[:, j // 4, (j % 4) * P:(j % 4 + 1) * P], TT, L3[:, j, :], start=True, stop=True)
                        last = pe.matmul(ps[:, 2 + j // 4, (j % 4) * P:(j % 4 + 1) * P], LT3[:, j, :], TT,
                                         start=True, stop=True)
                    last.then_inc(sem["uw_done"], 1)
                    c.wait("uw_read")
                S3, VN, VD = heads(X_, 8), heads(Lm, 8), heads(LT, 8)
                W4 = WT_.rearrange("p (m j s) -> p m j s", m=M, j=8)
                SC4 = SCT.rearrange("p (m j s) -> p m j s", m=M, j=8)
                c.wait("state_zero")
                for t in range(4):
                    for d in range(2):
                        ck = t if d == 0 else 3 - t
                        m, r = ck // 2, 64 * (ck % 2)
                        rs = slice(r, r + 64)
                        if t:
                            c.wait("state_ready")
                            c.wait("o_ready")
                        for h in range(NH):
                            last = pe.matmul(ps[rs, 2 * d, h * P:(h + 1) * P], W4[:, m, 4 * d + h, rs], S3[:, 4 * d + h, :],
                                             start=True, stop=True)
                        last.then_inc(sem["ws_done"], 1)
                    for d in range(2):
                        ck = t if d == 0 else 3 - t
                        m, r = ck // 2, 64 * (ck % 2)
                        rs = slice(r, r + 64)
                        c.wait("vn_ready")
                        for h in range(NH):
                            pe.matmul(ps[rs, 2 * d, h * P:(h + 1) * P], qT[:, h, ck * 64:ck * 64 + 64], S3[:, 4 * d + h, :],
                                      start=True, stop=True)
                        for h in range(NH):
                            last = pe.matmul(ps[:, 2 * d + 1, h * P:(h + 1) * P],
                                             kn[rs, (m * NH + h) * P:(m * NH + h + 1) * P],
                                             VD[rs, 4 * d + h, :], start=True, stop=True)
                        last.then_inc(sem["kv_done"], 1)
                    for d in range(2):
                        ck = t if d == 0 else 3 - t
                        m, r = ck // 2, 64 * (ck % 2)
                        rs = slice(r, r + 64)
                        c.wait("sv_read")
                        for h in range(NH):
                            last = pe.matmul(ps[rs, 2 * d, h * P:(h + 1) * P], SC4[rs, m, 4 * d + h, rs],
                                             VN[rs, 4 * d + h, :], start=True, stop=True)
                        last.then_inc(sem["sv_done"], 1)
                c.wait("state_ready", 2)
                c.wait("o_ready", 2)
                gemm(D, (512,), ("evac_act",))
                c.wait("y_ready")
                transpose_split(o_acc.rearrange("p (m d) -> p m d", m=M), NH, 8)

            def retention():
                gemm(D, (512,) * 4, ("evac_dve", "evac_dve", "evac_act", "evac_act"))
                q, k = V(0), V(1024)
                for t, src in enumerate((q, k)):
                    pe.wait_ge(sem["evac_dve"], st.evacs["evac_dve"] - 1 + t)
                    s = src.rearrange("p (m d) -> p m d", m=M)
                    for h in range(NH):
                        for m in range(M):
                            last = pe.transpose(ps[:, 2 * t + h // 2, ((h % 2) * M + m) * P:((h % 2) * M + m + 1) * P],
                                                s[:, m, h * P:(h + 1) * P], ident)
                    last.then_inc(sem["feat_tr"], 1)
                c.wait("feat_read", 2)
                pe.wait_ge(sem["evac_act"], st.evacs["evac_act"])
                kT, qT = V(2048).rearrange("p (h s) -> p h s", h=NH), V(3072).rearrange("p (h s) -> p h s", h=NH)
                v = V(4096).rearrange("p (m h e) -> p m h e", m=M, h=NH)
                for h in range(NH):
                    b = h % 2
                    if h >= 2:
                        c.wait("sc_ready")
                    for jm in range(M):
                        last = pe.matmul(ps[:, b, jm * S:(jm + 1) * S], kT[:, h, jm * P:(jm + 1) * P], qT[:, h, :],
                                         start=True, stop=True)
                    last.then_inc(sem["qk_done"], 1)
                    if h >= 1:
                        g = h - 1
                        if h == 1:
                            c.wait("sc_ready")
                        sc = V(5120 + 512 * (g % 2), 512).rearrange("p (j s) -> p j s", j=M)
                        for im in range(M):
                            for jm in range(M):
                                last = pe.matmul(ps[:, 2 + im, g * P:(g + 1) * P], sc[:, jm, im * P:(im + 1) * P],
                                                 v[:, jm, g, :], start=(jm == 0), stop=(jm == M - 1))
                        last.then_inc(sem["ov_done"], 1)
                c.wait("sc_ready")
                g = NH - 1
                sc = V(5120 + 512 * (g % 2), 512).rearrange("p (j s) -> p j s", j=M)
                for im in range(M):
                    for jm in range(M):
                        last = pe.matmul(ps[:, 2 + im, g * P:(g + 1) * P], sc[:, jm, im * P:(im + 1) * P],
                                         v[:, jm, g, :], start=(jm == 0), stop=(jm == M - 1))
                last.then_inc(sem["ov_done"], 1)
                c.wait("y_ready")
                transpose_split(V(0).rearrange("p (m d) -> p m d", m=M), NH, 12)

            def gmlp(l):
                gemm(D, (512,) * 3, ("evac_act",) * 3)
                c.wait("v_ready")
                pe.wait_ge(sem["mix_landed"], 16 * (l + 1))
                v = V(1024).rearrange("p (m g e) -> p m g e", m=M, g=NH)
                ws = V(13312, 512).rearrange("p (g q) -> p g q", g=NH)
                for m in range(M):
                    for g in range(NH):
                        last = pe.matmul(ps[:, m, g * P:(g + 1) * P], ws[:, g, :], v[:, m, g, :], start=True, stop=True)
                last.then_inc(sem["mix_done"], 1)
                c.wait("y_ready")
                transpose_split(V(0).rearrange("p (m d) -> p m d", m=M), NH, 16)

            def merge_out():
                for n in range(3):
                    gemm(D, (512,) * 2, ("evac_act",) * 2)
                    gemm(BW, (512,) * 2, ("evac_dve",) * 2, chunk0=16 - 4 * n)
                c.wait("y_ready")
                transpose_split(V(0, 2048).rearrange("p (m d) -> p m d", m=M), KD, 0, drain=False)
                gemm(D, (512,) * 2, ("evac_dve",) * 2)

            def ffn():
                features_of_x(X_AT)
                hid = V(0, 2 * FF).rearrange("p (m f) -> p m f", m=M)
                for j, w in enumerate(FF_WIDTHS):
                    gemm(D, (w, w), ("evac_act", "evac_dve"), chunk0=X_AT)
                    if j:
                        pe.wait_ge(sem["evac_dve"], st.evacs["evac_dve"] - 1)
                        transpose_groups(hid, [g for g in EARLY if g // 2 == j - 1], 0)

                def late():
                    pe.wait_ge(sem["evac_dve"], hidden_done)
                    transpose_groups(hid, LATE, 0)
                hidden_done = st.evacs["evac_dve"]
                gemm(FF, (512,) * 2, ("evac_dve",) * 2, between=late)

            def hybrid():
                features_of_x()
                gemm(D, (512,) * 5, ("evac_act",) * 5)
                small_gemm(24)
                c.wait("small_read")
                raw3 = V(0, 3072).rearrange("p (m f) -> p m f", m=M)
                pe.wait_ge(sem["evac_act"], st.evacs["evac_act"])
                for g in range(6):
                    if g >= 4:
                        c.wait("conv_read")
                    for j in range(2):
                        for m in range(M):
                            last = pe.transpose(ps[:, g % 4, (2 * j + m) * P:(2 * j + m + 1) * P],
                                                raw3[:, m, (2 * g + j) * P:(2 * g + j + 1) * P], ident)
                    last.then_inc(sem["conv_tr"], 1)
                c.wait("conv_read", 4)
                cv = V(3072, 3072).rearrange("p (k s) -> p k s", k=12)
                c.wait("conv_act")
                for m in range(M):
                    for k in range(8):
                        last = pe.transpose(ps[:, 2 * m + k // 4, (k % 4) * P:(k % 4 + 1) * P],
                                            cv[:, k, m * P:(m + 1) * P], ident)
                last.then_inc(sem["back_tr"], 1)
                c.wait("back_read")
                c.wait("gate_g")
                for m in range(M):
                    o = 24 * m
                    pe.matmul(ps[:, 0, o:o + 24], C["up128"], SG[:, 24 * m:24 * m + 24], start=True, stop=(m == 0))
                    if m:
                        last = pe.matmul(ps[:, 0, o:o + 24], C["ones"], SG[:, 0:24], start=False, stop=True)
                last.then_inc(sem["cum_done"], 1)
                c.wait("cum_read")
                for m in range(M):
                    last = pe.transpose(ps[0:24, 1, m * P:(m + 1) * P], SCUM[:, 24 * m:24 * m + 24], ident)
                last.then_inc(sem["cum_t"], 1)
                c.wait("cum_t_read")
                for g in range(2):
                    for jm in range(M):
                        n = S - jm * P
                        last = pe.matmul(ps[:, 2 + g, jm * S:jm * S + n], cv[:, 8 + g, jm * P:(jm + 1) * P],
                                         cv[:, 10 + g, jm * P:S], start=True, stop=True)
                last.then_inc(sem["gram_done"], 1)
                c.wait("cb_ready")
                Xd = V(0, 2048).rearrange("p (m h e) -> p m h e", m=M, h=16)
                for h in range(16):
                    if h >= 2:
                        c.wait("ssd_decay")
                    last = pe.matmul(ps[:, h % 2, 0:S], ident[0:24, h:h + 1].broadcast_to([24, P]), SCUMT,
                                     start=True, stop=True)
                    last.then_inc(sem["row_done"], 1)
                    if h >= 1:
                        ssd_out(h - 1, Xd)
                ssd_out(15, Xd)
                c.wait("ssd_decay", 2)
                c.wait("y_ready")
                transpose_split(V(8192, 2048).rearrange("p (m d) -> p m d", m=M), KD, 8)
                gemm(D, (512,) * 6, ("evac_act",) * 6)
                pe.wait_ge(sem["evac_act"], st.evacs["evac_act"])
                for t in range(2):
                    src = V(2048 * t, 2048).rearrange("p (m d) -> p m d", m=M)
                    for g in range(4):
                        if t:
                            c.wait("feat_read")
                        for j in range(2):
                            for m in range(M):
                                last = pe.transpose(ps[:, g, (2 * j + m) * P:(2 * j + m + 1) * P],
                                                    src[:, m, (2 * g + j) * P:(2 * g + j + 1) * P], ident)
                        last.then_inc(sem["feat_tr"], 1)
                c.wait("feat_read", 4)
                qT, kT = (V(o, 2048).rearrange("p (h s) -> p h s", h=8) for o in (6144, 8192))
                v = V(4096, 2048).rearrange("p (m h e) -> p m h e", m=M, h=8)
                for h in range(8):
                    b = h % 2
                    if h >= 2:
                        c.wait("logits_read")
                    for m in range(M):
                        n = (m + 1) * P
                        pe.matmul(ps[:, b, m * S:m * S + n], qT[:, h, m * P:(m + 1) * P], kT[:, h, 0:n],
                                  start=True, stop=False)
                        last = pe.matmul(ps[:, b, m * S:m * S + n], ident[0:24, 16 + h:17 + h].broadcast_to([24, P]),
                                         SCUMTN[:, 0:n], start=False, stop=True)
                    last.then_inc(sem["qk_done"], 1)
                    if h >= 1:
                        fox_out(h - 1, v)
                fox_out(7, v)
                c.wait("logits_read", 2)
                c.wait("fox_read")
                transpose_split(V(10240, 2048).rearrange("p (m d) -> p m d", m=M), KD, 0, drain=False)
                gemm(2 * D, (512,) * 2, ("evac_dve",) * 2, order=[8 + i for i in range(8)] + list(range(8)))

            def ssd_out(h, Xd):
                c.wait("ssd_mask")
                E = V(6144 + 512 * (h % 2), 384)
                q = h % 8
                for im in range(M):
                    dst = ps[:, 2 + im, q * 64:(q + 1) * 64]
                    if h == 8 and im == 0:
                        c.wait("out_read")
                    pe.matmul(dst, E[:, im * P:(im + 1) * P], Xd[:, 0, h, :], start=True, stop=(im == 0))
                    if im:
                        last = pe.matmul(dst, E[:, 2 * P:3 * P], Xd[:, 1, h, :], start=False, stop=True)
                last.then_inc(sem["ssd_done"], 1)

            def fox_out(h, v):
                c.wait("probs_ready")
                pr = V(12288 + 512 * (h % 2), 384)
                if h >= 1:
                    c.wait("fox_read")
                for i in range(3):
                    last = pe.transpose(ps[:, 2, i * P:(i + 1) * P], pr[:, i * P:(i + 1) * P], ident)
                last.then_inc(sem["probs_t"], 1)
                c.wait("probs_t_read")
                pT = V(13312, 384)
                pe.matmul(ps[:, 3, 0:P], pT[:, 0:P], v[:, 0, h, :], start=True, stop=True)
                pe.matmul(ps[:, 3, P:2 * P], pT[:, P:2 * P], v[:, 0, h, :], start=True, stop=False)
                last = pe.matmul(ps[:, 3, P:2 * P], pT[:, 2 * P:3 * P], v[:, 1, h, :], start=False, stop=True)
                last.then_inc(sem["fox_done"], 1)

            def recurrent():
                features_of_x()
                gemm(D, (512,) * 4, ("evac_act",) * 4)
                pe.wait_ge(sem["evac_act"], st.evacs["evac_act"])
                xr = V(0, 2048).rearrange("p (m f) -> p m f", m=M)
                for g in range(4):
                    for j in range(2):
                        for m in range(M):
                            last = pe.transpose(ps[:, g, (2 * j + m) * P:(2 * j + m + 1) * P],
                                                xr[:, m, (2 * g + j) * P:(2 * g + j + 1) * P], ident)
                    last.then_inc(sem["conv_tr"], 1)
                c.wait("conv_read", 4)
                pe.wait_ge(sem["mix_landed"], 16 * (DEPTH + 1))
                xT = V(4096, 2048).rearrange("p (n s) -> p n s", n=8)
                for t in range(2):
                    wt = V(11776 + 1024 * t).rearrange("p (n k) -> p n k", n=8)
                    for n in range(8):
                        last = pe.matmul(ps[:, n // 2, (n % 2) * S:(n % 2 + 1) * S], wt[:, n, :], xT[:, n, :],
                                         start=True, stop=True)
                    last.then_inc(sem["lin_done"], 1)
                    c.wait("r_ready")
                gt = V(2048, 2048).rearrange("p (m f) -> p m f", m=M)
                for g in range(4):
                    for j in range(2):
                        for m in range(M):
                            last = pe.transpose(ps[:, g, (2 * j + m) * P:(2 * j + m + 1) * P],
                                                gt[:, m, (2 * g + j) * P:(2 * g + j + 1) * P], ident)
                last.then_inc(sem["gt_done"], 1)
                groups["made"] += 1
                for k in range(KD):
                    group_of[k] = groups["made"]
                gemm(D, (512,) * 2, ("evac_dve",) * 2)

            pe.wait_ge(sem["const_landed"], 16)
            for l in range(DEPTH):
                features_of_x()
                gdn()
                retention()
                gmlp(l)
                merge_out()
            ffn()
            hybrid()
            ffn()
            ffn()
            recurrent()
            ffn()

        @block.scalar
        def _(act):
            c = Counter(act, sem, "act_step")
            st = Stream()

            def pump(to):
                while st.split < min(to, NU):
                    u = st.split
                    slot = u % SPLIT_SLOTS
                    act.wait_ge(weight_landed[u % RAW_SLOTS], 16 * (u // RAW_SLOTS + 1))
                    if u >= SPLIT_SLOTS:
                        act.wait_ge(sem["unit_used"], u - SPLIT_SLOTS + 1)
                    act.activation(wh[:, slot, :], raw[:, u % RAW_SLOTS, :], ACT.Copy).then_inc(sem["split_high"], 1)
                    st.split += 1

            def gemm(rows_, widths, evacs, read=None):
                for i, (w, by) in enumerate(zip(widths, evacs)):
                    st.used += len(units_of(rows_, w))
                    pump(st.used + 2)
                    if by == "evac_act":
                        act.wait_ge(sem["unit_used"], st.used)
                        read(i, 2 * (st.block % 2), w).then_inc(sem["evac_act"], 1)
                    st.evacs[by] += 1
                    st.block += 1
                pump(st.used + 3)

            made = [0]

            def split_groups(gs, dst, gain=None):
                for g in gs:
                    bank = made[0] % 4
                    made[0] += 1
                    c.wait("tr_done")
                    if gain is None:
                        last = act.activation(hTh[:, dst + 2 * g:dst + 2 * g + 2, :],
                                              ps[:, bank, :].rearrange("p (k s) -> p k s", k=2), ACT.Copy)
                    else:
                        for j in range(2):
                            k = 2 * g + j
                            last = act.activation(hTh[:, dst + k, :], ps[:, bank, j * S:(j + 1) * S], ACT.Copy,
                                                  scale=gain(k))
                    last.then_inc(sem["tr_high"], 1)

            def transpose_split(chunks, dst, gain=None):
                split_groups(range(chunks // 2), dst, gain)

            def features_of_x(gain, dst=0):
                for b in range(2):
                    c.wait("x_ready")
                    for m in range(M):
                        last = act.activation(xn[:, 0:512], x[:, m, 512 * b:512 * b + 512], ACT.Square,
                                              accum_out=SX4[:, 2 * b + m:2 * b + m + 1])
                        if 2 * b + m < 3:
                            c.step(last)
                    if b:
                        last.then_inc(sem["x_squares"], 1)
                    split_groups((2 * b, 2 * b + 1), dst, gain)
                c.wait("rs_ready")

            def small_w(n, name):
                act.activation(swh[:, 0:KD * n], name[:, 0:KD * n], ACT.Copy).then_inc(sem["small_w_high"], 1)

            def copy_tile(dst):
                return lambda pair: [act.activation(dst[:, m, :], pg[:, pair + m, :], ACT.Copy) for m in range(M)][-1]

            def read_pair(dst, pair, f, w=512):
                c.step(act.activation(dst[:, 0, :], pg[:, pair, 0:w], f, scale=RS[:, 0:1]))
                return act.activation(dst[:, 1, :], pg[:, pair + 1, 0:w], f, scale=RS[:, 1:2])

            def tiles(ap):
                return ap.rearrange("p (m d) -> p m d", m=M)

            def gdn():
                def read(i, pair, w):
                    d3 = rawp[i].rearrange("p (m d) -> p m d", m=M)
                    return read_pair(d3, pair, ACT.Copy)
                gemm(D, (512,) * 3, ("evac_act",) * 3, read)
                c.wait("gate_abs")
                c.step(act.activation(SPL, ABS, ACT.Exp, scale=-1.0))
                c.step(act.activation(NEGA, fp("a_log"), ACT.Exp))
                c.step(act.activation(SMR, QS, ACT.Exp, scale=-1.0))
                act.activation(SPL, SPL, ACT.Ln, bias=1.0).then_inc(sem["gate_exp"], 1)
                for t in range(3):
                    c.wait("conv_read")
                    act.activation(cvp[t], cvp[t], ACT.Silu).then_inc(sem["conv_act"], 1)
                for t in range(2):
                    c.wait("back_tr")
                    if t:
                        c.wait("sq_free")
                    for m in range(M):
                        last = act.activation(sq[:, 512 * m:512 * m + 512], ps[:, 2 * t + m, :], ACT.Square)
                    last.then_inc(sem["sq_ready"], 1)
                c.wait("back_tr")
                for m in range(M):
                    last = act.activation(vt[:, 512 * m:512 * m + 512], ps[:, m, :], ACT.Copy)
                    if m == 0:
                        c.step(last)
                last.then_inc(sem["back_read"], 1)
                c.wait("sq_free")
                for t, dst in enumerate((qnT, knT)):
                    c.wait("feat_tr")
                    c.step(act.activation(dst[:, 0:512], ps[:, 2 * t, :], ACT.Copy))
                    act.activation(dst[:, 512:1024], ps[:, 2 * t + 1, :], ACT.Copy).then_inc(sem["feat_read"], 1)
                c.wait("cum_read")
                c.step(act.activation(EGC, GC, ACT.Exp))
                c.step(act.activation(EKD, EKD, ACT.Exp))
                act.activation(EGL, GL, ACT.Exp).then_inc(sem["cum_exp"], 1)
                U4 = U_.rearrange("p (m n) -> p m n", m=M)
                W4 = WT_.rearrange("p (m n) -> p m n", m=M)
                for m in range(M):
                    c.wait("row_done")
                    for j in range(8):
                        row = ps[:, 2 + j // 4, (j % 4) * P:(j % 4 + 1) * P]
                        col = slice(8 * m + j, 8 * m + j + 1)
                        act.activation(X_[:, j * P:(j + 1) * P], row, ACT.Relu, scale=1.0, bias=NGC[:, col])
                        last = act.activation(XT_[:, j * P:(j + 1) * P], row, ACT.Relu, scale=-1.0, bias=GC[:, col])
                    c.step(last)
                    act.activation(X_, X_, ACT.Exp, scale=-1.0)
                    act.activation(XT_, XT_, ACT.Exp, scale=-1.0).then_inc(sem["decay_ready"], 1)
                    c.wait("low_t")
                    c.step(act.activation(LT[:, 0:512], ps[:, 0, :], ACT.Copy))
                    act.activation(LT[:, 512:1024], ps[:, 1, :], ACT.Copy).then_inc(sem["low_t_read"], 1)
                    c.wait("uw_done")
                    for b in range(2):
                        c.step(act.activation(U4[:, m, 512 * b:512 * b + 512], ps[:, b, :], ACT.Copy))
                        if b:
                            act.activation(W4[:, m, 512:1024], ps[:, 3, :], ACT.Copy).then_inc(sem["uw_read"], 1)
                        else:
                            c.step(act.activation(W4[:, m, 0:512], ps[:, 2, :], ACT.Copy))
                def read_z(i, pair, w):
                    return read_pair(tiles(V(0)), pair, ACT.Silu)
                gemm(D, (512,), ("evac_act",), read_z)
                c.wait("o_ready", 8)
                act.activation(Lm, o_acc, ACT.Square).then_inc(sem["sq_done"], 1)
                transpose_split(NH, 8, lambda k: fp("gdn_g"))

            def retention():
                def read(i, pair, w):
                    dst, f = ((V(4096), ACT.Copy), (V(7168), ACT.Silu))[i - 2]
                    return read_pair(tiles(dst), pair, f)
                c.step(act.activation(E8, fp("decay"), ACT.Abs))
                c.step(act.activation(E8, E8, ACT.Exp, scale=-1.0))
                act.activation(LAM, E8, ACT.Ln, bias=1.0).then_inc(sem["lam_ready"], 1)
                c.wait("mask_arg")
                act.activation(V(8192, 2048), V(8192, 2048), ACT.Exp).then_inc(sem["mask_ready"], 1)
                gemm(D, (512,) * 4, ("evac_dve", "evac_dve", "evac_act", "evac_act"), read)
                for t, dst in enumerate((V(3072), V(2048))):
                    c.wait("feat_tr")
                    scale = 1.0 if t == 0 else HD ** -0.5
                    c.step(act.activation(dst[:, 0:512], ps[:, 2 * t, :], ACT.Copy, scale=scale))
                    act.activation(dst[:, 512:1024], ps[:, 2 * t + 1, :], ACT.Copy, scale=scale)\
                       .then_inc(sem["feat_read"], 1)
                transpose_split(NH, 12, lambda k: fp("ret_g")[:, k:k + 1])

            def gmlp():
                def read(i, pair, w):
                    dst, f = ((V(2048), ACT.Gelu), (V(1024), ACT.Gelu), (V(3072), ACT.Silu))[i]
                    return read_pair(tiles(dst), pair, f)
                gemm(D, (512,) * 3, ("evac_act",) * 3, read)
                transpose_split(NH, 16)

            def merge_out():
                used_gates = []
                for n in range(3):
                    def read(i, pair, w):
                        g = V(2048 + 2048 * (n % 2), 2048).rearrange("p (m d) -> p m d", m=M)
                        if n == 2 and i == 0:
                            act.wait_ge(sem["evac_dve"], used_gates[0])
                        return read_pair(g[:, :, 512 * i:512 * i + 512], pair, ACT.Sigmoid)
                    gemm(D, (512,) * 2, ("evac_act",) * 2, read)
                    gemm(BW, (512,) * 2, ("evac_dve",) * 2)
                    used_gates.append(st.evacs["evac_dve"])
                transpose_split(KD, 0)
                gemm(D, (512,) * 2, ("evac_dve",) * 2)

            def product_squares(i, pair):
                act.wait_ge(sem["unit_used"], st.used)
                for m in range(M):
                    last = act.activation(V(0, 512), pg[:, pair + m, :], ACT.Square,
                                          accum_out=SS4[:, 2 * i + m:2 * i + m + 1])
                    c.sig(last, "product_sq")

            def gemm_out(rows_, between=None):
                for i in range(2):
                    for n in range(len(units_of(rows_, 512))):
                        st.used += 1
                        if between and i == 0 and n == 1:
                            pump(st.used + 2)
                            between()
                    pump(st.used + 2)
                    product_squares(i, 2 * (st.block % 2))
                    st.evacs["evac_dve"] += 1
                    st.block += 1
                pump(st.used + 3)

            def ffn(name):
                features_of_x(lambda k: name[:, k:k + 1], X_AT)
                hid = V(0, 2 * FF).rearrange("p (m f) -> p m f", m=M)
                at_ = 0
                for j, w in enumerate(FF_WIDTHS):
                    gemm(D, (w, w), ("evac_act", "evac_dve"),
                         lambda i, pair, w: read_pair(hid[:, :, at_:at_ + w], pair, ACT.Silu, w))
                    at_ += w
                    if j:
                        split_groups([g for g in EARLY if g // 2 == j - 1], 0)
                gemm_out(FF, lambda: split_groups(LATE, 0))

            def hybrid():
                features_of_x(lambda k: spar("g2")[:, k:k + 1])
                z = V(10240, 2048).rearrange("p (m f) -> p m f", m=M)
                raw3 = V(0, 3072).rearrange("p (m f) -> p m f", m=M)

                def read(i, pair, w):
                    if i < 2:
                        dst, f = z[:, :, 512 * i:512 * i + 512], ACT.Silu
                    else:
                        dst, f = raw3[:, :, 512 * (i - 2):512 * (i - 2) + 512], ACT.Copy
                    return read_pair(dst, pair, f)
                gemm(D, (512,) * 5, ("evac_act",) * 5, read)
                c.wait("gate_abs")
                c.step(act.activation(SEXP, SEXP, ACT.Exp, scale=-1.0))
                c.step(act.activation(SNEGA[:, 0:16], spar("a_log"), ACT.Exp))
                act.activation(SEXP, SEXP, ACT.Ln, bias=1.0).then_inc(sem["gate_exp"], 1)
                c.wait("conv_read", 6)
                act.activation(V(3072, 3072), V(3072, 3072), ACT.Silu).then_inc(sem["conv_act"], 1)
                c.wait("back_tr")
                xs = V(8192, 2048)
                for b in range(4):
                    last = act.activation(xs[:, 512 * b:512 * b + 512], ps[:, b, :], ACT.Copy)
                    if b < 3:
                        c.step(last)
                last.then_inc(sem["back_read"], 1)
                c.wait("cb_ready")
                for h in range(16):
                    c.wait("row_done")
                    if h >= 2:
                        c.wait("ssd_done")
                    E = V(6144 + 512 * (h % 2), 384)
                    act.activation(E[:, 0:S], ps[:, h % 2, 0:S], ACT.Relu, scale=-1.0, bias=SCUM[:, h:h + 1])
                    c.step(act.activation(E[:, S:S + P], ps[:, h % 2, P:S], ACT.Relu, scale=-1.0,
                                          bias=SCUM[:, 24 + h:25 + h]))
                    act.activation(E, E, ACT.Exp, scale=-1.0).then_inc(sem["ssd_decay"], 1)
                c.wait("ssd_done", 2)
                c.wait("o_sq")
                for m in range(M):
                    for g in range(2):
                        last = act.activation(xn[:, 512 * (2 * m + g):512 * (2 * m + g) + 512],
                                              xs[:, 512 * (2 * m + g):512 * (2 * m + g) + 512], ACT.Square,
                                              accum_out=SS4[:, 2 * m + g:2 * m + g + 1])
                        if (m, g) != (1, 1):
                            c.step(last)
                last.then_inc(sem["sq_done"], 1)
                transpose_split(KD, 8, lambda k: spar("norm_g")[:, k:k + 1])

                def read_qkv(i, pair, w):
                    dst = V(2048 * (i // 2), 2048).rearrange("p (m f) -> p m f", m=M)
                    o = 512 * (i % 2)
                    return read_pair(dst[:, :, o:o + 512], pair, ACT.Copy)
                gemm(D, (512,) * 6, ("evac_act",) * 6, read_qkv)
                for t, o in enumerate((6144, 8192)):
                    for g in range(4):
                        c.wait("feat_tr")
                        act.activation(V(o + 512 * g, 512), ps[:, g, :], ACT.Copy,
                                       scale=HD ** -0.5 if t == 0 else 1.0).then_inc(sem["feat_read"], 1)
                for h in range(8):
                    c.wait("logits_ready")
                    pr = V(12288 + 512 * (h % 2), 384)
                    c.step(act.activation(pr[:, 0:P], pr[:, 0:P], ACT.Exp, bias=NMAX[:, 2 * h:2 * h + 1],
                                          accum_out=RSUM[:, 2 * h:2 * h + 1]))
                    act.activation(pr[:, P:3 * P], pr[:, P:3 * P], ACT.Exp, bias=NMAX[:, 2 * h + 1:2 * h + 2],
                                   accum_out=RSUM[:, 2 * h + 1:2 * h + 2]).then_inc(sem["probs_ready"], 1)
                    c.wait("probs_t")
                    if h >= 1:
                        c.wait("fox_done")
                    act.activation(V(13312, 384), ps[:, 2, 0:3 * P], ACT.Copy).then_inc(sem["probs_t_read"], 1)
                c.wait("fox_done")
                transpose_split(KD, 0)
                gemm_out(2 * D)

            def recurrent():
                features_of_x(lambda k: rp("g2")[:, k:k + 1])

                def read(i, pair, w):
                    dst = V(2048 if i < 2 else 0, 2048).rearrange("p (m f) -> p m f", m=M)
                    f = ACT.Gelu_apprx_tanh if i < 2 else ACT.Copy
                    o = 512 * (i % 2)
                    return read_pair(dst[:, :, o:o + 512], pair, f)
                gemm(D, (512,) * 4, ("evac_act",) * 4, read)
                c.step(act.activation(E8, rp("lam"), ACT.Abs))
                c.step(act.activation(E8, E8, ACT.Exp, scale=-1.0))
                act.activation(LAM, E8, ACT.Ln, bias=1.0).then_inc(sem["lam_ready"], 1)
                for t in range(2):
                    c.wait("lin_done")
                    dst = V(6144 + 2048 * t, 2048).rearrange("p (n s) -> p n s", n=8)
                    for n in range(8):
                        last = act.activation(dst[:, n, :], ps[:, n // 2, (n % 2) * S:(n % 2 + 1) * S], ACT.Sigmoid,
                                              bias=rp("b_a" if t == 0 else "b_x")[:, n:n + 1])
                    last.then_inc(sem["r_ready"], 1)
                c.wait("a_ready")
                la, a2 = V(6144, 2048), V(10240, 2048)
                c.step(act.activation(a2, la, ACT.Tanh))
                act.activation(la, la, ACT.Exp).then_inc(sem["u_ready"], 1)
                c.wait("u_sqrt")
                act.activation(a2, a2, ACT.Sqrt, scale=-1.0).then_inc(sem["h_ready"], 1)
                c.wait("rec_out")
                act.activation(hTh[:, 0:8, :], V(8192, 2048).rearrange("p (n s) -> p n s", n=8), ACT.Copy)\
                   .then_inc(sem["tr_high"], 1)
                made[0] += 1
                gemm_out(D)

            act.wait_ge(sem["const_landed"], 16)
            for l in range(DEPTH):
                act.wait_ge(sem["params_landed"], 16 * (l + 1))
                small_w(16, fp("small_w"))
                pump(st.used + 3)
                features_of_x(lambda k: fp("norm_g")[:, k:k + 1])
                gdn()
                retention()
                gmlp()
                merge_out()
            act.wait_ge(sem["params_landed"], 16 * 3)
            small_w(24, spar("small_w"))
            ffn(spar("g0"))
            hybrid()
            ffn(spar("g4"))
            act.wait_ge(sem["params_landed"], 16 * 4)
            ffn(rp("g0"))
            recurrent()
            ffn(rp("g4"))

        @block.vector
        def _(dve):
            c = Counter(dve, sem, "dve_step")
            st = Stream()
            tt, ts, stt = dve.tensor_tensor, dve.tensor_scalar, dve.scalar_tensor_tensor

            def pump(to):
                while st.split < min(to, NU):
                    u = st.split
                    slot = u % SPLIT_SLOTS
                    dve.wait_ge(sem["split_high"], u + 1)
                    tt(wl[:, slot, :], raw[:, u % RAW_SLOTS, :], wh[:, slot, :], ALU.subtract)\
                        .then_inc(sem["split_low"], 1)
                    st.split += 1

            def gemm(rows_, widths, evacs, read=None):
                for i, (w, by) in enumerate(zip(widths, evacs)):
                    st.used += len(units_of(rows_, w))
                    pump(st.used + 2)
                    if by == "evac_dve":
                        if read is not None:
                            dve.wait_ge(sem["unit_used"], st.used)
                            c.sig(read(i, 2 * (st.block % 2), w), "evac_dve")
                    st.evacs[by] += 1
                    st.block += 1
                pump(st.used + 3)

            made = [0]

            def split_groups(gs, dst, gain=None):
                for g in gs:
                    bank = made[0] % 4
                    made[0] += 1
                    c.wait("tr_high")
                    if gain is None:
                        h = slice(dst + 2 * g, dst + 2 * g + 2)
                        last = tt(hTl[:, h, :], ps[:, bank, :].rearrange("p (k s) -> p k s", k=2), hTh[:, h, :],
                                  ALU.subtract)
                    else:
                        for j in range(2):
                            k = 2 * g + j
                            last = stt(hTl[:, dst + k, :], ps[:, bank, j * S:(j + 1) * S], gain(k), hTh[:, dst + k, :],
                                       ALU.mult, ALU.subtract)
                    last.then_inc(sem["tr_low"], 1)

            def transpose_split(chunks, dst, gain=None):
                split_groups(range(chunks // 2), dst, gain)

            def features_of_x(gain, dst=0):
                split_groups(range(KD // 2), dst, gain)
                c.wait("x_squares")
                c.step(tt(RS, SX4[:, 0:2], SX4[:, 2:4], ALU.add))
                rstd_of(RS, D, "rs_ready")

            def small_w(n, name):
                c.wait("small_w_high")
                tt(swl[:, 0:KD * n], name[:, 0:KD * n], swh[:, 0:KD * n], ALU.subtract).then_inc(sem["small_w_low"], 1)

            def rstd_of(ss, n, done="dve_step"):
                w = ss.shape[1]
                y, t, h = NEWTON[:, 0:w], NEWTON[:, 16:16 + w], NEWTON[:, 32:32 + w]
                c.step(ts(ss, ss, 1.0 / n, EPS, ALU.mult, ALU.add))
                ts(h, ss, -0.5, None, ALU.mult)
                c.step(ts(y.bitcast(I32), ss.bitcast(I32), 1, None, ALU.logical_shift_right))
                c.step(ts(y.bitcast(I32), y.bitcast(I32), -1.0, float(0x5F3759DF), ALU.mult, ALU.add))
                for i in range(3):
                    c.step(tt(t, y, y, ALU.mult))
                    c.step(tt(t, t, h, ALU.mult))
                    c.sig(stt(ss if i == 2 else y, t, 1.5, y, ALU.add, ALU.mult), done if i == 2 else "dve_step")

            def normalise(dst):
                for m in range(M):
                    last = dve.tensor_tensor_reduce(dst[:, m, :], x[:, m, :], x[:, m, :], 1.0, 0.0, ALU.mult, ALU.add,
                                                    SS[:, m:m + 1])
                c.step(last)
                rstd_of(SS, D)
                for m in range(M):
                    last = ts(dst[:, m, :], x[:, m, :], SS[:, m:m + 1], None, ALU.mult)
                return last

            XN = xn[:, :].rearrange("p (m d) -> p m d", m=M)

            def head_rstd(src, n, dst):
                c.step(dve.tensor_reduce(dst, src.rearrange("p (k e) -> p k e", e=HD), AX.X, ALU.add))
                rstd_of(dst, n)

            def gdn():
                gemm(D, (512,) * 3, ("evac_act",) * 3)
                c.wait("small_done")
                for m in range(M):
                    src = ps[:, m, 0:16].rearrange("p (d t h) -> p d t h", d=2, t=2)
                    ts(QS[:, 8 * m:8 * m + 8].rearrange("p (d h) -> p d h", d=2), src[:, :, 1, :], RS[:, m:m + 1], None,
                       ALU.mult)
                    last = stt(TOT[:, 8 * m:8 * m + 8].rearrange("p (d h) -> p d h", d=2), src[:, :, 0, :],
                               RS[:, m:m + 1], fp("dtb").rearrange("p (d h) -> p d h", d=2), ALU.mult, ALU.add)
                c.sig(last, "small_read")
                stt(ABS, TOT, -1.0, TOT, ALU.mult, ALU.max).then_inc(sem["gate_abs"], 1)
                w = fp("conv")
                for t in range(3):
                    c.wait("conv_tr")
                    acc = cvp[t].rearrange("p (h s) -> p h s", h=NH)
                    src = [ps[:, 2 * (t % 2) + h // 2, (h % 2) * S:(h % 2 + 1) * S] for h in range(NH)]
                    k = 4 * t
                    for h in range(NH):
                        last = ts(acc[:, h, :], src[h], w[:, 12 + k + h:13 + k + h], None, ALU.mult)
                    c.step(last)
                    for h in range(NH):
                        last = stt(acc[:, h, 1:S], src[h][:, 0:S - 1], w[:, k + h:k + h + 1], acc[:, h, 1:S],
                                   ALU.mult, ALU.add)
                    c.step(last)
                    for h in range(NH):
                        last = stt(acc[:, h, 0:S - 1], src[h][:, 1:S], w[:, 24 + k + h:25 + k + h], acc[:, h, 0:S - 1],
                                   ALU.mult, ALU.add)
                    c.sig(last, "conv_read")
                c.wait("gate_exp")
                c.step(stt(SPL, TOT, 0.0, SPL, ALU.max, ALU.add))
                c.step(ts(SMR, SMR, 1.0, None, ALU.add))
                c.step(dve.reciprocal(BETA, SMR))
                c.sig(stt(GLOG.rearrange("p (m k) -> p m k", m=M), SPL.rearrange("p (m k) -> p m k", m=M), -1.0,
                          times(NEGA, M), ALU.mult, ALU.mult), "gate_g")
                for t, dst in enumerate((qn, kn)):
                    c.wait("sq_ready")
                    c.sig(dve.tensor_reduce(STATS, sq.rearrange("p (k e) -> p k e", e=HD), AX.X, ALU.add), "sq_free")
                    rstd_of(STATS, 1.0)
                    if t == 0:
                        c.step(ts(STATS, STATS, HD ** -0.5, None, ALU.mult))
                    src = ps[:, 2 * t:2 * t + 2, :].rearrange("p m (h e) -> p (m h) e", h=NH)
                    c.sig(tt(heads(dst, 8), src, over(STATS, HD), ALU.mult), "qk_ready")
                c.wait("cum_done")
                c.step(dve.tensor_copy(GC, ps[:, 0, 0:16]))
                ts(NGC, ps[:, 0, 0:16], -1.0, None, ALU.mult)
                tt(EKD, ps[:, 0, 16:32], GC, ALU.subtract)
                c.sig(dve.tensor_copy(GL, ps[:, 0, 32:64]), "cum_read")
                c.wait("cum_t")
                c.sig(dve.tensor_copy(GCT, ps[0:8, 1, 0:S]), "cum_t_read")
                c.wait("cum_exp")
                c.step(tt(BEG, BETA, EGC, ALU.mult))
                SC4 = SCT.rearrange("p (m j s) -> p m j s", m=M, j=8)
                L3, LT3, X3, XT3, T3 = (heads(v, 8) for v in (Lm, LT, X_, XT_, TM_))
                U4 = U_.rearrange("p (m j e) -> p m j e", m=M, j=8)
                for m in range(M):
                    c.wait("decay_ready")
                    c.wait("gram_done")
                    kk, qk = heads(ps[:, 0, :]), heads(ps[:, 1, :])
                    for d in range(2):
                        js = slice(4 * d, 4 * d + 4)
                        tt(L3[:, js, :], X3[:, js, :], kk, ALU.mult)
                        last = tt(SC4[:, m, js, :], XT3[:, js, :], qk, ALU.mult)
                    c.step(last)
                    for d in range(2):
                        js = slice(4 * d, 4 * d + 4)
                        tt(L3[:, js, :], L3[:, js, :], times(C["los64" if d == 0 else "ups64"], NH), ALU.mult)
                        last = tt(SC4[:, m, js, :], SC4[:, m, js, :], times(C["up64" if d == 0 else "lo64"], NH), ALU.mult)
                    c.step(last)
                    c.sig(tt(L3, L3, over(BETA[:, 8 * m:8 * m + 8], P), ALU.mult), "low_ready")
                    c.wait("low_t_read")
                    for d in range(2):
                        js = slice(4 * d, 4 * d + 4)
                        A, AT = (L3, LT3) if d == 0 else (LT3, L3)
                        tt(X3[:, js, :], A[:, js, :], times(C["nlo1"], NH), ALU.mult)
                        c.step(tt(XT3[:, js, :], AT[:, js, :], times(C["nup1"], NH), ALU.mult))
                        tt(X3[:, js, :], X3[:, js, :], times(ident, NH), ALU.add)
                        c.sig(tt(XT3[:, js, :], XT3[:, js, :], times(ident, NH), ALU.add), "inv_x")
                    for s in (2, 4, 8, 16, 32):
                        for d in range(2):
                            js = slice(4 * d, 4 * d + 4)
                            c.wait("inv_t")
                            c.sig(tt(T3[:, js, :], heads(ps[:, d, :]), times(C[f"nlo{s}"], NH), ALU.mult), "inv_tm")
                        for d in range(2):
                            js = slice(4 * d, 4 * d + 4)
                            if s < 32 or d == 1:
                                c.wait("inv_y")
                                last = tt(X3[:, js, :], X3[:, js, :], heads(ps[:, 2 + d, :]), ALU.add)
                            if s < 32 or d == 0:
                                c.wait("inv_yt")
                                last = tt(XT3[:, js, :], XT3[:, js, :], heads(ps[:, d, :]), ALU.add)
                            c.sig(last, "inv_x")
                    for d in range(2):
                        js = slice(4 * d, 4 * d + 4)
                        o = 8 * m + 4 * d
                        tt(L3[:, js, :], heads(vt[:, 512 * m:512 * m + 512]), over(BETA[:, o:o + 4], P), ALU.mult)
                        last = tt(LT3[:, js, :], heads(kn[:, 512 * m:512 * m + 512]), over(BEG[:, o:o + 4], P), ALU.mult)
                    c.sig(last, "rhs_ready")
                c.wait("uw_read", 2)
                dve.memset(o_acc, 0.0)
                c.sig(dve.memset(X_, 0.0), "state_zero")
                O4 = o_acc.rearrange("p (m h e) -> p m h e", m=M, h=NH)
                for t in range(4):
                    where = []
                    for d in range(2):
                        ck = t if d == 0 else 3 - t
                        m, r = ck // 2, 64 * (ck % 2)
                        where.append((ck, m, slice(r, r + 64), slice(4 * d, 4 * d + 4), 8 * m + 4 * d))
                    for d, (ck, m, rs, js, o) in enumerate(where):
                        c.wait("ws_done")
                        c.step(tt(L3[rs, js, :], U4[rs, m, js, :], heads(ps[rs, 2 * d, :]), ALU.subtract))
                        c.sig(tt(LT3[rs, js, :], L3[rs, js, :], over(EKD[rs, o:o + 4], P), ALU.mult), "vn_ready")
                    for d, (ck, m, rs, js, o) in enumerate(where):
                        c.wait("kv_done")
                        e = 8 * ck + 4 * d
                        c.step(tt(X3[:, js, :], X3[:, js, :], over(EGL[:, e:e + 4], P), ALU.mult))
                        c.sig(tt(X3[:, js, :], X3[:, js, :], heads(ps[:, 2 * d + 1, :]), ALU.add), "state_ready")
                        c.sig(tt(T3[rs, js, :], heads(ps[rs, 2 * d, :]), over(EGC[rs, o:o + 4], P), ALU.mult), "sv_read")
                        c.step(tt(O4[rs, m, :, :], O4[rs, m, :, :], T3[rs, js, :], ALU.add))
                    for d, (ck, m, rs, js, o) in enumerate(where):
                        c.wait("sv_done")
                        c.sig(tt(O4[rs, m, :, :], O4[rs, m, :, :], heads(ps[rs, 2 * d, :]), ALU.add), "o_ready")
                gemm(D, (512,), ("evac_act",))
                c.wait("sq_done")
                head_rstd(Lm, HD, STATS)
                c.step(tt(heads(o_acc, 8), heads(o_acc, 8), over(STATS, HD), ALU.mult))
                dve.wait_ge(sem["evac_act"], st.evacs["evac_act"])
                tt(o_acc, o_acc, V(0), ALU.mult).then_inc(sem["y_ready"], 1)
                transpose_split(NH, 8, lambda k: fp("gdn_g"))

            def log_sigmoid(v):
                c.wait("lam_ready")
                c.step(ts(TMP8, E8, 1.0, None, ALU.add))
                c.step(ts(TMP8, TMP8, -1.0, 1e-30, ALU.add, ALU.max))
                c.step(dve.reciprocal(TMP8, TMP8))
                c.step(tt(TMP8, TMP8, E8, ALU.mult))
                c.step(tt(LAM, LAM, TMP8, ALU.mult))
                c.step(stt(LAM, v, 0.0, LAM, ALU.min, ALU.subtract))

            def retention(l):
                log_sigmoid(fp("decay"))
                dve.wait_ge(sem["dist_landed"], 16 * (l + 1))
                RD = V(10240).rearrange("p (s n) -> p s n", s=2)
                for h in range(NH):
                    mk = V(8192 + 512 * h, 512)
                    c.step(ts(mk, RD[:, 0, :], LAM[:, h:h + 1], None, ALU.mult))
                    last = stt(mk, RD[:, 1, :], LAM[:, 4 + h:5 + h], mk, ALU.mult, ALU.add)
                last.then_inc(sem["mask_arg"], 1)

                def read(i, pair, w):
                    dst = V(1024 * i).rearrange("p (m h e) -> p m h e", m=M, h=NH)
                    tmp = V(11264).rearrange("p (m h e) -> p m h e", m=M, h=NH)
                    for m in range(M):
                        src = heads(pg[:, pair + m, :])
                        x1, x2 = src[:, :, 0:64], src[:, :, 64:P]
                        co, si = times(COS[:, m, :], NH), times(SIN[:, m, :], NH)
                        r = RS[:, m:m + 1]
                        stt(dst[:, m, :, 0:64], x1, r, co, ALU.mult, ALU.mult)
                        stt(dst[:, m, :, 64:P], x2, r, co, ALU.mult, ALU.mult)
                        stt(tmp[:, m, :, 0:64], x2, r, si, ALU.mult, ALU.mult)
                        last = stt(tmp[:, m, :, 64:P], x1, r, si, ALU.mult, ALU.mult)
                    return last

                def read_and_add(i, pair, w):
                    last = read(i, pair, w)
                    c.step(last)
                    dst = V(1024 * i).rearrange("p (k e) -> p k e", k=8)
                    tmp = V(11264).rearrange("p (k e) -> p k e", k=8)
                    tt(dst[:, :, 0:64], dst[:, :, 0:64], tmp[:, :, 0:64], ALU.subtract)
                    return tt(dst[:, :, 64:P], dst[:, :, 64:P], tmp[:, :, 64:P], ALU.add)

                gemm(D, (512,) * 4, ("evac_dve", "evac_dve", "evac_act", "evac_act"), read_and_add)
                c.wait("mask_ready")
                for h in range(NH):
                    c.wait("qk_done")
                    if h >= 2:
                        c.wait("ov_done")
                    c.sig(tt(V(5120 + 512 * (h % 2), 512), ps[:, h % 2, :], V(8192 + 512 * h, 512), ALU.mult), "sc_ready")
                c.wait("ov_done", 2)
                for m in range(M):
                    for h in range(NH):
                        k = 4 * m + h
                        last = dve.bn_stats(BN[:, 6 * k:6 * k + 6], ps[:, 2 + m, h * P:(h + 1) * P])
                c.step(last)
                for k in range(8):
                    last = dve.bn_aggr(MV[:, 2 * k:2 * k + 2], BN[:, 6 * k:6 * k + 6])
                c.step(last)
                mv = MV.rearrange("p (k t) -> p k t", t=2)
                c.step(dve.tensor_copy(STATS, mv[:, :, 1]))
                rstd_of(STATS, 1.0)
                for m in range(M):
                    for h in range(NH):
                        k = 4 * m + h
                        last = ts(V(0)[:, k * P:(k + 1) * P], ps[:, 2 + m, h * P:(h + 1) * P], MV[:, 2 * k:2 * k + 1],
                                  STATS[:, k:k + 1], ALU.subtract, ALU.mult)
                c.step(last)
                dve.wait_ge(sem["evac_act"], st.evacs["evac_act"])
                tt(V(0), V(0), V(7168), ALU.mult).then_inc(sem["y_ready"], 1)
                transpose_split(NH, 12, lambda k: fp("ret_g")[:, k:k + 1])

            def gmlp(l):
                gemm(D, (512,) * 3, ("evac_act",) * 3)
                dve.wait_ge(sem["evac_act"], st.evacs["evac_act"])
                dve.wait_ge(sem["wide_landed"], 16 * (l + 1))
                v = V(1024)
                for m in range(M):
                    last = dve.bn_stats(BN[:, 6 * m:6 * m + 6], v[:, 512 * m:512 * m + 512])
                c.step(last)
                for m in range(M):
                    last = dve.bn_aggr(MV[:, 2 * m:2 * m + 2], BN[:, 6 * m:6 * m + 6])
                c.step(last)
                c.step(dve.tensor_copy(STATS[:, 0:2], MV.rearrange("p (k t) -> p k t", t=2)[:, 0:2, 1]))
                rstd_of(STATS[:, 0:2], 1.0)
                for m in range(M):
                    last = ts(v[:, 512 * m:512 * m + 512], v[:, 512 * m:512 * m + 512], MV[:, 2 * m:2 * m + 1],
                              STATS[:, m:m + 1], ALU.subtract, ALU.mult)
                c.step(last)
                v2 = v.rearrange("p (m e) -> p m e", m=M)
                c.step(tt(v2, v2, times(V(12288, 512), M), ALU.mult))
                c.sig(tt(v2, v2, times(V(12800, 512), M), ALU.add), "v_ready")
                c.step(tt(V(2048), V(2048), V(3072), ALU.mult))
                c.wait("mix_done")
                for m in range(M):
                    for g in range(NH):
                        o = 512 * m + g * P
                        last = stt(V(0)[:, o:o + P], ps[:, m, g * P:(g + 1) * P], fp("b_s")[:, g:g + 1],
                                   V(2048)[:, o:o + P], ALU.add, ALU.mult)
                last.then_inc(sem["y_ready"], 1)
                transpose_split(NH, 16)

            def merge_out(last_layer):
                for n in range(3):
                    def read(i, pair, w):
                        if i == 0:
                            dve.wait_ge(sem["evac_act"], st.evacs["evac_act"])
                        g = V(2048 + 2048 * (n % 2), 2048).rearrange("p (m d) -> p m d", m=M)
                        o = slice(512 * i, 512 * i + 512)
                        dst = V(0 if n == 0 else 6144, 2048).rearrange("p (m d) -> p m d", m=M)
                        return tt(dst[:, :, o], g[:, :, o], pg[:, pair:pair + 2, :], ALU.mult)
                    gemm(D, (512,) * 2, ("evac_act",) * 2)
                    gemm(BW, (512,) * 2, ("evac_dve",) * 2, read)
                    if n == 1:
                        c.step(tt(V(0, 2048), V(0, 2048), V(6144, 2048), ALU.add))
                tt(V(0, 2048), V(0, 2048), V(6144, 2048), ALU.add).then_inc(sem["y_ready"], 1)
                transpose_split(KD, 0)

                def add(i, pair, w):
                    o = slice(512 * i, 512 * i + 512)
                    last = tt(x[:, :, o], x[:, :, o], pg[:, pair:pair + 2, :], ALU.add)
                    if last_layer:
                        return last
                    c.sig(last, "x_ready")
                    return dve.engine_nop()
                gemm(D, (512,) * 2, ("evac_dve",) * 2, add)

            posts = [0]
            G = V(13824)

            def gemm_out(rows_, half, between=None):
                for i in range(2):
                    for n in range(len(units_of(rows_, 512))):
                        st.used += 1
                        if between and i == 0 and n == 1:
                            pump(st.used + 2)
                            between()
                    pump(st.used + 2)
                    if i == 0:
                        dve.wait_ge(sem["wide_landed"], 16 * (DEPTH + 1 + posts[0]))
                        posts[0] += 1
                    pair = 2 * (st.block % 2)
                    dve.wait_ge(sem["unit_used"], st.used)
                    o = slice(512 * i, 512 * i + 512)
                    for m in range(M):
                        c.wait("product_sq")
                        last = tt(XN[:, m, o], pg[:, pair + m, :], G[:, o], ALU.mult)
                    c.sig(last, "evac_dve")
                    st.evacs["evac_dve"] += 1
                    st.block += 1
                c.step(tt(SS, SS4[:, 0:2], SS4[:, 2:4], ALU.add))
                rstd_of(SS, D)
                if half != 1.0:
                    c.step(ts(SS, SS, half, None, ALU.mult))
                for b in range(2):
                    o = slice(512 * b, 512 * b + 512)
                    for m in range(M):
                        last = stt(x[:, m, o], XN[:, m, o], SS[:, m:m + 1], x[:, m, o], ALU.mult, ALU.add)
                    c.sig(last, "x_ready")
                pump(st.used + 3)

            def ffn():
                features_of_x(gains[0], X_AT)
                hid = V(0, 2 * FF).rearrange("p (m f) -> p m f", m=M)
                at_ = 0

                def read(i, pair, w):
                    dve.wait_ge(sem["evac_act"], st.evacs["evac_act"])
                    for m in range(M):
                        last = stt(hid[:, m, at_:at_ + w], pg[:, pair + m, 0:w], RS[:, m:m + 1], hid[:, m, at_:at_ + w],
                                   ALU.mult, ALU.mult)
                    return last
                for j, w in enumerate(FF_WIDTHS):
                    gemm(D, (w, w), ("evac_act", "evac_dve"), read)
                    at_ += w
                    if j:
                        split_groups([g for g in EARLY if g // 2 == j - 1], 0)
                gemm_out(FF, 0.5, lambda: split_groups(LATE, 0))

            gains = [None]

            def hybrid():
                features_of_x(lambda k: spar("g2")[:, k:k + 1])
                gemm(D, (512,) * 5, ("evac_act",) * 5)
                c.wait("small_done")
                for m in range(M):
                    o = 24 * m
                    stt(SAB[:, o:o + 16], ps[:, m, 0:16], RS[:, m:m + 1], spar("dtb"), ALU.mult, ALU.add)
                    last = stt(SAB[:, o + 16:o + 24], ps[:, m, 16:24], RS[:, m:m + 1], spar("fox_b"), ALU.mult, ALU.add)
                c.sig(last, "small_read")
                for m in range(M):
                    o = 24 * m
                    last = ts(SAB[:, o + 16:o + 24], SAB[:, o + 16:o + 24], -1.0, None, ALU.mult)
                c.step(last)
                dve.memset(SNEGA[:, 16:24], 1.0)
                stt(SEXP, SAB, -1.0, SAB, ALU.mult, ALU.max).then_inc(sem["gate_abs"], 1)
                w, b = spar("conv"), spar("conv_b")
                cv = V(3072, 3072).rearrange("p (k s) -> p k s", k=12)
                for g in range(6):
                    c.wait("conv_tr")
                    ks = (2 * g, 2 * g + 1)
                    src = {k: ps[:, g % 4, (k % 2) * S:(k % 2 + 1) * S] for k in ks}
                    for k in ks:
                        last = ts(cv[:, k, :], src[k], w[:, 36 + k:37 + k], b[:, k:k + 1], ALU.mult, ALU.add)
                    c.step(last)
                    for tap in (2, 1, 0):
                        sh = 3 - tap
                        for k in ks:
                            last = stt(cv[:, k, sh:S], src[k][:, 0:S - sh], w[:, 12 * tap + k:12 * tap + k + 1],
                                       cv[:, k, sh:S], ALU.mult, ALU.add)
                        if tap:
                            c.step(last)
                    c.sig(last, "conv_read")
                c.wait("gate_exp")
                c.step(stt(SEXP, SAB, 0.0, SEXP, ALU.max, ALU.add))
                dve.tensor_copy(DT.rearrange("p (m k) -> p m k", m=M), SEXP.rearrange("p (m k) -> p m k", m=M)[:, :, 0:16])
                c.sig(stt(SG.rearrange("p (m k) -> p m k", m=M), SEXP.rearrange("p (m k) -> p m k", m=M), -1.0,
                          times(SNEGA, M), ALU.mult, ALU.mult), "gate_g")
                c.wait("cum_done")
                c.sig(dve.tensor_copy(SCUM, ps[:, 0, 0:48]), "cum_read")
                c.wait("cum_t")
                c.step(dve.tensor_copy(SCUMT, ps[0:24, 1, 0:S]))
                c.sig(ts(SCUMTN, ps[0:24, 1, 0:S], -1.0, None, ALU.mult), "cum_t_read")
                dve.wait_ge(sem["back_read"], DEPTH + 1)
                xs = V(8192, 2048)
                tt(V(0, 2048).rearrange("p (m h e) -> p (m h) e", m=M, h=16), xs.rearrange("p (m h e) -> p (m h) e", m=M, h=16),
                   over(DT, 64), ALU.mult)
                c.wait("gram_done")
                CB = V(2048, 768).rearrange("p (g s) -> p g s", g=2)
                tt(CB[:, :, 0:P], ps[:, 2:4, 0:P], times(C["up128"], 2), ALU.mult)
                dve.tensor_copy(CB[:, :, P:2 * P], ps[:, 2:4, P:2 * P])
                c.sig(tt(CB[:, :, 2 * P:3 * P], ps[:, 2:4, 2 * P:3 * P], times(C["up128"], 2), ALU.mult), "cb_ready")
                c.step(tt(xs.rearrange("p (m h e) -> p m h e", m=M, h=16)[:, 0], xs.rearrange("p (m h e) -> p m h e", m=M, h=16)[:, 0],
                          over(spar("d"), 64), ALU.mult))
                c.step(tt(xs.rearrange("p (m h e) -> p m h e", m=M, h=16)[:, 1], xs.rearrange("p (m h e) -> p m h e", m=M, h=16)[:, 1],
                          over(spar("d"), 64), ALU.mult))
                xs3 = xs.rearrange("p (m f) -> p m f", m=M)
                for h in range(16):
                    c.wait("ssd_decay")
                    E = V(6144 + 512 * (h % 2), 384)
                    c.sig(tt(E, E, CB[:, h // 8, :], ALU.mult), "ssd_mask")
                    if h % 8 == 7:
                        c.wait("ssd_done", 8)
                        o = slice(512 * (h // 8), 512 * (h // 8) + 512)
                        c.sig(tt(xs3[:, :, o], xs3[:, :, o], ps[:, 2:4, :], ALU.add), "out_read")
                c.sig(tt(xs, xs, V(10240, 2048), ALU.mult), "o_sq")
                c.wait("sq_done")
                rstd_of(SS4, 512)
                for m in range(M):
                    for g in range(2):
                        o = 1024 * m + 512 * g
                        last = ts(xs[:, o:o + 512], xs[:, o:o + 512], SS4[:, 2 * m + g:2 * m + g + 1], None, ALU.mult)
                last.then_inc(sem["y_ready"], 1)
                transpose_split(KD, 8, lambda k: spar("norm_g")[:, k:k + 1])
                gemm(D, (512,) * 6, ("evac_act",) * 6)
                for h in range(8):
                    c.wait("qk_done")
                    if h >= 2:
                        c.wait("probs_t")
                    pr = V(12288 + 512 * (h % 2), 384)
                    b = h % 2
                    tt(pr[:, 0:P], ps[:, b, 0:P], C["neg_causal"], ALU.add)
                    dve.tensor_copy(pr[:, P:2 * P], ps[:, b, S:S + P])
                    c.sig(tt(pr[:, 2 * P:3 * P], ps[:, b, S + P:2 * S], C["neg_causal"], ALU.add), "logits_read")
                    dve.tensor_reduce(NMAX[:, 2 * h:2 * h + 1], pr[:, 0:P], AX.X, ALU.max)
                    c.step(dve.tensor_reduce(NMAX[:, 2 * h + 1:2 * h + 2], pr[:, P:3 * P], AX.X, ALU.max))
                    c.sig(ts(NMAX[:, 2 * h:2 * h + 2], NMAX[:, 2 * h:2 * h + 2], -1.0, None, ALU.mult), "logits_ready")
                    if h:
                        fox_read(h - 1)
                c.wait("probs_t", 2)
                fox_read(7)
                transpose_split(KD, 0)
                gemm_out(2 * D, 1.0)

            def fox_read(h):
                c.wait("fox_done")
                dve.wait_ge(sem["probs_ready"], h + 1)
                c.step(dve.reciprocal(RSUM[:, 2 * h:2 * h + 2], RSUM[:, 2 * h:2 * h + 2]))
                o = V(10240, 2048).rearrange("p (m h e) -> p m h e", m=M, h=8)
                for m in range(M):
                    last = ts(o[:, m, h, :], ps[:, 3, m * P:(m + 1) * P], RSUM[:, 2 * h + m:2 * h + m + 1], None, ALU.mult)
                c.sig(last, "fox_read")

            def recurrent():
                features_of_x(lambda k: rp("g2")[:, k:k + 1])
                gemm(D, (512,) * 4, ("evac_act",) * 4)
                w, b = rp("conv"), rp("conv_b")
                xT = V(4096, 2048).rearrange("p (n s) -> p n s", n=8)
                for g in range(4):
                    c.wait("conv_tr")
                    ks = (2 * g, 2 * g + 1)
                    src = {k: ps[:, g, (k % 2) * S:(k % 2 + 1) * S] for k in ks}
                    for k in ks:
                        last = ts(xT[:, k, :], src[k], w[:, 24 + k:25 + k], b[:, k:k + 1], ALU.mult, ALU.add)
                    c.step(last)
                    for tap in (2, 1, 0):
                        sh = 3 - tap
                        for k in ks:
                            last = stt(xT[:, k, sh:S], src[k][:, 0:S - sh], w[:, 8 * tap + k:8 * tap + k + 1],
                                       xT[:, k, sh:S], ALU.mult, ALU.add)
                        if tap:
                            c.step(last)
                    c.sig(last, "conv_read")
                log_sigmoid(rp("lam"))
                c.step(ts(LAM, LAM, 8.0, None, ALU.mult))
                c.wait("r_ready")
                la = V(6144, 2048).rearrange("p (n s) -> p n s", n=8)
                c.sig(tt(la, la, over(LAM, S), ALU.mult), "a_ready")
                c.wait("r_ready")
                u = V(8192, 2048)
                c.step(tt(u, u, V(4096, 2048), ALU.mult))
                c.wait("u_ready")
                a, a2, th = V(6144, 2048), V(4096, 2048), V(10240, 2048)
                c.step(tt(a2, a, a, ALU.mult))
                c.sig(stt(th, a2, 1.0, th, ALU.add, ALU.mult), "u_sqrt")
                c.wait("h_ready")
                c.step(tt(u, u, th, ALU.mult))
                hs = a2.rearrange("p (n s) -> p n s", n=8)
                u3, a3 = u.rearrange("p (n s) -> p n s", n=8), a.rearrange("p (n s) -> p n s", n=8)
                for n in range(8):
                    last = dve.tensor_tensor_scan(hs[:, n, :], a3[:, n, :], u3[:, n, :], 0.0, ALU.mult, ALU.add)
                c.step(last)
                c.wait("gt_done")
                c.sig(tt(u3, hs, ps[:, :, :].rearrange("p b (k s) -> p (b k) s", k=2), ALU.mult), "rec_out")
                c.wait("tr_high")
                tt(hTl[:, 0:8, :], u3, hTh[:, 0:8, :], ALU.subtract).then_inc(sem["tr_low"], 1)
                made[0] += 1
                gemm_out(D, 1.0)

            dve.wait_ge(sem["const_landed"], 16)
            dve.wait_ge(sem["x_landed"], 16)
            for b in range(2):
                dve.engine_nop().then_inc(sem["x_ready"], 1)
                c.wait("x_ready")
            for l in range(DEPTH):
                dve.wait_ge(sem["params_landed"], 16 * (l + 1))
                small_w(16, fp("small_w"))
                pump(st.used + 3)
                features_of_x(lambda k: fp("norm_g")[:, k:k + 1])
                gdn()
                retention(l)
                gmlp(l)
                merge_out(l == DEPTH - 1)
                dve.engine_nop().then_inc(sem["layer_done"], 1)
            dve.wait_ge(sem["final_g_landed"], 16)
            c.step(normalise(XN))
            for b in range(2):
                o = slice(512 * b, 512 * b + 512)
                c.sig(tt(x[:, :, o], XN[:, :, o], times(G[:, o], M), ALU.mult), "x_ready")
            dve.wait_ge(sem["params_landed"], 16 * 3)
            small_w(24, spar("small_w"))
            gains[0] = lambda k: spar("g0")[:, k:k + 1]
            ffn()
            hybrid()
            gains[0] = lambda k: spar("g4")[:, k:k + 1]
            ffn()
            dve.wait_ge(sem["params_landed"], 16 * 4)
            gains[0] = lambda k: rp("g0")[:, k:k + 1]
            ffn()
            recurrent()
            gains[0] = lambda k: rp("g4")[:, k:k + 1]
            ffn()

        @block.sync
        def _(sp):
            sp.dma_start(cst[:, :], const).then_inc(sem["const_landed"], 16)
            for u in range(NU):
                if u >= RAW_SLOTS:
                    sp.wait_ge(sem["split_low"], u - RAW_SLOTS + 1)
                sp.dma_start(raw[:, u % RAW_SLOTS, :], weights[u]).then_inc(weight_landed[u % RAW_SLOTS], 16)

        @block.gpsimd
        def _(pool):
            c = Counter(pool, sem, None)
            pool.dma_start(x[:, :, :], x_in.rearrange("a (m p) d -> p (a m) d", p=P)).then_inc(sem["x_landed"], 16)
            pool.dma_start(par[:, :], params[0]).then_inc(sem["params_landed"], 16)
            for l in range(DEPTH):
                c.wait("o_ready", 8)
                pool.dma_start(V(10240), dist).then_inc(sem["dist_landed"], 16)
                pool.dma_start(V(12288), wide[7 + l]).then_inc(sem["wide_landed"], 16)
                pool.dma_start(V(13312, 512), token_mix[l]).then_inc(sem["mix_landed"], 16)
                if l == DEPTH - 1:
                    pool.dma_start(V(13824), wide[6]).then_inc(sem["final_g_landed"], 16)
                c.wait("layer_done")
                pool.dma_start(par[:, :], params[l + 1]).then_inc(sem["params_landed"], 16)
            c.wait("x_ready", 2 * DEPTH)
            for i in range(6):
                c.wait("x_ready", 2)
                pool.dma_start(V(13824), wide[i]).then_inc(sem["wide_landed"], 16)
                if i == 2:
                    pool.dma_start(V(11776, 2048).rearrange("p (t n) -> p t n", t=2),
                                   gate_mix.rearrange("t p n -> p t n")).then_inc(sem["mix_landed"], 16)
                if i == 3:
                    pool.dma_start(par[:, :], params[3]).then_inc(sem["params_landed"], 16)
            c.wait("x_ready", 2)
            pool.dma_start(out.rearrange("a (m p) d -> p (a m) d", p=P), x[:, :, :]).then_inc(sem["out_landed"], 16)
            pool.wait_ge(sem["out_landed"], 16)


def kernel(**inputs):
    import concourse.bacc as bacc
    from concourse.bass_utils import run_bass_kernel_spmd as run

    a = {k: np.asarray(v) for k, v in inputs.items()}
    const, dist = constants()
    mix, gate_mix = pack_token_mix(a)
    arrays = {"x_in": a["x"], "weights": pack_weights(a), "params": pack_params(a), "wide": pack_wide(a),
              "token_mix": mix, "gate_mix": gate_mix, "const_tables": const, "dist_tables": dist}
    nc = bacc.Bacc("TRN2", target_bir_lowering=False, num_devices=1)
    args = []
    for name, v in arrays.items():
        args.append(nc.dram_tensor(name, v.shape, mybir.dt.from_np(v.dtype), kind="ExternalInput").ap())
    args.append(nc.dram_tensor("y_out", (1, S, D), F32, kind="ExternalOutput").ap())
    program(nc, *args)
    return run(nc, [arrays], core_ids=[0]).results[0]["y_out"]
```

```python
from contextlib import ExitStack

import concourse.bass as bass
from concourse import mybir
import numpy as np

F32 = mybir.dt.float32
F32R = mybir.dt.float32r
I32 = mybir.dt.int32
ALU = mybir.AluOpType
ACT = mybir.ActivationFunctionType
AX = mybir.AxisListType

P = 128
S = 256
M = S // P
D = 1024
DEPTH = 2
BW = 512
NH = 4
HD = 128
FF = 2816
EPS = 1e-6
UNIT = 2048
RAW_SLOTS = 3
SPLIT_SLOTS = 3
KD = D // P
KF = FF // P

W_IN_STAGES = (("dq", 7), ("dk", 8), ("dv", 9), ("dz", 10), ("rq", 3), ("rk", 4), ("rv", 5), ("rz", 6),
               ("gu", 0), ("gv", 1), ("gz", 2))
FF_WIDTHS = (512,) * 5 + (256,)
HYB_SPLIT = (("z", 0, 2), ("xbc", 1024, 3), ("q", 2576, 2), ("k", 3600, 2), ("v", 4624, 2))


def units_of(rows, width):
    per, chunks = UNIT // width, rows // P
    return [min(per, chunks - c) for c in range(0, chunks, per)]


def pack_block(matrix, col, width):
    out, row = [], 0
    for kc in units_of(matrix.shape[0], width):
        u = np.zeros((P, UNIT), np.float32)
        part = matrix[row:row + kc * P, col:col + width].reshape(kc, P, width).transpose(1, 0, 2)
        u[:, :kc * width] = part.reshape(P, kc * width)
        out.append(u)
        row += kc * P
    return out


def pack_ffn(w_in, w_out):
    out, col = [], 0
    for w in FF_WIDTHS:
        out += pack_block(w_in, col, w) + pack_block(w_in, FF + col, w)
        col += w
    for b in range(2):
        out += pack_block(w_out, 512 * b, 512)
    return out


def pack_weights(a):
    out = []
    for l in range(DEPTH):
        for _, b in W_IN_STAGES:
            out += pack_block(a["w_in"][l], 512 * b, 512)
        for part, n in (("w_gate", 0), ("w_gate", 1), ("w_branch_out", 0), ("w_branch_out", 1), ("w_gate", 2),
                        ("w_branch_out", 2)):
            w = a[part][l]
            for b in range(2):
                out += pack_block(w[:, n, :] if part == "w_gate" else w[n], 512 * b, 512)
        for b in range(2):
            out += pack_block(a["w_out"][l], 512 * b, 512)
    out += pack_ffn(a["ffn_w_in_2"][0, 0], a["ffn_w_out_2"][0, 0])
    for _, col, n in HYB_SPLIT:
        for b in range(n):
            out += pack_block(a["hyb_w_in_2"][0], col + 512 * b, 512)
    for b in range(2):
        out += pack_block(a["hyb_w_out_2"][0], 512 * b, 512)
    out += pack_ffn(a["ffn_w_in_2"][0, 1], a["ffn_w_out_2"][0, 1])
    out += pack_ffn(a["ffn_w_in_2"][1, 0], a["ffn_w_out_2"][1, 0])
    for b in (2, 3, 0, 1):
        out += pack_block(a["rec_w_in_2"][0], 512 * b, 512)
    for b in range(2):
        out += pack_block(a["rec_w_out_2"][0], 512 * b, 512)
    out += pack_ffn(a["ffn_w_in_2"][1, 1], a["ffn_w_out_2"][1, 1])
    return np.stack(out)


def cols(v):
    return np.asarray(v, np.float32).reshape(-1, P).T


def rows(v):
    v = np.asarray(v, np.float32).reshape(1, -1)
    return np.broadcast_to(v, (P, v.shape[1]))


def chunked(m):
    k, n = m.shape
    return np.asarray(m, np.float32).reshape(k // P, P, n).transpose(1, 0, 2).reshape(P, -1)


FP = {}
_at = 0
for _n, _w in (("small_w", KD * 16), ("norm_g", KD), ("conv", 36), ("dtb", 8), ("a_log", 8), ("ret_g", 4),
               ("gdn_g", 1), ("b_s", 4), ("decay", 8)):
    FP[_n] = (_at, _at + _w)
    _at += _w
FP_W = _at
SP = {}
_at = 0
for _n, _w in (("small_w", KD * 24), ("g0", KD), ("g2", KD), ("g4", KD), ("conv", 48), ("conv_b", 12),
               ("dtb", 16), ("a_log", 16), ("d", 16), ("norm_g", KD), ("fox_b", 8)):
    SP[_n] = (_at, _at + _w)
    _at += _w
SP_W = _at
RP = {}
_at = 0
for _n, _w in (("g0", KD), ("g2", KD), ("g4", KD), ("conv", 32), ("conv_b", 8), ("b_a", 8), ("b_x", 8), ("lam", 8)):
    RP[_n] = (_at, _at + _w)
    _at += _w
RP_W = _at
PAR_W = max(FP_W, SP_W, RP_W)


def pack_params(a):
    out = np.zeros((4, P, PAR_W), np.float32)
    for l in range(DEPTH):
        parts = {
            "small_w": chunked(a["w_in"][l][:, 11 * 512:]), "norm_g": cols(a["norm_g"][l]),
            "conv": np.concatenate([cols(a["gdn_conv_w"][l, k]) for k in range(3)], 1),
            "dtb": rows(a["gdn_dt_bias"][l]), "a_log": rows(a["gdn_a_log"][l]),
            "ret_g": cols(a["ret_norm_g"][l]), "gdn_g": cols(a["gdn_norm_g"][l]),
            "b_s": np.asarray(a["gm_b_s"][l]).T, "decay": rows(a["ret_decay_logit"][l]),
        }
        for n, v in parts.items():
            out[l, :, FP[n][0]:FP[n][1]] = v
    w = a["hyb_w_in_2"][0]
    g = a["norm_g_2"]
    parts = {
        "small_w": chunked(np.concatenate([w[:, 2560:2576], w[:, 5648:5656]], 1)),
        "g0": cols(g[0, 0]), "g2": cols(g[0, 2]), "g4": cols(g[0, 4]),
        "conv": np.concatenate([cols(a["ssm_conv_w_2"][0, k]) for k in range(4)], 1),
        "conv_b": cols(a["ssm_conv_b_2"][0]), "dtb": rows(a["ssm_dt_bias_2"][0]),
        "a_log": rows(a["ssm_a_log_2"][0]), "d": rows(a["ssm_d_2"][0]), "norm_g": cols(a["ssm_norm_g_2"][0]),
        "fox_b": rows(a["fox_b_f_2"][0]),
    }
    for n, v in parts.items():
        out[2, :, SP[n][0]:SP[n][1]] = v
    parts = {
        "g0": cols(g[1, 0]), "g2": cols(g[1, 2]), "g4": cols(g[1, 4]),
        "conv": np.concatenate([cols(a["rec_conv_w_2"][0, k]) for k in range(4)], 1),
        "conv_b": cols(a["rec_conv_b_2"][0]), "b_a": cols(a["rec_b_a_2"][0]), "b_x": cols(a["rec_b_x_2"][0]),
        "lam": cols(a["rec_lambda_2"][0]),
    }
    for n, v in parts.items():
        out[3, :, RP[n][0]:RP[n][1]] = v
    return out


def pack_wide(a):
    g = a["norm_g_2"]
    v = [g[0, 1], g[0, 3], g[0, 5], g[1, 1], g[1, 3], g[1, 5], a["final_norm_g"]]
    v += [np.concatenate([a["gm_ln_g"][l], a["gm_ln_b"][l]]) for l in range(DEPTH)]
    return np.ascontiguousarray(np.stack([np.broadcast_to(np.asarray(x, np.float32), (P, D)) for x in v]))


def pack_token_mix(a):
    ws = np.ascontiguousarray(np.asarray(a["gm_w_s"]).transpose(0, 3, 1, 2).reshape(DEPTH, P, 4 * P))
    wax = [np.asarray(a[n][0]).transpose(1, 0, 2).reshape(P, 8 * P) for n in ("rec_w_a_2", "rec_w_x_2")]
    return ws, np.ascontiguousarray(np.stack(wax))


CONST_NAMES = ("ident", "up64", "lo64", "same64", "half0", "half1", "up128", "ones", "neg_causal")
CHUNK = 64
MASK_NAMES = ("eye", "up", "lo", "ups", "los", "nlo1", "nlo2", "nlo4", "nlo8", "nlo16", "nlo32", "nup1")


def constants():
    i = np.arange(P)
    p, f = i[:, None], i[None, :]
    same = (p // 64) == (f // 64)
    c = {
        "ident": p == f, "up64": same & (p <= f), "lo64": same & (p >= f),
        "same64": same, "half0": (p < 64) & (f >= 0), "half1": (p >= 64) & (f >= 0),
        "up128": p <= f, "ones": np.ones((P, P)), "neg_causal": np.where(f > p, -1e30, 0.0),
    }
    q, g = p % CHUNK, np.arange(CHUNK)[None, :]
    c |= {"eye": q == g, "up": q <= g, "lo": q >= g, "ups": q < g, "los": q > g}
    for s in (1, 2, 4, 8, 16, 32):
        c[f"nlo{s}"] = -1.0 * ((q // (2 * s) == g // (2 * s)) & (q // s > g // s))
    c["nup1"] = -1.0 * ((q // 2 == g // 2) & (q < g))
    main = np.concatenate([np.asarray(c[n], np.float32) for n in CONST_NAMES + MASK_NAMES], 1)
    inv = np.float32(10000.0) ** (-np.arange(0, HD, 2, dtype=np.float32) / np.float32(HD))
    ang = np.arange(S, dtype=np.float32)[:, None] * inv[None, :]
    rope = [t.reshape(M, P, HD // 2).transpose(1, 0, 2).reshape(P, M * HD // 2) for t in (np.cos(ang), np.sin(ang))]
    dist = []
    for sign in (1, -1):
        for jm in range(M):
            q = np.arange(S)[None, :]
            k = (jm * P + i)[:, None]
            dist.append(np.maximum(sign * (q - k), 0))
    return (np.ascontiguousarray(np.concatenate([main] + rope, 1).astype(np.float32)),
            np.ascontiguousarray(np.concatenate(dist, 1).astype(np.float32)))


class Counter:

    def __init__(self, eng, sems, own):
        self.eng, self.sems, self.own, self.seen = eng, sems, own, {}

    def wait(self, name, k=1):
        self.seen[name] = self.seen.get(name, 0) + k
        self.eng.wait_ge(self.sems[name], self.seen[name])

    def sig(self, ins, name):
        ins.then_inc(self.sems[name], 1)
        self.wait(name)

    def step(self, ins):
        self.sig(ins, self.own)


class Stream:

    def __init__(self):
        self.split = self.used = self.block = 0
        self.evacs = {"evac_act": 0, "evac_dve": 0}
        self.history = []


def program(nc, x_in, weights, params, wide, token_mix, gate_mix, const, dist, out):
    NU = weights.shape[0]
    with ExitStack() as ctx:
        def sb(name, shape, dt=F32):
            return ctx.enter_context(nc.sbuf_tensor(name, shape, dt))

        SEMS = (
            "a_ready", "act_step", "back_read", "back_tr", "cb_ready", "const_landed", "conv_act", "conv_read",
            "conv_tr", "cum_done", "cum_exp", "cum_read", "cum_t", "cum_t_read", "decay_ready", "delta_z_ready",
            "dist_landed", "dist_ready", "dve_step", "evac_act", "evac_dve", "feat_read", "feat_tr",
            "final_g_landed", "first_params_landed", "fox_done", "fox_read", "gate_abs", "gate_exp", "gate_g",
            "gram_done", "gt_done", "h_ready", "ident_landed", "inv_scaled", "inv_t", "inv_tm", "inv_x",
            "inv_y", "inv_yt", "kv_done", "lam_ready", "lin_done", "logits_read", "logits_ready", "low_ready",
            "low_t", "low_t_read", "mask_arg", "mask_ready", "mix_done", "mix_landed", "o_ready", "o_sq",
            "ot_ready", "out_landed", "out_read", "ov_done", "params_landed", "params_used", "probs_ready",
            "probs_t", "probs_t_read", "product_sq", "qk_done", "qk_ready", "qs_done", "r_ready", "rec_out",
            "rope_done", "row_done", "rs_ready", "rv_ready", "sc_masked", "sc_ready", "small_done",
            "small_read", "small_w_high", "small_w_low", "split_high", "split_low", "sq_done", "sq_free",
            "sq_ready", "ssd_decay", "ssd_done", "ssd_mask", "state_ready", "state_scaled", "sv_done",
            "tr_done", "tr_high", "tr_low", "u_ready", "u_sqrt", "unit_used", "uw_done", "v_ready", "vd_ready",
            "vn_ready", "wide_landed", "ws_done", "x_landed", "x_ready", "x_squares", "y_ready",
        )
        sem = {n: ctx.enter_context(nc.semaphore(n)) for n in SEMS}
        weight_landed = [ctx.enter_context(nc.semaphore(f"weight_landed{i}")) for i in range(RAW_SLOTS)]

        raw = sb("raw", [P, RAW_SLOTS, UNIT])
        wh = sb("wh", [P, SPLIT_SLOTS, UNIT], F32R)
        wl = sb("wl", [P, SPLIT_SLOTS, UNIT], F32R)
        with nc.sbuf_tensor("plainh", [P, KF, S], F32) as plainh, nc.sbuf_tensor("plainl", [P, KF, S], F32) as plainl:
            pass
        hTh = sb("hTh", [P, KF, S], F32R)
        hTl = sb("hTl", [P, KF, S], F32R)
        x = sb("x", [P, M, D])
        xn = sb("xn", [P, M * D])
        cst = sb("cst", [P, const.shape[1]])
        par = sb("par", [P, PAR_W])
        swh = sb("swh", [P, KD * 24], F32R)
        swl = sb("swl", [P, KD * 24], F32R)
        sm = sb("sm", [P, 948])
        arena = sb("arena", [P, 14848])
        pg = ctx.enter_context(nc.psum_tensor("pg", [P, 4, 512], F32))
        ps = ctx.enter_context(nc.psum_tensor("ps", [P, 4, 512], F32))

        C = {n: cst[:, i * P:(i + 1) * P] for i, n in enumerate(CONST_NAMES)}
        at = len(CONST_NAMES) * P
        MASK = {n: cst[:, at + i * CHUNK:at + (i + 1) * CHUNK] for i, n in enumerate(MASK_NAMES)}
        at += len(MASK_NAMES) * CHUNK
        COS = cst[:, at:at + P].rearrange("p (m d) -> p m d", m=M)
        SIN = cst[:, at + P:at + 2 * P].rearrange("p (m d) -> p m d", m=M)
        ident = C["ident"]

        def V(off, n=1024):
            return arena[:, off:off + n]

        def heads(ap, n=NH):
            return ap.rearrange("p (h e) -> p h e", h=n)

        def fp(name):
            return par[:, FP[name][0]:FP[name][1]]

        def spar(name):
            return par[:, SP[name][0]:SP[name][1]]

        def rp(name):
            return par[:, RP[name][0]:RP[name][1]]

        def over(ap, n):
            return ap.unsqueeze(2).broadcast_to([ap.shape[0], ap.shape[1], n])

        def blocks(ap):
            return ap.rearrange("p (j m f) -> p j m f", m=M, f=CHUNK)

        def half(i):
            return slice(i * CHUNK, (i + 1) * CHUNK)

        def scan_chunk(t, d):
            ck = t if d == 0 else 3 - t
            return ck // 2, ck % 2

        def times(ap, n):
            return ap.unsqueeze(1).broadcast_to([ap.shape[0], n, ap.shape[1]])

        SS, RS, SS4, SX4 = sm[:, 0:2], sm[:, 2:4], sm[:, 4:8], sm[:, 940:944]
        SPL = sm[:, 8:24]
        STATS = sm[:, 24:32]
        ABS = sm[:, 56:72]
        BETA = sm[:, 72:88]
        GLOG = sm[:, 88:104]
        NEGA = sm[:, 104:112]
        GC = sm[:, 112:128]
        GCJ = sm[:, 128:144]
        MV = sm[:, 288:304]
        BETAJ = sm[:, 664:680]
        EKD = sm[:, 160:176]
        EGL = sm[:, 176:208]
        EGS = sm[:, 208:224]
        TOT = sm[:, 224:240]
        BN = sm[:, 240:288]
        GL = sm[:, 304:336]
        LAM, E8, TMP8 = sm[:, 336:344], sm[:, 8:16], sm[:, 16:24]
        GCT = sm[0:8, 344:600]
        SMR = sm[:, 600:616]
        EKS, NEGS = sm[:, 632:648], sm[:, 648:664]
        NEWTON = sm[:, 892:940]
        QS = sm[:, 616:632]

        SAB, SG, SCUM = sm[:, 40:88], sm[:, 88:136], sm[:, 136:184]
        DT, SEXP = sm[:, 232:264], sm[:, 264:312]
        SCUMT, SCUMTN = sm[0:24, 344:600], sm[0:24, 632:888]
        SNEGA = sm[:, 312:336]
        NMAX, RSUM = sm[:, 600:616], sm[:, 616:632]

        kn, TB, knT, qnT, o_acc = V(0), V(1024), V(2048), V(3072), V(4096)
        Lm, LT, X_, XT_, TM_ = V(5120), V(6144), V(7168), V(8192), V(9216)
        SC_, LMASK = xn[:, 0:1024], xn[:, 1024:2048]
        STATE = V(5120)
        RV, VN, VD, OT = V(6144, 512), V(6656, 512), V(9216, 512), V(9728, 512)
        VS = V(10240, 2048).rearrange("p (t e) -> p t e", t=4)
        rawp = [V(5120), V(6144), V(7168)]
        cvp = [V(8192), V(9216), V(10240)]
        sq, qn = V(12288), V(13312)

        def spare(t, at, n=4):
            return t[:, at:at + n, :].rearrange("p k s -> p (k s)")

        DELTA_Z, RET_Q, RET_K, RET_V = (spare(plainl, 16), spare(plainh, 16), spare(plainh, 12), spare(plainl, 12))
        RET_Z = (spare(plainh, 20, 2), spare(plainl, 20, 2))
        MLP_U, MLP_V, MLP_Z = xn[:, 1024:2048], V(7168), spare(plainh, 16)
        DELTA_BLOCKS = [(v[:, 0:512], v[:, 512:1024], ACT.Copy) for v in (DELTA_Z, RET_Q, RET_K, RET_V)]
        DELTA_BLOCKS += [RET_Z + (ACT.Silu,)]
        DELTA_BLOCKS += [(v[:, 0:512], v[:, 512:1024], f)
                         for v, f in ((MLP_U, ACT.Gelu), (MLP_V, ACT.Gelu), (MLP_Z, ACT.Silu))]

        def column_halves(v, f):
            return [(v[:, o:o + 512], v[:, D + o:D + o + 512], f) for o in (0, 512)]

        FOX_Q, FOX_K, FOX_V, REC_GATE = xn[:, :], V(2048, 2048), V(4096, 2048), V(2048, 2048)
        FOX_BLOCKS = [b for v in (FOX_Q, FOX_K, FOX_V) for b in column_halves(v, ACT.Copy)]
        REC_BLOCKS = column_halves(REC_GATE, ACT.Gelu_apprx_tanh)

        IN_SCAN = 3 + 4 * 2 + 3
        PREPARE_AFTER_SCAN = 8 * KD - (3 + 5 + 3 + 3 + 2 + 1 + 1 + 4 + 4 + 2 * 5) - IN_SCAN - 4 - 4

        DIST, MASKS, LN_GAINS, TOKEN_MIX = spare(plainh, 8), V(12288, 2048), V(8192), V(9216, 512)

        X_AT = KF - KD
        EARLY = range(X_AT // 2)
        LATE = range(X_AT // 2, KF // 2)

        block = ctx.enter_context(nc.Block())

        @block.tensor
        def _(pe):
            c = Counter(pe, sem, None)
            st = Stream()

            def split_product(dst, lh, ll, rh, rl, first, last):
                pe.matmul(dst, lh, rh, start=first, stop=False)
                pe.matmul(dst, lh, rl, start=False, stop=False)
                return pe.matmul(dst, ll, rh, start=False, stop=last)

            prepared = [0]

            def prepare(n):
                for _ in range(n):
                    k = prepared[0] % KD
                    if k == 0:
                        pe.wait_ge(sem[st.history[-2][0]], st.history[-2][1])
                    if k % 4 == 0:
                        pe.wait_ge(sem["split_low"], st.used + 1)
                    pair, slot, i = st.block % 2, st.used % SPLIT_SLOTS, k % 4
                    for m in range(M):
                        last = split_product(pg[:, 2 * pair + m, :], hTh[:, k, m * P:(m + 1) * P],
                                             hTl[:, k, m * P:(m + 1) * P], wh[:, slot, i * 512:(i + 1) * 512],
                                             wl[:, slot, i * 512:(i + 1) * 512], k == 0, k == KD - 1)
                    if i == 3:
                        last.then_inc(sem["unit_used"], 1)
                        st.used += 1
                    prepared[0] += 1
                    if k == KD - 1:
                        st.evacs["evac_act"] += 1
                        st.history.append(("evac_act", st.evacs["evac_act"]))
                        st.block += 1

            groups = {"made": 0, "waited": 0}
            group_of = {}

            def low_parts_of(position):
                need = group_of.get(position, 0)
                if need > groups["waited"]:
                    pe.wait_ge(sem["tr_low"], need)
                    groups["waited"] = need

            def gemm(rows_, widths, evacs, chunk0=0, order=None, between=None, after=2):
                units_done = 0
                for w, by in zip(widths, evacs):
                    if st.block >= 2:
                        pe.wait_ge(sem[st.history[-2][0]], st.history[-2][1])
                    pair = st.block % 2
                    k = 0
                    units = units_of(rows_, w)
                    for kc in units:
                        slot = st.used % SPLIT_SLOTS
                        pe.wait_ge(sem["split_low"], st.used + 1)
                        for i in range(kc):
                            ch = order[k] if order else chunk0 + k
                            low_parts_of(ch)
                            for m in range(M):
                                last = split_product(
                                    pg[:, 2 * pair + m, 0:w], hTh[:, ch, m * P:(m + 1) * P],
                                    hTl[:, ch, m * P:(m + 1) * P], wh[:, slot, i * w:(i + 1) * w],
                                    wl[:, slot, i * w:(i + 1) * w], k == 0, k == rows_ // P - 1)
                            k += 1
                        last.then_inc(sem["unit_used"], 1)
                        st.used += 1
                        units_done += 1
                        if between and units_done == after:
                            between()
                    st.evacs[by] += 1
                    st.history.append((by, st.evacs[by]))
                    st.block += 1

            def transpose_groups(src, gs, dst):
                for g in gs:
                    n = groups["made"]
                    if n - 3 > groups["waited"]:
                        pe.wait_ge(sem["tr_low"], n - 3)
                        groups["waited"] = n - 3
                    for j in range(2):
                        for m in range(M):
                            last = pe.transpose(ps[:, n % 4, (2 * j + m) * P:(2 * j + m + 1) * P],
                                                src[:, m, (2 * g + j) * P:(2 * g + j + 1) * P], ident)
                    last.then_inc(sem["tr_done"], 1)
                    groups["made"] = n + 1
                    group_of[dst + 2 * g] = group_of[dst + 2 * g + 1] = n + 1

            def transpose_split(src, chunks, dst=0, drain=True):
                transpose_groups(src, range(chunks // 2), dst)
                if drain and groups["made"] > groups["waited"]:
                    pe.wait_ge(sem["tr_low"], groups["made"])
                    groups["waited"] = groups["made"]

            def small_gemm(n):
                c.wait("small_w_low")
                for m in range(M):
                    for k in range(KD):
                        last = split_product(ps[:, m, 0:n], hTh[:, k, m * P:(m + 1) * P], hTl[:, k, m * P:(m + 1) * P],
                                             swh[:, k * n:(k + 1) * n], swl[:, k * n:(k + 1) * n], k == 0, k == KD - 1)
                last.then_inc(sem["small_done"], 1)

            def features_of_x(dst=0):
                for b in range(2):
                    c.wait("x_ready")
                    transpose_groups(x, (2 * b, 2 * b + 1), dst)

            def gdn():
                gemm(D, (512,) * 3, ("evac_act",) * 3)
                small_gemm(16)
                c.wait("small_read")
                for t in range(3):
                    pe.wait_ge(sem["evac_act"], st.evacs["evac_act"] - 2 + t)
                    if t == 2:
                        c.wait("conv_read")
                    src = rawp[t].rearrange("p (m d) -> p m d", m=M)
                    for h in range(NH):
                        for m in range(M):
                            b = 2 * (t % 2) + h // 2
                            last = pe.transpose(ps[:, b, ((h % 2) * M + m) * P:((h % 2) * M + m + 1) * P],
                                                src[:, m, h * P:(h + 1) * P], ident)
                    last.then_inc(sem["conv_tr"], 1)
                    if t == 1:
                        prepare(3)
                prepare(5)
                c.wait("conv_read", 2)
                for t in range(3):
                    c.wait("conv_act")
                    if t == 2:
                        prepare(3)
                        c.wait("qk_ready")
                    src = cvp[t].rearrange("p (h s) -> p h s", h=NH)
                    for m in range(M):
                        for h in range(NH):
                            last = pe.transpose(ps[:, 2 * (t % 2) + m, h * P:(h + 1) * P],
                                                src[:, h, m * P:(m + 1) * P], ident)
                    last.then_inc(sem["back_tr"], 1)
                prepare(3)
                c.wait("qk_ready")
                c.wait("back_read")
                for t, src in enumerate((qn, kn)):
                    s = src.rearrange("p (m d) -> p m d", m=M)
                    for h in range(NH):
                        for m in range(M):
                            last = pe.transpose(ps[:, 2 * t + h // 2, ((h % 2) * M + m) * P:((h % 2) * M + m + 1) * P],
                                                s[:, m, h * P:(h + 1) * P], ident)
                    last.then_inc(sem["feat_tr"], 1)
                prepare(2)
                c.wait("feat_read", 2)
                pe.wait_ge(sem["const_landed"], 16)
                c.wait("gate_g")
                g3 = GLOG.rearrange("p (m j) -> p m j", m=M)
                gc = ps[:, 0, 0:16].rearrange("p (m j) -> p m j", m=M)
                pe.matmul(gc[:, :, 0:4], C["up64"], g3[:, :, 0:4], start=True, stop=True)
                pe.matmul(gc[:, :, 4:8], C["lo64"], g3[:, :, 4:8], start=True, stop=True)
                pe.matmul(ps[:, 0, 16:32], C["same64"], GLOG, start=True, stop=True)
                totals = ps[:, 0, 32:64].rearrange("p (m r j) -> p m r j", m=M, r=2)
                for r in range(2):
                    last = pe.matmul(totals[:, :, r, :], C[f"half{r}"], g3, start=True, stop=True)
                last.then_inc(sem["cum_done"], 1)
                prepare(1)
                c.wait("cum_read")
                for m in range(M):
                    last = pe.transpose(ps[0:8, 1, m * P:(m + 1) * P], GC[:, 8 * m:8 * m + 8], ident)
                last.then_inc(sem["cum_t"], 1)
                prepare(1)
                c.wait("cum_t_read")
                kT, qT = knT.rearrange("p (h s) -> p h s", h=NH), qnT.rearrange("p (h s) -> p h s", h=NH)
                L4, LT4, X4, XT4, T4 = (blocks(v) for v in (Lm, LT, X_, XT_, TM_))

                def tokens(m, r):
                    return slice(m * P + r * CHUNK, m * P + (r + 1) * CHUNK)

                gct = GCT.rearrange("p (m r f) -> p m r f", m=M, r=2)
                for j in range(8):
                    for r in range(2):
                        last = pe.matmul(ps[half(r), 2 + j // 4, (j % 4) * P:(j % 4 + 1) * P],
                                         ident[0:8, j:j + 1].broadcast_to([8, CHUNK]), gct[:, :, r, :],
                                         start=True, stop=True)
                last.then_inc(sem["row_done"], 1)
                for b, src in enumerate((kT, qT)):
                    for h in range(NH):
                        for m in range(M):
                            for r in range(2):
                                last = pe.matmul(ps[half(r), b, (h * M + m) * CHUNK:(h * M + m + 1) * CHUNK],
                                                 kT[:, h, tokens(m, r)], src[:, h, tokens(m, r)], start=True, stop=True)
                    last.then_inc(sem["gram_done"], 1)

                def block_products(d, bank, lhs, rhs, done):
                    for h in range(NH):
                        for m in range(M):
                            for r in range(2):
                                last = pe.matmul(ps[half(r), bank, (h * M + m) * CHUNK:(h * M + m + 1) * CHUNK],
                                                 lhs[half(r), 4 * d + h, m, :], rhs[half(r), 4 * d + h, m, :],
                                                 start=True, stop=True)
                    last.then_inc(sem[done], 1)

                prepare(4)
                c.wait("low_ready")
                for d in range(2):
                    for h in range(NH):
                        for m in range(M):
                            for r in range(2):
                                last = pe.matmul(ps[half(r), 2 + d, (h * M + m) * CHUNK:(h * M + m + 1) * CHUNK],
                                                 L4[half(r), 4 * d + h, m, :], ident[half(r), half(r)],
                                                 start=True, stop=True)
                last.then_inc(sem["low_t"], 1)
                prepare(4)
                for s in (2, 4, 8, 16, 32):
                    for d in range(2):
                        c.wait("inv_x")
                        block_products(d, d, LT4 if d == 0 else L4, X4, "inv_t")
                    prepare(1)
                    for d in range(2):
                        c.wait("inv_tm")
                        if s < 32 or d == 1:
                            block_products(d, 2 + d, XT4, T4, "inv_y")
                        if s < 32 or d == 0:
                            block_products(d, d, T4, XT4, "inv_yt")
                    prepare(1)
                c.wait("inv_scaled")
                TB4, SC4, S3 = blocks(TB), blocks(SC_), heads(STATE, 8)
                places = [[(d, *scan_chunk(t, d)) for d in range(2)] for t in range(4)]
                for t in range(4):
                    if t:
                        c.wait("state_ready")
                        for bank, src, done in ((0, kT, "ws_done"), (1, qT, "qs_done")):
                            if bank:
                                c.wait("o_ready")
                            for h in range(NH):
                                for d, m, r in places[t]:
                                    last = pe.matmul(ps[half(r), bank, h * P:(h + 1) * P], src[:, h, tokens(m, r)],
                                                     S3[:, 4 * d + h, :], start=True, stop=True)
                            last.then_inc(sem[done], 1)
                        prepare(1)
                        c.wait("rv_ready")
                    for h in range(NH):
                        for d, m, r in places[t]:
                            rhs = RV[half(r), h * P:(h + 1) * P] if t else VS[half(r), 0, h * P:(h + 1) * P]
                            last = pe.matmul(ps[half(r), 0, h * P:(h + 1) * P], TB4[half(r), 4 * d + h, m, :], rhs,
                                             start=True, stop=True)
                    last.then_inc(sem["uw_done"], 1)
                    prepare(1)
                    if t < 3:
                        c.wait("vd_ready")
                        for h in range(NH):
                            for d, m, r in places[t]:
                                last = pe.matmul(ps[:, 2 + d, h * P:(h + 1) * P],
                                                 kn[half(r), (m * NH + h) * P:(m * NH + h + 1) * P],
                                                 VD[half(r), h * P:(h + 1) * P], start=True, stop=True)
                        last.then_inc(sem["kv_done"], 1)
                        prepare(1)
                    c.wait("vn_ready")
                    if t:
                        c.wait("ot_ready")
                    for h in range(NH):
                        for d, m, r in places[t]:
                            last = pe.matmul(ps[half(r), 1, h * P:(h + 1) * P], SC4[half(r), 4 * d + h, m, :],
                                             VN[half(r), h * P:(h + 1) * P], start=True, stop=True)
                    last.then_inc(sem["sv_done"], 1)
                    prepare(1)
                c.wait("o_ready")

            def retention():
                prepare(PREPARE_AFTER_SCAN)
                for t, src in enumerate((V(0), V(1024))):
                    c.wait("rope_done")
                    v = src.rearrange("p (m d) -> p m d", m=M)
                    for h in range(NH):
                        for m in range(M):
                            last = pe.transpose(ps[:, 2 * t + h // 2, ((h % 2) * M + m) * P:((h % 2) * M + m + 1) * P],
                                                v[:, m, h * P:(h + 1) * P], ident)
                    last.then_inc(sem["feat_tr"], 1)
                prepare(4)
                c.wait("feat_read", 2)
                c.wait("y_ready")
                transpose_split(o_acc.rearrange("p (m d) -> p m d", m=M), NH, 8, drain=False)
                prepare(4)
                pe.wait_ge(sem["tr_low"], groups["made"])
                groups["waited"] = groups["made"]
                kT, qT = V(2048).rearrange("p (h s) -> p h s", h=NH), V(3072).rearrange("p (h s) -> p h s", h=NH)
                v = RET_V.rearrange("p (m h e) -> p m h e", m=M, h=NH)
                for h in range(NH):
                    b = h % 2
                    if h >= 2:
                        c.wait("sc_ready")
                    for jm in range(M):
                        last = pe.matmul(ps[:, b, jm * S:(jm + 1) * S], kT[:, h, jm * P:(jm + 1) * P], qT[:, h, :],
                                         start=True, stop=True)
                    last.then_inc(sem["qk_done"], 1)
                    if h == 1:
                        c.wait("sc_ready")
                    if h >= 1:
                        values(h - 1, v)
                c.wait("sc_ready")
                values(NH - 1, v)

            def values(g, v):
                sc = V(5120 + 512 * (g % 2), 512).rearrange("p (j s) -> p j s", j=M)
                for im in range(M):
                    for jm in range(M):
                        last = pe.matmul(ps[:, 2 + im, g * P:(g + 1) * P], sc[:, jm, im * P:(im + 1) * P],
                                         v[:, jm, g, :], start=(jm == 0), stop=(jm == M - 1))
                last.then_inc(sem["ov_done"], 1)

            def gmlp(l):
                c.wait("v_ready")
                pe.wait_ge(sem["mix_landed"], 16 * (l + 1))
                v = MLP_V.rearrange("p (m g e) -> p m g e", m=M, g=NH)
                ws = TOKEN_MIX.rearrange("p (g q) -> p g q", g=NH)
                for m in range(M):
                    for g in range(NH):
                        last = pe.matmul(ps[:, m, g * P:(g + 1) * P], ws[:, g, :], v[:, m, g, :], start=True, stop=True)
                last.then_inc(sem["mix_done"], 1)

            def merge_out(l):
                gemm(D, (512,) * 2, ("evac_act",) * 2)
                gmlp(l)
                gemm(D, (512,), ("evac_act",))
                c.wait("y_ready", 2)
                transpose_split(V(0).rearrange("p (m d) -> p m d", m=M), NH, 12, drain=False)
                transpose_split(V(1024).rearrange("p (m d) -> p m d", m=M), NH, 16, drain=False)
                gemm(D, (512,), ("evac_act",))
                for n in range(3):
                    if n == 2:
                        gemm(D, (512,) * 2, ("evac_act",) * 2)
                    gemm(BW, (512,) * 2, ("evac_dve",) * 2, chunk0=16 - 4 * n)
                merged = V(0, 2048).rearrange("p (m d) -> p m d", m=M)
                c.wait("y_ready")
                transpose_groups(merged, (0, 1), 0)

                def second_half():
                    c.wait("y_ready")
                    transpose_groups(merged, (2, 3), 0)
                gemm(D, (512,) * 2, ("evac_dve",) * 2, between=second_half, after=1)

            def ffn():
                features_of_x(X_AT)
                hid = V(0, 2 * FF).rearrange("p (m f) -> p m f", m=M)
                for j, w in enumerate(FF_WIDTHS):
                    gemm(D, (w, w), ("evac_act", "evac_dve"), chunk0=X_AT)
                    if j:
                        pe.wait_ge(sem["evac_dve"], st.evacs["evac_dve"] - 1)
                        transpose_groups(hid, [g for g in EARLY if g // 2 == j - 1], 0)

                def late():
                    pe.wait_ge(sem["evac_dve"], hidden_done)
                    transpose_groups(hid, LATE, 0)
                hidden_done = st.evacs["evac_dve"]
                gemm(FF, (512,) * 2, ("evac_dve",) * 2, between=late)

            def hybrid():
                features_of_x()
                gemm(D, (512,) * 5, ("evac_act",) * 5)
                small_gemm(24)
                c.wait("small_read")
                raw3 = V(0, 3072).rearrange("p (m f) -> p m f", m=M)
                pe.wait_ge(sem["evac_act"], st.evacs["evac_act"])
                for g in range(6):
                    if g == 4:
                        prepare(3)
                    if g >= 4:
                        c.wait("conv_read")
                    for j in range(2):
                        for m in range(M):
                            last = pe.transpose(ps[:, g % 4, (2 * j + m) * P:(2 * j + m + 1) * P],
                                                raw3[:, m, (2 * g + j) * P:(2 * g + j + 1) * P], ident)
                    last.then_inc(sem["conv_tr"], 1)
                prepare(7)
                prepare(7)
                c.wait("conv_read", 4)
                cv = V(3072, 3072).rearrange("p (k s) -> p k s", k=12)
                c.wait("conv_act")
                for m in range(M):
                    for k in range(8):
                        last = pe.transpose(ps[:, 2 * m + k // 4, (k % 4) * P:(k % 4 + 1) * P],
                                            cv[:, k, m * P:(m + 1) * P], ident)
                last.then_inc(sem["back_tr"], 1)
                prepare(2)
                c.wait("back_read")
                c.wait("gate_g")
                for m in range(M):
                    o = 24 * m
                    pe.matmul(ps[:, 0, o:o + 24], C["up128"], SG[:, 24 * m:24 * m + 24], start=True, stop=(m == 0))
                    if m:
                        last = pe.matmul(ps[:, 0, o:o + 24], C["ones"], SG[:, 0:24], start=False, stop=True)
                last.then_inc(sem["cum_done"], 1)
                prepare(1)
                c.wait("cum_read")
                for m in range(M):
                    last = pe.transpose(ps[0:24, 1, m * P:(m + 1) * P], SCUM[:, 24 * m:24 * m + 24], ident)
                last.then_inc(sem["cum_t"], 1)
                prepare(1)
                c.wait("cum_t_read")
                for g in range(2):
                    for jm in range(M):
                        n = S - jm * P
                        last = pe.matmul(ps[:, 2 + g, jm * S:jm * S + n], cv[:, 8 + g, jm * P:(jm + 1) * P],
                                         cv[:, 10 + g, jm * P:S], start=True, stop=True)
                last.then_inc(sem["gram_done"], 1)
                prepare(2)
                c.wait("cb_ready")
                Xd = V(0, 2048).rearrange("p (m h e) -> p m h e", m=M, h=16)
                for h in range(16):
                    if h >= 2:
                        c.wait("ssd_decay")
                    last = pe.matmul(ps[:, h % 2, 0:S], ident[0:24, h:h + 1].broadcast_to([24, P]), SCUMT,
                                     start=True, stop=True)
                    last.then_inc(sem["row_done"], 1)
                    prepare(1)
                    if h >= 1:
                        ssd_out(h - 1, Xd)
                ssd_out(15, Xd)
                c.wait("ssd_decay", 2)
                prepare(4)
                prepare(5)
                c.wait("y_ready")
                transpose_split(V(8192, 2048).rearrange("p (m d) -> p m d", m=M), KD, 8)
                pe.wait_ge(sem["evac_act"], st.evacs["evac_act"])
                for t in range(2):
                    src = (FOX_Q, FOX_K)[t].rearrange("p (m d) -> p m d", m=M)
                    for g in range(4):
                        if t:
                            c.wait("feat_read")
                        for j in range(2):
                            for m in range(M):
                                last = pe.transpose(ps[:, g, (2 * j + m) * P:(2 * j + m + 1) * P],
                                                    src[:, m, (2 * g + j) * P:(2 * g + j + 1) * P], ident)
                        last.then_inc(sem["feat_tr"], 1)
                c.wait("feat_read", 4)
                qT, kT = (V(o, 2048).rearrange("p (h s) -> p h s", h=8) for o in (6144, 8192))
                v = FOX_V.rearrange("p (m h e) -> p m h e", m=M, h=8)
                for h in range(8):
                    b = h % 2
                    if h >= 2:
                        c.wait("logits_read")
                    for m in range(M):
                        n = (m + 1) * P
                        pe.matmul(ps[:, b, m * S:m * S + n], qT[:, h, m * P:(m + 1) * P], kT[:, h, 0:n],
                                  start=True, stop=False)
                        last = pe.matmul(ps[:, b, m * S:m * S + n], ident[0:24, 16 + h:17 + h].broadcast_to([24, P]),
                                         SCUMTN[:, 0:n], start=False, stop=True)
                    last.then_inc(sem["qk_done"], 1)
                    if h >= 1:
                        fox_out(h - 1, v)
                fox_out(7, v)
                c.wait("logits_read", 2)
                c.wait("fox_read")
                transpose_split(V(10240, 2048).rearrange("p (m d) -> p m d", m=M), KD, 0, drain=False)
                gemm(2 * D, (512,) * 2, ("evac_dve",) * 2, order=[8 + i for i in range(8)] + list(range(8)))

            def ssd_out(h, Xd):
                c.wait("ssd_mask")
                E = V(6144 + 512 * (h % 2), 384)
                q = h % 8
                for im in range(M):
                    dst = ps[:, 2 + im, q * 64:(q + 1) * 64]
                    if h == 8 and im == 0:
                        c.wait("out_read")
                    pe.matmul(dst, E[:, im * P:(im + 1) * P], Xd[:, 0, h, :], start=True, stop=(im == 0))
                    if im:
                        last = pe.matmul(dst, E[:, 2 * P:3 * P], Xd[:, 1, h, :], start=False, stop=True)
                last.then_inc(sem["ssd_done"], 1)

            def fox_out(h, v):
                c.wait("probs_ready")
                pr = V(12288 + 512 * (h % 2), 384)
                if h >= 1:
                    c.wait("fox_read")
                for i in range(3):
                    last = pe.transpose(ps[:, 2, i * P:(i + 1) * P], pr[:, i * P:(i + 1) * P], ident)
                last.then_inc(sem["probs_t"], 1)
                c.wait("probs_t_read")
                pT = V(13312, 384)
                pe.matmul(ps[:, 3, 0:P], pT[:, 0:P], v[:, 0, h, :], start=True, stop=True)
                pe.matmul(ps[:, 3, P:2 * P], pT[:, P:2 * P], v[:, 0, h, :], start=True, stop=False)
                last = pe.matmul(ps[:, 3, P:2 * P], pT[:, 2 * P:3 * P], v[:, 1, h, :], start=False, stop=True)
                last.then_inc(sem["fox_done"], 1)

            def recurrent():
                features_of_x()
                gemm(D, (512,) * 2, ("evac_act",) * 2)
                pe.wait_ge(sem["evac_act"], st.evacs["evac_act"])
                xr = V(0, 2048).rearrange("p (m f) -> p m f", m=M)
                for g in range(4):
                    for j in range(2):
                        for m in range(M):
                            last = pe.transpose(ps[:, g, (2 * j + m) * P:(2 * j + m + 1) * P],
                                                xr[:, m, (2 * g + j) * P:(2 * g + j + 1) * P], ident)
                    last.then_inc(sem["conv_tr"], 1)
                prepare(6)
                prepare(6)
                c.wait("conv_read", 4)
                pe.wait_ge(sem["mix_landed"], 16 * (DEPTH + 1))
                xT = V(4096, 2048).rearrange("p (n s) -> p n s", n=8)
                for t in range(2):
                    wt = V(11776 + 1024 * t).rearrange("p (n k) -> p n k", n=8)
                    for n in range(8):
                        last = pe.matmul(ps[:, n // 2, (n % 2) * S:(n % 2 + 1) * S], wt[:, n, :], xT[:, n, :],
                                         start=True, stop=True)
                    last.then_inc(sem["lin_done"], 1)
                    prepare(2)
                    c.wait("r_ready")
                pe.wait_ge(sem["evac_act"], st.evacs["evac_act"])
                gt = V(2048, 2048).rearrange("p (m f) -> p m f", m=M)
                for g in range(4):
                    for j in range(2):
                        for m in range(M):
                            last = pe.transpose(ps[:, g, (2 * j + m) * P:(2 * j + m + 1) * P],
                                                gt[:, m, (2 * g + j) * P:(2 * g + j + 1) * P], ident)
                last.then_inc(sem["gt_done"], 1)
                for k in range(KD):
                    group_of[k] = groups["made"] + 1 + k // 4
                groups["made"] += 2
                gemm(D, (512,) * 2, ("evac_dve",) * 2)

            pe.wait_ge(sem["ident_landed"], 16)
            for l in range(DEPTH):
                features_of_x()
                gdn()
                retention()
                merge_out(l)
            ffn()
            hybrid()
            ffn()
            ffn()
            recurrent()
            ffn()

        @block.scalar
        def _(act):
            c = Counter(act, sem, "act_step")
            st = Stream()

            def pump(to):
                while st.split < min(to, NU):
                    u = st.split
                    slot = u % SPLIT_SLOTS
                    act.wait_ge(weight_landed[u % RAW_SLOTS], 16 * (u // RAW_SLOTS + 1))
                    if u >= SPLIT_SLOTS:
                        act.wait_ge(sem["unit_used"], u - SPLIT_SLOTS + 1)
                    act.activation(wh[:, slot, :], raw[:, u % RAW_SLOTS, :], ACT.Copy).then_inc(sem["split_high"], 1)
                    st.split += 1

            def gemm(rows_, widths, evacs, read=None):
                for i, (w, by) in enumerate(zip(widths, evacs)):
                    st.used += len(units_of(rows_, w))
                    pump(st.used + 2)
                    if by == "evac_act":
                        act.wait_ge(sem["unit_used"], st.used)
                        read(i, 2 * (st.block % 2), w).then_inc(sem["evac_act"], 1)
                    st.evacs[by] += 1
                    st.block += 1
                pump(st.used + 3)

            prepared, plan = [0], []

            def plan_blocks(blocks):
                prepared[0] = 0
                plan[:] = blocks

            def prepare(n):
                before = prepared[0] // 4
                prepared[0] += n
                st.used += prepared[0] // 4 - before
                pump(st.used + 2)
                if prepared[0] // KD > before // 2:
                    first, second, f = plan[before // 2]
                    act.wait_ge(sem["unit_used"], st.used - (prepared[0] // 4) % 2)
                    pair = 2 * (st.block % 2)
                    c.step(act.activation(first, pg[:, pair, :], f, scale=RS[:, 0:1]))
                    act.activation(second, pg[:, pair + 1, :], f, scale=RS[:, 1:2])\
                       .then_inc(sem["evac_act"], 1)
                    st.evacs["evac_act"] += 1
                    st.block += 1

            made = [0]

            def split_groups(gs, dst, gain=None):
                for g in gs:
                    bank = made[0] % 4
                    made[0] += 1
                    c.wait("tr_done")
                    if gain is None:
                        last = act.activation(hTh[:, dst + 2 * g:dst + 2 * g + 2, :],
                                              ps[:, bank, :].rearrange("p (k s) -> p k s", k=2), ACT.Copy)
                    else:
                        for j in range(2):
                            k = 2 * g + j
                            last = act.activation(hTh[:, dst + k, :], ps[:, bank, j * S:(j + 1) * S], ACT.Copy,
                                                  scale=gain(k))
                    last.then_inc(sem["tr_high"], 1)

            def transpose_split(chunks, dst, gain=None):
                split_groups(range(chunks // 2), dst, gain)

            def features_of_x(gain, dst=0):
                for b in range(2):
                    c.wait("x_ready")
                    for m in range(M):
                        last = act.activation(xn[:, 0:512], x[:, m, 512 * b:512 * b + 512], ACT.Square,
                                              accum_out=SX4[:, 2 * b + m:2 * b + m + 1])
                        if 2 * b + m < 3:
                            c.step(last)
                    if b:
                        last.then_inc(sem["x_squares"], 1)
                    split_groups((2 * b, 2 * b + 1), dst, gain)
                pump(st.used + 3)
                c.wait("rs_ready")

            def small_w(n, name):
                act.activation(swh[:, 0:KD * n], name[:, 0:KD * n], ACT.Copy).then_inc(sem["small_w_high"], 1)

            def read_pair(dst, pair, f, w=512):
                c.step(act.activation(dst[:, 0, :], pg[:, pair, 0:w], f, scale=RS[:, 0:1]))
                return act.activation(dst[:, 1, :], pg[:, pair + 1, 0:w], f, scale=RS[:, 1:2])

            def tiles(ap):
                return ap.rearrange("p (m d) -> p m d", m=M)

            def gdn():
                def read(i, pair, w):
                    d3 = rawp[i].rearrange("p (m d) -> p m d", m=M)
                    return read_pair(d3, pair, ACT.Copy)
                gemm(D, (512,) * 3, ("evac_act",) * 3, read)
                plan_blocks(DELTA_BLOCKS)
                c.wait("gate_abs")
                c.step(act.activation(SPL, ABS, ACT.Exp, scale=-1.0))
                c.step(act.activation(NEGA, fp("a_log"), ACT.Exp))
                c.step(act.activation(SMR, QS, ACT.Exp, scale=-1.0))
                act.activation(SPL, SPL, ACT.Ln, bias=1.0).then_inc(sem["gate_exp"], 1)
                for t in range(3):
                    c.wait("conv_read")
                    act.activation(cvp[t], cvp[t], ACT.Silu).then_inc(sem["conv_act"], 1)
                    if t == 1:
                        prepare(3)
                prepare(5)
                for t in range(2):
                    c.wait("back_tr")
                    if t:
                        c.wait("sq_free")
                    for m in range(M):
                        last = act.activation(sq[:, 512 * m:512 * m + 512], ps[:, 2 * t + m, :], ACT.Square)
                    last.then_inc(sem["sq_ready"], 1)
                prepare(3)
                c.wait("back_tr")
                for t in range(4):
                    for d in range(2):
                        m, r = scan_chunk(t, d)
                        last = act.activation(VS[half(r), t, :], ps[half(r), m, :], ACT.Copy)
                last.then_inc(sem["back_read"], 1)
                prepare(3)
                c.wait("sq_free")
                for t, dst in enumerate((qnT, knT)):
                    c.wait("feat_tr")
                    c.step(act.activation(dst[:, 0:512], ps[:, 2 * t, :], ACT.Copy))
                    act.activation(dst[:, 512:1024], ps[:, 2 * t + 1, :], ACT.Copy).then_inc(sem["feat_read"], 1)
                for n in (2, 1, 1):
                    prepare(n)
                c.wait("row_done")
                c.wait("dist_ready")
                act.activation(XT_, X_, ACT.Relu, scale=-1.0)
                c.step(act.activation(Lm, X_, ACT.Relu))
                act.activation(X_, Lm, ACT.Exp, scale=-1.0).then_inc(sem["decay_ready"], 1)
                act.activation(LT, XT_, ACT.Exp, scale=-1.0).then_inc(sem["decay_ready"], 1)
                prepare(4)
                for t in range(4):
                    for d in range(2):
                        m, r = scan_chunk(t, d)
                        o = 8 * m + 4 * d
                        act.activation(EGS[half(r), 4 * t:4 * t + 4], GC[half(r), o:o + 4], ACT.Exp)
                        act.activation(EKS[half(r), 4 * t:4 * t + 4], EKD[half(r), o:o + 4], ACT.Exp)
                c.sig(act.activation(EGL, GL, ACT.Exp), "cum_exp")
                c.step(act.activation(E8, fp("decay"), ACT.Abs))
                c.step(act.activation(E8, E8, ACT.Exp, scale=-1.0))
                act.activation(LAM, E8, ACT.Ln, bias=1.0).then_inc(sem["lam_ready"], 1)
                c.wait("low_t")
                c.wait("sc_masked")
                for d in range(2):
                    act.activation(LT[:, 512 * d:512 * d + 512], ps[:, 2 + d, :], ACT.Copy).then_inc(sem["low_t_read"], 1)
                prepare(4)
                act.activation(DELTA_Z, DELTA_Z, ACT.Silu).then_inc(sem["delta_z_ready"], 1)
                for level in range(5):
                    prepare(1)
                    prepare(1)
                    if level == 2:
                        c.wait("mask_arg")
                        act.activation(MASKS, MASKS, ACT.Exp).then_inc(sem["mask_ready"], 1)
                for _ in range(3):
                    prepare(1)
                for t in range(1, 4):
                    c.wait("qs_done")
                    for h in range(NH):
                        last = act.activation(OT[:, h * P:(h + 1) * P], ps[:, 1, h * P:(h + 1) * P], ACT.Copy,
                                              scale=EGS[:, 4 * t + h:4 * t + h + 1])
                    last.then_inc(sem["ot_ready"], 1)
                    if t < 3:
                        for d in range(2):
                            m, r = scan_chunk(t, d)
                            for h in range(NH):
                                j = 4 * d + h
                                e = 8 * (2 * m + r) + j
                                last = act.activation(STATE[:, j * P:(j + 1) * P], STATE[:, j * P:(j + 1) * P], ACT.Copy,
                                                      scale=EGL[:, e:e + 1])
                        last.then_inc(sem["state_scaled"], 1)
                    for _ in range(4 if t < 3 else 3):
                        prepare(1)
                c.wait("o_ready", 4)
                act.activation(Lm, o_acc, ACT.Square).then_inc(sem["sq_done"], 1)

            def retention():
                prepare(PREPARE_AFTER_SCAN)
                for t, dst in enumerate((V(3072), V(2048))):
                    c.wait("feat_tr")
                    scale = 1.0 if t == 0 else HD ** -0.5
                    c.step(act.activation(dst[:, 0:512], ps[:, 2 * t, :], ACT.Copy, scale=scale))
                    act.activation(dst[:, 512:1024], ps[:, 2 * t + 1, :], ACT.Copy, scale=scale)\
                       .then_inc(sem["feat_read"], 1)
                prepare(4)
                transpose_split(NH, 8, lambda k: fp("gdn_g"))
                prepare(4)

            def merge_out():
                def read_gates(n, first=0):
                    def read(i, pair, w):
                        g = V(2048 + 2048 * (n % 2), 2048).rearrange("p (m d) -> p m d", m=M)
                        o = 512 * (first + i)
                        return read_pair(g[:, :, o:o + 512], pair, ACT.Sigmoid)
                    return read
                gemm(D, (512,) * 2, ("evac_act",) * 2, read_gates(0))
                gemm(D, (512,), ("evac_act",), read_gates(1))
                transpose_split(NH, 12, lambda k: fp("ret_g")[:, k:k + 1])
                transpose_split(NH, 16)
                gemm(D, (512,), ("evac_act",), read_gates(1, 1))
                gemm(BW, (512,) * 2, ("evac_dve",) * 2)
                first_used = st.evacs["evac_dve"]
                gemm(BW, (512,) * 2, ("evac_dve",) * 2)
                act.wait_ge(sem["evac_dve"], first_used)
                gemm(D, (512,) * 2, ("evac_act",) * 2, read_gates(2))
                gemm(BW, (512,) * 2, ("evac_dve",) * 2)
                transpose_split(KD, 0)
                gemm(D, (512,) * 2, ("evac_dve",) * 2)

            def product_squares(i, pair):
                act.wait_ge(sem["unit_used"], st.used)
                for m in range(M):
                    last = act.activation(V(0, 512), pg[:, pair + m, :], ACT.Square,
                                          accum_out=SS4[:, 2 * i + m:2 * i + m + 1])
                    c.sig(last, "product_sq")

            def gemm_out(rows_, between=None):
                for i in range(2):
                    for n in range(len(units_of(rows_, 512))):
                        st.used += 1
                        if between and i == 0 and n == 1:
                            pump(st.used + 2)
                            between()
                    pump(st.used + 2)
                    product_squares(i, 2 * (st.block % 2))
                    st.evacs["evac_dve"] += 1
                    st.block += 1
                pump(st.used + 3)

            def ffn(name):
                features_of_x(lambda k: name[:, k:k + 1], X_AT)
                hid = V(0, 2 * FF).rearrange("p (m f) -> p m f", m=M)
                at_ = 0
                for j, w in enumerate(FF_WIDTHS):
                    gemm(D, (w, w), ("evac_act", "evac_dve"),
                         lambda i, pair, w: read_pair(hid[:, :, at_:at_ + w], pair, ACT.Silu, w))
                    at_ += w
                    if j:
                        split_groups([g for g in EARLY if g // 2 == j - 1], 0)
                gemm_out(FF, lambda: split_groups(LATE, 0))

            def hybrid():
                features_of_x(lambda k: spar("g2")[:, k:k + 1])
                z = V(10240, 2048).rearrange("p (m f) -> p m f", m=M)
                raw3 = V(0, 3072).rearrange("p (m f) -> p m f", m=M)

                def read(i, pair, w):
                    if i < 2:
                        dst, f = z[:, :, 512 * i:512 * i + 512], ACT.Silu
                    else:
                        dst, f = raw3[:, :, 512 * (i - 2):512 * (i - 2) + 512], ACT.Copy
                    return read_pair(dst, pair, f)
                gemm(D, (512,) * 5, ("evac_act",) * 5, read)
                plan_blocks(FOX_BLOCKS)
                c.wait("gate_abs")
                c.step(act.activation(SEXP, SEXP, ACT.Exp, scale=-1.0))
                c.step(act.activation(SNEGA[:, 0:16], spar("a_log"), ACT.Exp))
                act.activation(SEXP, SEXP, ACT.Ln, bias=1.0).then_inc(sem["gate_exp"], 1)
                for n in (3, 7, 7):
                    prepare(n)
                c.wait("conv_read", 6)
                act.activation(V(3072, 3072), V(3072, 3072), ACT.Silu).then_inc(sem["conv_act"], 1)
                c.wait("back_tr")
                xs = V(8192, 2048)
                for b in range(4):
                    last = act.activation(xs[:, 512 * b:512 * b + 512], ps[:, b, :], ACT.Copy)
                    if b < 3:
                        c.step(last)
                last.then_inc(sem["back_read"], 1)
                for n in (2, 1, 1, 2):
                    prepare(n)
                c.wait("cb_ready")
                for h in range(16):
                    c.wait("row_done")
                    if h >= 2:
                        c.wait("ssd_done")
                    E = V(6144 + 512 * (h % 2), 384)
                    act.activation(E[:, 0:S], ps[:, h % 2, 0:S], ACT.Relu, scale=-1.0, bias=SCUM[:, h:h + 1])
                    c.step(act.activation(E[:, S:S + P], ps[:, h % 2, P:S], ACT.Relu, scale=-1.0,
                                          bias=SCUM[:, 24 + h:25 + h]))
                    act.activation(E, E, ACT.Exp, scale=-1.0).then_inc(sem["ssd_decay"], 1)
                    prepare(1)
                c.wait("ssd_done", 2)
                prepare(4)
                c.wait("o_sq")
                for m in range(M):
                    for g in range(2):
                        last = act.activation(V(6144, 512),
                                              xs[:, 512 * (2 * m + g):512 * (2 * m + g) + 512], ACT.Square,
                                              accum_out=SS4[:, 2 * m + g:2 * m + g + 1])
                        if (m, g) != (1, 1):
                            c.step(last)
                last.then_inc(sem["sq_done"], 1)
                prepare(5)
                transpose_split(KD, 8, lambda k: spar("norm_g")[:, k:k + 1])
                for t, o in enumerate((6144, 8192)):
                    for g in range(4):
                        c.wait("feat_tr")
                        act.activation(V(o + 512 * g, 512), ps[:, g, :], ACT.Copy,
                                       scale=HD ** -0.5 if t == 0 else 1.0).then_inc(sem["feat_read"], 1)
                for h in range(8):
                    c.wait("logits_ready")
                    pr = V(12288 + 512 * (h % 2), 384)
                    c.step(act.activation(pr[:, 0:P], pr[:, 0:P], ACT.Exp, bias=NMAX[:, 2 * h:2 * h + 1],
                                          accum_out=RSUM[:, 2 * h:2 * h + 1]))
                    act.activation(pr[:, P:3 * P], pr[:, P:3 * P], ACT.Exp, bias=NMAX[:, 2 * h + 1:2 * h + 2],
                                   accum_out=RSUM[:, 2 * h + 1:2 * h + 2]).then_inc(sem["probs_ready"], 1)
                    c.wait("probs_t")
                    if h >= 1:
                        c.wait("fox_done")
                    act.activation(V(13312, 384), ps[:, 2, 0:3 * P], ACT.Copy).then_inc(sem["probs_t_read"], 1)
                c.wait("fox_done")
                transpose_split(KD, 0)
                gemm_out(2 * D)

            def recurrent():
                features_of_x(lambda k: rp("g2")[:, k:k + 1])

                def read(i, pair, w):
                    return read_pair(V(0, 2048).rearrange("p (m f) -> p m f", m=M)[:, :, 512 * i:512 * i + 512], pair,
                                     ACT.Copy)
                gemm(D, (512,) * 2, ("evac_act",) * 2, read)
                plan_blocks(REC_BLOCKS)
                c.step(act.activation(E8, rp("lam"), ACT.Abs))
                c.step(act.activation(E8, E8, ACT.Exp, scale=-1.0))
                act.activation(LAM, E8, ACT.Ln, bias=1.0).then_inc(sem["lam_ready"], 1)
                prepare(6)
                prepare(6)
                for t in range(2):
                    c.wait("lin_done")
                    dst = V(6144 + 2048 * t, 2048).rearrange("p (n s) -> p n s", n=8)
                    for n in range(8):
                        last = act.activation(dst[:, n, :], ps[:, n // 2, (n % 2) * S:(n % 2 + 1) * S], ACT.Sigmoid,
                                              bias=rp("b_a" if t == 0 else "b_x")[:, n:n + 1])
                    last.then_inc(sem["r_ready"], 1)
                    if t == 0:
                        prepare(2)
                c.wait("a_ready")
                c.step(act.activation(V(10240, 2048), V(6144, 2048), ACT.Tanh))
                for i in range(2):
                    act.activation(V(6144 + 1024 * i), V(6144 + 1024 * i), ACT.Exp).then_inc(sem["u_ready"], 1)
                prepare(2)
                for i in range(2):
                    c.wait("u_sqrt")
                    a2 = V(10240 + 1024 * i)
                    act.activation(a2, a2, ACT.Sqrt, scale=-1.0).then_inc(sem["h_ready"], 1)
                for i in range(2):
                    c.wait("rec_out")
                    act.activation(hTh[:, 4 * i:4 * i + 4, :], V(8192 + 1024 * i).rearrange("p (n s) -> p n s", n=4),
                                   ACT.Copy).then_inc(sem["tr_high"], 1)
                made[0] += 2
                gemm_out(D)

            for l in range(DEPTH):
                act.wait_ge(sem["params_landed" if l else "first_params_landed"], 16 * max(l, 1))
                features_of_x(lambda k: fp("norm_g")[:, k:k + 1])
                small_w(16, fp("small_w"))
                gdn()
                retention()
                merge_out()
            act.wait_ge(sem["params_landed"], 16 * 2)
            small_w(24, spar("small_w"))
            ffn(spar("g0"))
            hybrid()
            ffn(spar("g4"))
            act.wait_ge(sem["params_landed"], 16 * 3)
            ffn(rp("g0"))
            recurrent()
            ffn(rp("g4"))

        @block.vector
        def _(dve):
            c = Counter(dve, sem, "dve_step")
            st = Stream()
            tt, ts, stt = dve.tensor_tensor, dve.tensor_scalar, dve.scalar_tensor_tensor

            def pump(to):
                while st.split < min(to, NU):
                    u = st.split
                    slot = u % SPLIT_SLOTS
                    dve.wait_ge(sem["split_high"], u + 1)
                    tt(wl[:, slot, :], raw[:, u % RAW_SLOTS, :], wh[:, slot, :], ALU.subtract)\
                        .then_inc(sem["split_low"], 1)
                    st.split += 1

            def gemm(rows_, widths, evacs, read=None):
                for i, (w, by) in enumerate(zip(widths, evacs)):
                    st.used += len(units_of(rows_, w))
                    pump(st.used + 2)
                    if by == "evac_dve":
                        if read is not None:
                            dve.wait_ge(sem["unit_used"], st.used)
                            last = read(i, 2 * (st.block % 2), w)
                            if last is not None:
                                c.sig(last, "evac_dve")
                    st.evacs[by] += 1
                    st.block += 1
                pump(st.used + 3)

            prepared = [0]

            def prepare(n):
                before = prepared[0]
                prepared[0] += n
                st.used += prepared[0] // 4 - before // 4
                pump(st.used + 2)
                if prepared[0] // KD > before // KD:
                    st.evacs["evac_act"] += 1
                    st.block += 1

            made = [0]

            def split_groups(gs, dst, gain=None):
                for g in gs:
                    bank = made[0] % 4
                    made[0] += 1
                    c.wait("tr_high")
                    if gain is None:
                        h = slice(dst + 2 * g, dst + 2 * g + 2)
                        last = tt(hTl[:, h, :], ps[:, bank, :].rearrange("p (k s) -> p k s", k=2), hTh[:, h, :],
                                  ALU.subtract)
                    else:
                        for j in range(2):
                            k = 2 * g + j
                            last = stt(hTl[:, dst + k, :], ps[:, bank, j * S:(j + 1) * S], gain(k), hTh[:, dst + k, :],
                                       ALU.mult, ALU.subtract)
                    last.then_inc(sem["tr_low"], 1)

            def transpose_split(chunks, dst, gain=None):
                split_groups(range(chunks // 2), dst, gain)

            def features_of_x(gain, dst=0):
                split_groups(range(KD // 2), dst, gain)
                pump(st.used + 3)
                c.wait("x_squares")
                c.step(tt(RS, SX4[:, 0:2], SX4[:, 2:4], ALU.add))
                rstd_of(RS, D, "rs_ready")

            def small_w(n, name):
                c.wait("small_w_high")
                tt(swl[:, 0:KD * n], name[:, 0:KD * n], swh[:, 0:KD * n], ALU.subtract).then_inc(sem["small_w_low"], 1)

            def rstd_of(ss, n, done="dve_step"):
                w = ss.shape[1]
                y, t, h = NEWTON[:, 0:w], NEWTON[:, 16:16 + w], NEWTON[:, 32:32 + w]
                c.step(ts(ss, ss, 1.0 / n, EPS, ALU.mult, ALU.add))
                ts(h, ss, -0.5, None, ALU.mult)
                c.step(ts(y.bitcast(I32), ss.bitcast(I32), 1, None, ALU.logical_shift_right))
                c.step(ts(y.bitcast(I32), y.bitcast(I32), -1.0, float(0x5F3759DF), ALU.mult, ALU.add))
                for i in range(3):
                    c.step(tt(t, y, y, ALU.mult))
                    c.step(tt(t, t, h, ALU.mult))
                    c.sig(stt(ss if i == 2 else y, t, 1.5, y, ALU.add, ALU.mult), done if i == 2 else "dve_step")

            XN = xn[:, :].rearrange("p (m d) -> p m d", m=M)

            def head_rstd(src, n, dst):
                c.step(dve.tensor_reduce(dst, src.rearrange("p (k e) -> p k e", e=HD), AX.X, ALU.add))
                rstd_of(dst, n)

            ret_qk_read = [0]

            def retention_masks(l, hs):
                dve.wait_ge(sem["dist_landed"], 16 * (l + 1))
                RD = DIST.rearrange("p (s n) -> p s n", s=2)
                for h in hs:
                    last = ts(MASKS[:, 512 * h:512 * h + 512], RD[:, 0, :], LAM[:, h:h + 1], None, ALU.mult)
                c.step(last)
                for h in hs:
                    mk = MASKS[:, 512 * h:512 * h + 512]
                    last = stt(mk, RD[:, 1, :], LAM[:, 4 + h:5 + h], mk, ALU.mult, ALU.add)
                if NH - 1 in hs:
                    last.then_inc(sem["mask_arg"], 1)

            def gdn(l):
                gemm(D, (512,) * 3, ("evac_act",) * 3)
                ret_qk_read[0] = st.evacs["evac_act"] + 3
                c.wait("small_done")
                for m in range(M):
                    src = ps[:, m, 0:16].rearrange("p (d t h) -> p d t h", d=2, t=2)
                    ts(QS[:, 8 * m:8 * m + 8].rearrange("p (d h) -> p d h", d=2), src[:, :, 1, :], RS[:, m:m + 1], None,
                       ALU.mult)
                    last = stt(TOT[:, 8 * m:8 * m + 8].rearrange("p (d h) -> p d h", d=2), src[:, :, 0, :],
                               RS[:, m:m + 1], fp("dtb").rearrange("p (d h) -> p d h", d=2), ALU.mult, ALU.add)
                c.sig(last, "small_read")
                stt(ABS, TOT, -1.0, TOT, ALU.mult, ALU.max).then_inc(sem["gate_abs"], 1)
                w = fp("conv")
                for t in range(3):
                    c.wait("conv_tr")
                    acc = cvp[t].rearrange("p (h s) -> p h s", h=NH)
                    src = [ps[:, 2 * (t % 2) + h // 2, (h % 2) * S:(h % 2 + 1) * S] for h in range(NH)]
                    k = 4 * t
                    for h in range(NH):
                        last = ts(acc[:, h, :], src[h], w[:, 12 + k + h:13 + k + h], None, ALU.mult)
                    c.step(last)
                    for h in range(NH):
                        last = stt(acc[:, h, 1:S], src[h][:, 0:S - 1], w[:, k + h:k + h + 1], acc[:, h, 1:S],
                                   ALU.mult, ALU.add)
                    c.step(last)
                    for h in range(NH):
                        last = stt(acc[:, h, 0:S - 1], src[h][:, 1:S], w[:, 24 + k + h:25 + k + h], acc[:, h, 0:S - 1],
                                   ALU.mult, ALU.add)
                    c.sig(last, "conv_read")
                prepare(3)
                c.wait("gate_exp")
                c.step(stt(SPL, TOT, 0.0, SPL, ALU.max, ALU.add))
                c.step(ts(SMR, SMR, 1.0, None, ALU.add))
                c.step(dve.reciprocal(BETA, SMR))
                c.sig(stt(GLOG.rearrange("p (m k) -> p m k", m=M), SPL.rearrange("p (m k) -> p m k", m=M), -1.0,
                          times(NEGA, M), ALU.mult, ALU.mult), "gate_g")
                for t, dst in enumerate((qn, kn)):
                    c.wait("sq_ready")
                    c.sig(dve.tensor_reduce(STATS, sq.rearrange("p (k e) -> p k e", e=HD), AX.X, ALU.add), "sq_free")
                    rstd_of(STATS, 1.0)
                    if t == 0:
                        c.step(ts(STATS, STATS, HD ** -0.5, None, ALU.mult))
                    src = ps[:, 2 * t:2 * t + 2, :].rearrange("p m (h e) -> p (m h) e", h=NH)
                    c.sig(tt(heads(dst, 8), src, over(STATS, HD), ALU.mult), "qk_ready")
                    if t == 0:
                        prepare(5)
                for n in (3, 3):
                    prepare(n)
                c.wait("cum_done")
                c.step(dve.tensor_copy(GC, ps[:, 0, 0:16]))
                dve.tensor_copy(GCJ.rearrange("p (j m) -> p j m", m=M), GC.rearrange("p (m j) -> p j m", m=M))
                tt(EKD, ps[:, 0, 16:32], GC, ALU.subtract)
                c.sig(dve.tensor_copy(GL, ps[:, 0, 32:64]), "cum_read")
                prepare(2)
                prepare(1)
                c.wait("cum_t")
                c.sig(dve.tensor_copy(GCT, ps[0:8, 1, 0:S]), "cum_t_read")
                prepare(1)
                dve.wait_ge(sem["const_landed"], 16)
                X3, XT3, T3, L3, LT3 = (v.rearrange("p (q f) -> p q f", f=CHUNK) for v in (X_, XT_, TM_, Lm, LT))
                SC3, LM3, TB3 = (v.rearrange("p (q f) -> p q f", f=CHUNK) for v in (SC_, LMASK, TB))
                both = (slice(0, 8), slice(8, 16))
                c.step(dve.tensor_copy(BETAJ.rearrange("p (j m) -> p j m", m=M), BETA.rearrange("p (m j) -> p j m", m=M)))
                for d, js in enumerate(both):
                    tt(LM3[:, js, :], times(MASK["los" if d == 0 else "ups"], 8), over(BETAJ[:, js], CHUNK), ALU.mult)
                c.wait("row_done")
                tt(X3, ps[:, 2:4, :].rearrange("p b (q f) -> p (b q) f", f=CHUNK), over(GCJ, CHUNK),
                   ALU.subtract).then_inc(sem["dist_ready"], 1)
                c.wait("decay_ready")
                c.step(tt(X_, X_, LMASK, ALU.mult))
                c.wait("gram_done")
                for d, js in enumerate(both):
                    last = tt(L3[:, js, :], X3[:, js, :], ps[:, 0, :].rearrange("p (q f) -> p q f", f=CHUNK), ALU.mult)
                c.sig(last, "low_ready")
                prepare(4)
                c.wait("decay_ready")
                for d, js in enumerate(both):
                    last = tt(SC3[:, js, :], LT3[:, js, :], times(MASK["up" if d == 0 else "lo"], 8), ALU.mult)
                c.sig(last, "sc_masked")
                c.wait("gram_done")
                for d, js in enumerate(both):
                    last = tt(SC3[:, js, :], SC3[:, js, :], ps[:, 1, :].rearrange("p (q f) -> p q f", f=CHUNK), ALU.mult)
                c.step(last)
                for d, js in enumerate(both):
                    A, AT = (L3, LT3) if d == 0 else (LT3, L3)
                    if d == 0:
                        c.wait("low_t_read", 2)
                    tt(X3[:, js, :], A[:, js, :], times(MASK["nlo1"], 8), ALU.mult)
                    c.step(tt(XT3[:, js, :], AT[:, js, :], times(MASK["nup1"], 8), ALU.mult))
                    tt(X3[:, js, :], X3[:, js, :], times(MASK["eye"], 8), ALU.add)
                    c.sig(tt(XT3[:, js, :], XT3[:, js, :], times(MASK["eye"], 8), ALU.add), "inv_x")
                prepare(4)
                for s in (2, 4, 8, 16, 32):
                    for d, js in enumerate(both):
                        c.wait("inv_t")
                        c.sig(tt(T3[:, js, :], ps[:, d, :].rearrange("p (q f) -> p q f", f=CHUNK),
                                 times(MASK[f"nlo{s}"], 8), ALU.mult), "inv_tm")
                    prepare(1)
                    for d, js in enumerate(both):
                        if s < 32 or d == 1:
                            c.wait("inv_y")
                            last = tt(X3[:, js, :], X3[:, js, :], ps[:, 2 + d, :].rearrange("p (q f) -> p q f", f=CHUNK),
                                      ALU.add)
                        if s < 32 or d == 0:
                            c.wait("inv_yt")
                            last = tt(XT3[:, js, :], XT3[:, js, :], ps[:, d, :].rearrange("p (q f) -> p q f", f=CHUNK),
                                      ALU.add)
                        c.sig(last, "inv_x") if s < 32 else c.step(last)
                    if s < 32:
                        prepare(1)
                    if s == 2:
                        log_sigmoid(fp("decay"))
                    if s in (4, 8):
                        retention_masks(l, (0, 1) if s == 4 else (2, 3))
                tt(TB3[:, both[0], :], XT3[:, both[0], :], over(BETAJ[:, 0:8], CHUNK), ALU.mult)
                c.sig(tt(TB3[:, both[1], :], X3[:, both[1], :], over(BETAJ[:, 8:16], CHUNK), ALU.mult), "inv_scaled")
                prepare(1)
                c.wait("cum_exp")
                c.step(ts(NEGS, EGS, -1.0, None, ALU.mult))
                O3 = o_acc.rearrange("p (m e) -> p m e", m=M)
                for t in range(4):
                    if t:
                        c.wait("ws_done")
                        for h in range(NH):
                            last = stt(RV[:, h * P:(h + 1) * P], ps[:, 0, h * P:(h + 1) * P],
                                       NEGS[:, 4 * t + h:4 * t + h + 1], VS[:, t, h * P:(h + 1) * P], ALU.mult, ALU.add)
                        last.then_inc(sem["rv_ready"], 1)
                    c.wait("uw_done")
                    if t < 3:
                        tt(heads(VD), heads(ps[:, 0, :]), over(EKS[:, 4 * t:4 * t + 4], P),
                           ALU.mult).then_inc(sem["vd_ready"], 1)
                    dve.tensor_copy(VN, ps[:, 0, :]).then_inc(sem["vn_ready"], 1)
                    for _ in range(2 if t else 1):
                        prepare(1)
                    if t:
                        c.wait("ot_ready")
                    if t >= 2:
                        for d in range(2):
                            m, r = scan_chunk(t, d)
                            last = tt(OT[half(r), :], OT[half(r), :], O3[half(r), m, :], ALU.add)
                        c.step(last)
                    if t < 3:
                        c.wait("kv_done")
                        src = ps[:, 2:4, :].rearrange("p b n -> p (b n)")
                        if t == 0:
                            last = dve.tensor_copy(STATE, src)
                        else:
                            c.wait("state_scaled")
                            last = tt(STATE, STATE, src, ALU.add)
                        c.sig(last, "state_ready")
                        prepare(1)
                    c.wait("sv_done")
                    for d in range(2):
                        m, r = scan_chunk(t, d)
                        if t == 0:
                            last = dve.tensor_copy(O3[half(r), m, :], ps[half(r), 1, :])
                        else:
                            last = tt(O3[half(r), m, :], OT[half(r), :], ps[half(r), 1, :], ALU.add)
                    c.sig(last, "o_ready")
                    prepare(1)

            def rotate(src, dst):
                tmp = V(11264)
                v, d, t = (a.rearrange("p (m h e) -> p m h e", m=M, h=NH) for a in (src, dst, tmp))
                lo, hi = slice(0, 64), slice(64, P)
                for m in range(M):
                    co, si = times(COS[:, m, :], NH), times(SIN[:, m, :], NH)
                    tt(d[:, m, :, lo], v[:, m, :, lo], co, ALU.mult)
                    tt(d[:, m, :, hi], v[:, m, :, hi], co, ALU.mult)
                    tt(t[:, m, :, lo], v[:, m, :, hi], si, ALU.mult)
                    last = tt(t[:, m, :, hi], v[:, m, :, lo], si, ALU.mult)
                c.step(last)
                d, t = (a.rearrange("p (k e) -> p k e", k=8) for a in (dst, tmp))
                tt(d[:, :, lo], d[:, :, lo], t[:, :, lo], ALU.subtract)
                return tt(d[:, :, hi], d[:, :, hi], t[:, :, hi], ALU.add)

            def delta_result():
                dve.wait_ge(sem["evac_act"], ret_qk_read[0])
                c.sig(rotate(RET_Q, V(0)), "rope_done")
                c.sig(rotate(RET_K, V(1024)), "rope_done")
                prepare(PREPARE_AFTER_SCAN)
                c.wait("sq_done")
                head_rstd(Lm, HD, STATS)
                c.wait("delta_z_ready")
                c.step(tt(heads(o_acc, 8), heads(o_acc, 8), over(STATS, HD), ALU.mult))
                tt(o_acc, o_acc, DELTA_Z, ALU.mult).then_inc(sem["y_ready"], 1)
                prepare(4)
                transpose_split(NH, 8, lambda k: fp("gdn_g"))
                prepare(4)

            def log_sigmoid(v):
                c.wait("lam_ready")
                c.step(ts(TMP8, E8, 1.0, None, ALU.add))
                c.step(ts(TMP8, TMP8, -1.0, 1e-30, ALU.add, ALU.max))
                c.step(dve.reciprocal(TMP8, TMP8))
                c.step(tt(TMP8, TMP8, E8, ALU.mult))
                c.step(tt(LAM, LAM, TMP8, ALU.mult))
                c.step(stt(LAM, v, 0.0, LAM, ALU.min, ALU.subtract))

            def retention():
                delta_result()
                c.wait("mask_ready")
                for h in range(NH):
                    c.wait("qk_done")
                    if h >= 2:
                        c.wait("ov_done")
                    c.sig(tt(V(5120 + 512 * (h % 2), 512), ps[:, h % 2, :], MASKS[:, 512 * h:512 * h + 512], ALU.mult), "sc_ready")
                c.wait("ov_done", 2)
                for m in range(M):
                    for h in range(NH):
                        k = 4 * m + h
                        last = dve.bn_stats(BN[:, 6 * k:6 * k + 6], ps[:, 2 + m, h * P:(h + 1) * P])
                c.step(last)
                for k in range(8):
                    last = dve.bn_aggr(MV[:, 2 * k:2 * k + 2], BN[:, 6 * k:6 * k + 6])
                c.step(last)
                mv = MV.rearrange("p (k t) -> p k t", t=2)
                c.step(dve.tensor_copy(STATS, mv[:, :, 1]))
                rstd_of(STATS, 1.0)
                for m in range(M):
                    for h in range(NH):
                        k = 4 * m + h
                        last = ts(V(0)[:, k * P:(k + 1) * P], ps[:, 2 + m, h * P:(h + 1) * P], MV[:, 2 * k:2 * k + 1],
                                  STATS[:, k:k + 1], ALU.subtract, ALU.mult)
                c.step(last)
                for m in range(M):
                    o = slice(512 * m, 512 * m + 512)
                    last = tt(V(0)[:, o], V(0)[:, o], RET_Z[m], ALU.mult)
                last.then_inc(sem["y_ready"], 1)

            def gmlp_values(l):
                dve.wait_ge(sem["evac_act"], st.evacs["evac_act"])
                dve.wait_ge(sem["wide_landed"], 16 * (l + 1))
                v = MLP_V
                for m in range(M):
                    last = dve.bn_stats(BN[:, 6 * m:6 * m + 6], v[:, 512 * m:512 * m + 512])
                c.step(last)
                for m in range(M):
                    last = dve.bn_aggr(MV[:, 2 * m:2 * m + 2], BN[:, 6 * m:6 * m + 6])
                c.step(last)
                c.step(dve.tensor_copy(STATS[:, 0:2], MV.rearrange("p (k t) -> p k t", t=2)[:, 0:2, 1]))
                rstd_of(STATS[:, 0:2], 1.0)
                for m in range(M):
                    last = ts(v[:, 512 * m:512 * m + 512], v[:, 512 * m:512 * m + 512], MV[:, 2 * m:2 * m + 1],
                              STATS[:, m:m + 1], ALU.subtract, ALU.mult)
                c.step(last)
                v2 = v.rearrange("p (m e) -> p m e", m=M)
                c.step(tt(v2, v2, times(LN_GAINS[:, 0:512], M), ALU.mult))
                c.sig(tt(v2, v2, times(LN_GAINS[:, 512:1024], M), ALU.add), "v_ready")
                c.step(tt(MLP_U, MLP_U, MLP_Z, ALU.mult))

            def gmlp():
                c.wait("mix_done")
                for m in range(M):
                    for g in range(NH):
                        o = 512 * m + g * P
                        last = stt(V(1024)[:, o:o + P], ps[:, m, g * P:(g + 1) * P], fp("b_s")[:, g:g + 1],
                                   MLP_U[:, o:o + P], ALU.add, ALU.mult)
                last.then_inc(sem["y_ready"], 1)

            def merge_out(l, last_layer):
                def read_branch(n):
                    def read(i, pair, w):
                        if i == 0:
                            dve.wait_ge(sem["evac_act"], st.evacs["evac_act"])
                        g = V(2048 + 2048 * (n % 2), 2048).rearrange("p (m d) -> p m d", m=M)
                        o = slice(512 * i, 512 * i + 512)
                        dst = V(0 if n == 0 else 6144, 2048).rearrange("p (m d) -> p m d", m=M)
                        last = tt(dst[:, :, o], g[:, :, o], pg[:, pair:pair + 2, :], ALU.mult)
                        if n == 2:
                            c.sig(last, "evac_dve")
                            y = V(0, 2048).rearrange("p (m d) -> p m d", m=M)
                            tt(y[:, :, o], y[:, :, o], dst[:, :, o], ALU.add).then_inc(sem["y_ready"], 1)
                            return None
                        return last
                    return read
                pump(st.used + 4)
                gmlp_values(l)
                gemm(D, (512,) * 2, ("evac_act",) * 2)
                gmlp()
                gemm(D, (512,), ("evac_act",))
                transpose_split(NH, 12, lambda k: fp("ret_g")[:, k:k + 1])
                transpose_split(NH, 16)
                dve.engine_nop().then_inc(sem["params_used"], 1)
                gemm(D, (512,), ("evac_act",))
                gemm(BW, (512,) * 2, ("evac_dve",) * 2, read_branch(0))
                gemm(BW, (512,) * 2, ("evac_dve",) * 2, read_branch(1))
                c.step(tt(V(0, 2048), V(0, 2048), V(6144, 2048), ALU.add))
                gemm(D, (512,) * 2, ("evac_act",) * 2)
                gemm(BW, (512,) * 2, ("evac_dve",) * 2, read_branch(2))
                transpose_split(KD, 0)

                def add(i, pair, w):
                    o = slice(512 * i, 512 * i + 512)
                    last = tt(x[:, :, o], x[:, :, o], pg[:, pair:pair + 2, :], ALU.add)
                    if last_layer:
                        c.step(last)
                        for m in range(M):
                            k = 2 * i + m
                            dve.tensor_tensor_reduce(V(2048 + 512 * k, 512), x[:, m, o], x[:, m, o], 1.0, 0.0, ALU.mult,
                                                     ALU.add, SX4[:, k:k + 1])
                        if i == 0:
                            dve.wait_ge(sem["final_g_landed"], 16)
                        return tt(XN[:, :, o], x[:, :, o], times(V(13824)[:, o], M), ALU.mult)
                    c.sig(last, "x_ready")
                    return dve.engine_nop()
                gemm(D, (512,) * 2, ("evac_dve",) * 2, add)

            posts = [0]
            G = V(13824)

            def gemm_out(rows_, half, between=None):
                for i in range(2):
                    for n in range(len(units_of(rows_, 512))):
                        st.used += 1
                        if between and i == 0 and n == 1:
                            pump(st.used + 2)
                            between()
                    pump(st.used + 2)
                    if i == 0:
                        dve.wait_ge(sem["wide_landed"], 16 * (DEPTH + 1 + posts[0]))
                        posts[0] += 1
                    pair = 2 * (st.block % 2)
                    dve.wait_ge(sem["unit_used"], st.used)
                    o = slice(512 * i, 512 * i + 512)
                    for m in range(M):
                        c.wait("product_sq")
                        last = tt(XN[:, m, o], pg[:, pair + m, :], G[:, o], ALU.mult)
                    c.sig(last, "evac_dve")
                    st.evacs["evac_dve"] += 1
                    st.block += 1
                c.step(tt(SS, SS4[:, 0:2], SS4[:, 2:4], ALU.add))
                rstd_of(SS, D)
                if half != 1.0:
                    c.step(ts(SS, SS, half, None, ALU.mult))
                for b in range(2):
                    o = slice(512 * b, 512 * b + 512)
                    for m in range(M):
                        last = stt(x[:, m, o], XN[:, m, o], SS[:, m:m + 1], x[:, m, o], ALU.mult, ALU.add)
                    c.sig(last, "x_ready")
                pump(st.used + 3)

            def ffn(last_of_block=False):
                features_of_x(gains[0], X_AT)
                if last_of_block:
                    dve.engine_nop().then_inc(sem["params_used"], 1)
                hid = V(0, 2 * FF).rearrange("p (m f) -> p m f", m=M)
                at_ = 0

                def read(i, pair, w):
                    dve.wait_ge(sem["evac_act"], st.evacs["evac_act"])
                    for m in range(M):
                        last = stt(hid[:, m, at_:at_ + w], pg[:, pair + m, 0:w], RS[:, m:m + 1], hid[:, m, at_:at_ + w],
                                   ALU.mult, ALU.mult)
                    return last
                for j, w in enumerate(FF_WIDTHS):
                    gemm(D, (w, w), ("evac_act", "evac_dve"), read)
                    at_ += w
                    if j:
                        split_groups([g for g in EARLY if g // 2 == j - 1], 0)
                gemm_out(FF, 0.5, lambda: split_groups(LATE, 0))

            gains = [None]

            def hybrid():
                features_of_x(lambda k: spar("g2")[:, k:k + 1])
                gemm(D, (512,) * 5, ("evac_act",) * 5)
                c.wait("small_done")
                for m in range(M):
                    o = 24 * m
                    stt(SAB[:, o:o + 16], ps[:, m, 0:16], RS[:, m:m + 1], spar("dtb"), ALU.mult, ALU.add)
                    last = stt(SAB[:, o + 16:o + 24], ps[:, m, 16:24], RS[:, m:m + 1], spar("fox_b"), ALU.mult, ALU.add)
                c.sig(last, "small_read")
                for m in range(M):
                    o = 24 * m
                    last = ts(SAB[:, o + 16:o + 24], SAB[:, o + 16:o + 24], -1.0, None, ALU.mult)
                c.step(last)
                dve.memset(SNEGA[:, 16:24], 1.0)
                stt(SEXP, SAB, -1.0, SAB, ALU.mult, ALU.max).then_inc(sem["gate_abs"], 1)
                w, b = spar("conv"), spar("conv_b")
                cv = V(3072, 3072).rearrange("p (k s) -> p k s", k=12)
                for g in range(6):
                    c.wait("conv_tr")
                    ks = (2 * g, 2 * g + 1)
                    src = {k: ps[:, g % 4, (k % 2) * S:(k % 2 + 1) * S] for k in ks}
                    for k in ks:
                        last = ts(cv[:, k, :], src[k], w[:, 36 + k:37 + k], b[:, k:k + 1], ALU.mult, ALU.add)
                    c.step(last)
                    for tap in (2, 1, 0):
                        sh = 3 - tap
                        for k in ks:
                            last = stt(cv[:, k, sh:S], src[k][:, 0:S - sh], w[:, 12 * tap + k:12 * tap + k + 1],
                                       cv[:, k, sh:S], ALU.mult, ALU.add)
                        if tap:
                            c.step(last)
                    c.sig(last, "conv_read")
                    if g in (1, 3, 5):
                        prepare(3 if g == 1 else 7)
                c.wait("gate_exp")
                c.step(stt(SEXP, SAB, 0.0, SEXP, ALU.max, ALU.add))
                dve.tensor_copy(DT.rearrange("p (m k) -> p m k", m=M), SEXP.rearrange("p (m k) -> p m k", m=M)[:, :, 0:16])
                c.sig(stt(SG.rearrange("p (m k) -> p m k", m=M), SEXP.rearrange("p (m k) -> p m k", m=M), -1.0,
                          times(SNEGA, M), ALU.mult, ALU.mult), "gate_g")
                c.wait("cum_done")
                c.sig(dve.tensor_copy(SCUM, ps[:, 0, 0:48]), "cum_read")
                prepare(2)
                prepare(1)
                c.wait("cum_t")
                c.step(dve.tensor_copy(SCUMT, ps[0:24, 1, 0:S]))
                c.sig(ts(SCUMTN, ps[0:24, 1, 0:S], -1.0, None, ALU.mult), "cum_t_read")
                prepare(1)
                dve.wait_ge(sem["back_read"], DEPTH + 1)
                xs = V(8192, 2048)
                tt(V(0, 2048).rearrange("p (m h e) -> p (m h) e", m=M, h=16), xs.rearrange("p (m h e) -> p (m h) e", m=M, h=16),
                   over(DT, 64), ALU.mult)
                c.wait("gram_done")
                CB = V(7168, 768).rearrange("p (g s) -> p g s", g=2)
                tt(CB[:, :, 0:P], ps[:, 2:4, 0:P], times(C["up128"], 2), ALU.mult)
                dve.tensor_copy(CB[:, :, P:2 * P], ps[:, 2:4, P:2 * P])
                c.sig(tt(CB[:, :, 2 * P:3 * P], ps[:, 2:4, 2 * P:3 * P], times(C["up128"], 2), ALU.mult), "cb_ready")
                prepare(2)
                c.step(tt(xs.rearrange("p (m h e) -> p m h e", m=M, h=16)[:, 0], xs.rearrange("p (m h e) -> p m h e", m=M, h=16)[:, 0],
                          over(spar("d"), 64), ALU.mult))
                c.step(tt(xs.rearrange("p (m h e) -> p m h e", m=M, h=16)[:, 1], xs.rearrange("p (m h e) -> p m h e", m=M, h=16)[:, 1],
                          over(spar("d"), 64), ALU.mult))
                xs3 = xs.rearrange("p (m f) -> p m f", m=M)
                for h in range(16):
                    c.wait("ssd_decay")
                    E = V(6144 + 512 * (h % 2), 384)
                    c.sig(tt(E, E, CB[:, h // 8, :], ALU.mult), "ssd_mask")
                    if h % 8 == 7:
                        c.wait("ssd_done", 8)
                        o = slice(512 * (h // 8), 512 * (h // 8) + 512)
                        c.sig(tt(xs3[:, :, o], xs3[:, :, o], ps[:, 2:4, :], ALU.add), "out_read")
                    prepare(1)
                c.sig(tt(xs, xs, V(10240, 2048), ALU.mult), "o_sq")
                prepare(4)
                c.wait("sq_done")
                rstd_of(SS4, 512)
                for m in range(M):
                    for g in range(2):
                        o = 1024 * m + 512 * g
                        last = ts(xs[:, o:o + 512], xs[:, o:o + 512], SS4[:, 2 * m + g:2 * m + g + 1], None, ALU.mult)
                last.then_inc(sem["y_ready"], 1)
                prepare(5)
                transpose_split(KD, 8, lambda k: spar("norm_g")[:, k:k + 1])
                for h in range(8):
                    c.wait("qk_done")
                    if h >= 2:
                        c.wait("probs_t")
                    pr = V(12288 + 512 * (h % 2), 384)
                    b = h % 2
                    tt(pr[:, 0:P], ps[:, b, 0:P], C["neg_causal"], ALU.add)
                    dve.tensor_copy(pr[:, P:2 * P], ps[:, b, S:S + P])
                    c.sig(tt(pr[:, 2 * P:3 * P], ps[:, b, S + P:2 * S], C["neg_causal"], ALU.add), "logits_read")
                    dve.tensor_reduce(NMAX[:, 2 * h:2 * h + 1], pr[:, 0:P], AX.X, ALU.max)
                    c.step(dve.tensor_reduce(NMAX[:, 2 * h + 1:2 * h + 2], pr[:, P:3 * P], AX.X, ALU.max))
                    c.sig(ts(NMAX[:, 2 * h:2 * h + 2], NMAX[:, 2 * h:2 * h + 2], -1.0, None, ALU.mult), "logits_ready")
                    if h:
                        fox_read(h - 1)
                c.wait("probs_t", 2)
                fox_read(7)
                transpose_split(KD, 0)
                gemm_out(2 * D, 1.0)

            def fox_read(h):
                c.wait("fox_done")
                dve.wait_ge(sem["probs_ready"], h + 1)
                c.step(dve.reciprocal(RSUM[:, 2 * h:2 * h + 2], RSUM[:, 2 * h:2 * h + 2]))
                o = V(10240, 2048).rearrange("p (m h e) -> p m h e", m=M, h=8)
                for m in range(M):
                    last = ts(o[:, m, h, :], ps[:, 3, m * P:(m + 1) * P], RSUM[:, 2 * h + m:2 * h + m + 1], None, ALU.mult)
                c.sig(last, "fox_read")

            def recurrent():
                features_of_x(lambda k: rp("g2")[:, k:k + 1])
                gemm(D, (512,) * 2, ("evac_act",) * 2)
                w, b = rp("conv"), rp("conv_b")
                xT = V(4096, 2048).rearrange("p (n s) -> p n s", n=8)
                for g in range(4):
                    c.wait("conv_tr")
                    ks = (2 * g, 2 * g + 1)
                    src = {k: ps[:, g, (k % 2) * S:(k % 2 + 1) * S] for k in ks}
                    for k in ks:
                        last = ts(xT[:, k, :], src[k], w[:, 24 + k:25 + k], b[:, k:k + 1], ALU.mult, ALU.add)
                    c.step(last)
                    for tap in (2, 1, 0):
                        sh = 3 - tap
                        for k in ks:
                            last = stt(xT[:, k, sh:S], src[k][:, 0:S - sh], w[:, 8 * tap + k:8 * tap + k + 1],
                                       xT[:, k, sh:S], ALU.mult, ALU.add)
                        if tap:
                            c.step(last)
                    c.sig(last, "conv_read")
                prepare(6)
                prepare(6)
                log_sigmoid(rp("lam"))
                c.step(ts(LAM, LAM, 8.0, None, ALU.mult))
                c.wait("r_ready")
                la = V(6144, 2048).rearrange("p (n s) -> p n s", n=8)
                c.sig(tt(la, la, over(LAM, S), ALU.mult), "a_ready")
                prepare(2)
                c.wait("r_ready")
                u = V(8192, 2048)
                c.step(tt(u, u, V(4096, 2048), ALU.mult))
                parts = [[V(o + 1024 * i) for o in (6144, 4096, 10240, 8192)] for i in range(2)]
                for a, a2, th, _ in parts:
                    c.wait("u_ready")
                    c.step(tt(a2, a, a, ALU.mult))
                    c.sig(stt(th, a2, 1.0, th, ALU.add, ALU.mult), "u_sqrt")
                prepare(2)
                for i, (a, h, th, u) in enumerate(parts):
                    c.wait("h_ready")
                    c.step(tt(u, u, th, ALU.mult))
                    h3, u3, a3 = (v.rearrange("p (n s) -> p n s", n=4) for v in (h, u, a))
                    for n in range(4):
                        last = dve.tensor_tensor_scan(h3[:, n, :], a3[:, n, :], u3[:, n, :], 0.0, ALU.mult, ALU.add)
                    c.step(last)
                    if i == 0:
                        c.wait("gt_done")
                    c.sig(tt(u3, h3, ps[:, 2 * i:2 * i + 2, :].rearrange("p b (k s) -> p (b k) s", k=2), ALU.mult),
                          "rec_out")
                for i, (_, _, _, u) in enumerate(parts):
                    c.wait("tr_high")
                    ch = slice(4 * i, 4 * i + 4)
                    tt(hTl[:, ch, :], u.rearrange("p (n s) -> p n s", n=4), hTh[:, ch, :],
                       ALU.subtract).then_inc(sem["tr_low"], 1)
                made[0] += 2
                gemm_out(D, 1.0)

            dve.wait_ge(sem["x_landed"], 16)
            for b in range(2):
                dve.engine_nop().then_inc(sem["x_ready"], 1)
                c.wait("x_ready")
            for l in range(DEPTH):
                dve.wait_ge(sem["params_landed" if l else "first_params_landed"], 16 * max(l, 1))
                features_of_x(lambda k: fp("norm_g")[:, k:k + 1])
                small_w(16, fp("small_w"))
                gdn(l)
                retention()
                merge_out(l, l == DEPTH - 1)
            c.step(tt(SS, SX4[:, 0:2], SX4[:, 2:4], ALU.add))
            rstd_of(SS, D)
            for b in range(2):
                o = slice(512 * b, 512 * b + 512)
                for m in range(M):
                    last = ts(x[:, m, o], XN[:, m, o], SS[:, m:m + 1], None, ALU.mult)
                c.sig(last, "x_ready")
            dve.wait_ge(sem["params_landed"], 16 * 2)
            small_w(24, spar("small_w"))
            gains[0] = lambda k: spar("g0")[:, k:k + 1]
            ffn()
            hybrid()
            gains[0] = lambda k: spar("g4")[:, k:k + 1]
            ffn(last_of_block=True)
            dve.wait_ge(sem["params_landed"], 16 * 3)
            gains[0] = lambda k: rp("g0")[:, k:k + 1]
            ffn()
            recurrent()
            gains[0] = lambda k: rp("g4")[:, k:k + 1]
            ffn()

        @block.sync
        def _(sp):
            sp.dma_start(x[:, :, :], x_in.rearrange("a (m p) d -> p (a m) d", p=P)).then_inc(sem["x_landed"], 16)
            sp.dma_start(par[:, :], params[0]).then_inc(sem["first_params_landed"], 16)
            for u in range(NU):
                if u >= RAW_SLOTS:
                    sp.wait_ge(sem["split_low"], u - RAW_SLOTS + 1)
                sp.dma_start(raw[:, u % RAW_SLOTS, :], weights[u]).then_inc(weight_landed[u % RAW_SLOTS], 16)

        @block.gpsimd
        def _(pool):
            c = Counter(pool, sem, None)
            pool.dma_start(ident, const[:, 0:P]).then_inc(sem["ident_landed"], 16)
            pool.wait_ge(weight_landed[RAW_SLOTS - 1], 16)
            pool.dma_start(cst[:, P:], const[:, P:]).then_inc(sem["const_landed"], 16)
            for l in range(DEPTH):
                pool.wait_ge(sem["x_ready"], 2 * (l + 1))
                pool.dma_start(DIST, dist).then_inc(sem["dist_landed"], 16)
                c.wait("o_ready", 4)
                pool.dma_start(LN_GAINS, wide[7 + l]).then_inc(sem["wide_landed"], 16)
                pool.dma_start(TOKEN_MIX, token_mix[l]).then_inc(sem["mix_landed"], 16)
                if l == DEPTH - 1:
                    pool.wait_ge(sem["mix_done"], DEPTH)
                    pool.dma_start(V(13824), wide[6]).then_inc(sem["final_g_landed"], 16)
                c.wait("params_used")
                pool.dma_start(par[:, :], params[l + 1]).then_inc(sem["params_landed"], 16)
            c.wait("x_ready", 2 * DEPTH)
            for i in range(6):
                c.wait("x_ready", 2)
                pool.dma_start(V(13824), wide[i]).then_inc(sem["wide_landed"], 16)
                if i == 2:
                    pool.dma_start(V(11776, 2048).rearrange("p (t n) -> p t n", t=2),
                                   gate_mix.rearrange("t p n -> p t n")).then_inc(sem["mix_landed"], 16)
                    c.wait("params_used")
                    pool.dma_start(par[:, :], params[3]).then_inc(sem["params_landed"], 16)
            c.wait("x_ready", 2)
            pool.dma_start(out.rearrange("a (m p) d -> p (a m) d", p=P), x[:, :, :]).then_inc(sem["out_landed"], 16)
            pool.wait_ge(sem["out_landed"], 16)


def kernel(**inputs):
    import concourse.bacc as bacc
    from concourse.bass_utils import run_bass_kernel_spmd as run

    a = {k: np.asarray(v) for k, v in inputs.items()}
    const, dist = constants()
    mix, gate_mix = pack_token_mix(a)
    arrays = {"x_in": a["x"], "weights": pack_weights(a), "params": pack_params(a), "wide": pack_wide(a),
              "token_mix": mix, "gate_mix": gate_mix, "const_tables": const, "dist_tables": dist}
    nc = bacc.Bacc("TRN2", target_bir_lowering=False, num_devices=1)
    args = []
    for name, v in arrays.items():
        args.append(nc.dram_tensor(name, v.shape, mybir.dt.from_np(v.dtype), kind="ExternalInput").ap())
    args.append(nc.dram_tensor("y_out", (1, S, D), F32, kind="ExternalOutput").ap())
    program(nc, *args)
    return run(nc, [arrays], core_ids=[0]).results[0]["y_out"]
```
